# Optimizing a Trainium2 kernel written in Bass

```python
import math
import functools
import numpy as np
import jax
import jax.numpy as jnp
from jax import lax

D_MODEL = 1024
BATCH = 1
SEQ = 256
DEPTH = 2
DEC_BATCH = 8
DEC_SEQ = 1
PAST_LEN = 2048
PAGE_SIZE = 128

D_MIX = 2 * D_MODEL
ML_WIDTH = 3 * D_MIX // 8
ML_HEADS = 6
ML_DH = ML_WIDTH // ML_HEADS
SSD_WIDTH = 3 * D_MIX // 8
SSD_HEADDIM = 64
SSD_HEADS = SSD_WIDTH // SSD_HEADDIM
SSD_STATE = 128
SSD_GROUPS = 2
SSD_CONV_DIM = SSD_WIDTH + 2 * SSD_GROUPS * SSD_STATE
CONV_W = 4
RET_WIDTH = D_MIX // 4
RET_HEADS = 4
RET_DH = RET_WIDTH // RET_HEADS
ROPE_BASE = 10000.0
CHUNK = 128
MEM_LEN = 256
CA_HEADS = 4
CA_DH = D_MODEL // CA_HEADS
D_FF = 11 * D_MODEL // 4
N_EXPERTS = 8
TOP_K = 2
D_EXPERT = D_FF // 2
N_DENSE = (DEPTH + 1) // 2
N_MOE = DEPTH // 2
D_IN_PROJ = 4 * ML_WIDTH + 2 * ML_HEADS + SSD_WIDTH + SSD_CONV_DIM + SSD_HEADS + 4 * RET_WIDTH
EPS = 1e-6

kernel_name = 'hybrid_mlstm_ssd_retention_decoder_step'

def _in_proj_splits():
    sizes = [ML_WIDTH] * 4 + [ML_HEADS, ML_HEADS, SSD_WIDTH, SSD_CONV_DIM, SSD_HEADS] + [RET_WIDTH] * 4
    return [int(s) for s in np.cumsum(sizes)[:-1]]

def rmsnorm(x, g):
    xf = x.astype(jnp.float32)
    y = xf * lax.rsqrt(jnp.mean(xf * xf, axis=-1, keepdims=True) + EPS)
    return (y * g.astype(jnp.float32)).astype(x.dtype)

def head_norm(x, g):
    y = x * lax.rsqrt(jnp.mean(x * x, axis=-1, keepdims=True) + EPS)
    return y.reshape(x.shape[0], x.shape[1], -1) * g.astype(jnp.float32)

def _chunk_len(length):
    return CHUNK if length % CHUNK == 0 else length

def _to_chunks(a, c):
    b, length = a.shape[0], a.shape[1]
    return jnp.moveaxis(a.reshape((b, length // c, c) + a.shape[2:]), 1, 0)

def _from_chunks(a):
    n, b, c = a.shape[0], a.shape[1], a.shape[2]
    return jnp.moveaxis(a, 0, 1).reshape((b, n * c) + a.shape[3:])

def _causal_mask(c):
    return jnp.tril(jnp.ones((c, c), dtype=bool))

def rotary(x, pos):
    half = x.shape[-1] // 2
    inv = ROPE_BASE ** (-jnp.arange(half, dtype=jnp.float32) / half)
    ang = pos[:, None] * inv[None, :]
    cos = jnp.cos(ang)[None, :, None, :]
    sin = jnp.sin(ang)[None, :, None, :]
    x1, x2 = x[..., :half], x[..., half:]
    return jnp.concatenate([x1 * cos - x2 * sin, x2 * cos + x1 * sin], axis=-1)

def mlstm_chunked(q, k, v, i_pre, f_pre, c0, n0, m0):
    c = _chunk_len(q.shape[1])
    mask = _causal_mask(c)
    k = k * (k.shape[-1] ** -0.5)
    log_f = jax.nn.log_sigmoid(f_pre)

    def step(carry, inp):
        cm, nv, m = carry
        qc, kc, vc, ic, fc = inp
        b = jnp.moveaxis(jnp.cumsum(fc, axis=1), 1, 2)
        ig = jnp.moveaxis(ic, 1, 2)
        log_w = jnp.where(mask, b[..., :, None] - b[..., None, :] + ig[..., None, :], -jnp.inf)
        log_a = b + m[..., None]
        m_t = jnp.maximum(log_a, jnp.max(log_w, axis=-1))
        w_intra = jnp.exp(log_w - m_t[..., None])
        w_inter = jnp.exp(log_a - m_t)
        s = w_intra * jnp.einsum('bthd,bshd->bhts', qc, kc)
        num = jnp.einsum('bhts,bshv->bthv', s, vc) + jnp.einsum('bht,bhvd,bthd->bthv', w_inter, cm, qc)
        den = jnp.sum(s, axis=-1) + w_inter * jnp.einsum('bhd,bthd->bht', nv, qc)
        den = jnp.maximum(jnp.abs(den), jnp.exp(-m_t))
        h = num / jnp.moveaxis(den, 1, 2)[..., None]
        m_new = m_t[..., -1]
        decay = jnp.exp(log_a[..., -1] - m_new)
        w_end = jnp.exp(b[..., -1:] - b + ig - m_new[..., None])
        cm_new = decay[..., None, None] * cm + jnp.einsum('bhs,bshv,bshd->bhvd', w_end, vc, kc)
        nv_new = decay[..., None] * nv + jnp.einsum('bhs,bshd->bhd', w_end, kc)
        return (cm_new, nv_new, m_new), h

    xs = tuple(_to_chunks(a, c) for a in (q, k, v, i_pre, log_f))
    (c1, n1, m1), h = lax.scan(step, (c0, n0, m0), xs)
    return _from_chunks(h), c1, n1, m1

def ssd_chunked(x, dt, a, bm, cm, h0):
    bsz, length = x.shape[0], x.shape[1]
    r = SSD_HEADS // SSD_GROUPS
    c = _chunk_len(length)
    mask = _causal_mask(c)
    xdt = (x * dt[..., None]).reshape(bsz, length, SSD_GROUPS, r, SSD_HEADDIM)
    log_a = (dt * a).reshape(bsz, length, SSD_GROUPS, r)

    def step(h, inp):
        xc, lac, bc, cc = inp
        acum = jnp.moveaxis(jnp.cumsum(lac, axis=1), 1, -1)
        decay = jnp.exp(jnp.where(mask, acum[..., :, None] - acum[..., None, :], -jnp.inf))
        cb = jnp.einsum('btgn,bsgn->bgts', cc, bc)
        y = jnp.einsum('bgrts,bsgrp->btgrp', decay * cb[:, :, None], xc)
        y = y + jnp.einsum('btgn,bgrpn,bgrt->btgrp', cc, h, jnp.exp(acum))
        w_end = jnp.exp(acum[..., -1:] - acum)
        h_new = jnp.exp(acum[..., -1])[..., None, None] * h + jnp.einsum('bgrs,bsgrp,bsgn->bgrpn', w_end, xc, bc)
        return h_new, y

    xs = tuple(_to_chunks(t, c) for t in (xdt, log_a, bm, cm))
    h1, y = lax.scan(step, h0.reshape(bsz, SSD_GROUPS, r, SSD_HEADDIM, SSD_STATE), xs)
    y = _from_chunks(y).reshape(bsz, length, SSD_HEADS, SSD_HEADDIM)
    return y, h1.reshape(bsz, SSD_HEADS, SSD_HEADDIM, SSD_STATE)

def retention_chunked(q, k, v, s0):
    c = _chunk_len(q.shape[1])
    log_g = jnp.log1p(-jnp.exp2(-5.0 - jnp.arange(RET_HEADS, dtype=jnp.float32)))
    j = jnp.arange(c, dtype=jnp.float32)
    rel = j[:, None] - j[None, :]
    w_intra = jnp.exp(jnp.where(_causal_mask(c), rel[None] * log_g[:, None, None], -jnp.inf))
    w_inter = jnp.exp((j[None, :] + 1.0) * log_g[:, None])
    w_end = jnp.exp((c - 1.0 - j[None, :]) * log_g[:, None])
    decay = jnp.exp(c * log_g)

    def step(s, inp):
        qc, kc, vc = inp
        att = jnp.einsum('bthd,bshd->bhts', qc, kc) * w_intra
        o = jnp.einsum('bhts,bshv->bthv', att, vc) + jnp.einsum('bthd,bhdv,ht->bthv', qc, s, w_inter)
        s_new = decay[:, None, None] * s + jnp.einsum('hs,bshd,bshv->bhdv', w_end, kc, vc)
        return s_new, o

    xs = tuple(_to_chunks(t, c) for t in (q, k, v))
    s1, o = lax.scan(step, s0, xs)
    return _from_chunks(o), s1

def causal_conv(u, conv_state, w, b):
    up = jnp.concatenate([conv_state, u], axis=1)
    y = lax.conv_general_dilated(up, w[:, None, :], window_strides=(1,), padding='VALID',
                                 dimension_numbers=('NWC', 'WIO', 'NWC'), feature_group_count=u.shape[-1])
    return jax.nn.silu(y + b), up[:, -(CONV_W - 1):]

def token_mixers(h, state, pos, lp):
    f32 = jnp.float32
    c0, n0, m0, conv0, ssd0, ret0 = state
    bsz, length = h.shape[0], h.shape[1]
    proj = jnp.einsum('bld,de->ble', h, lp['w_in'])
    (q_ml, k_ml, v_ml, o_ml, i_ml, f_ml, z, xbc, dt_raw, q_r, k_r, v_r, g_r) = jnp.split(proj, _in_proj_splits(), axis=-1)

    def heads(a, n):
        return a.astype(f32).reshape(bsz, length, n, -1)

    h_ml, c1, n1, m1 = mlstm_chunked(heads(q_ml, ML_HEADS), heads(k_ml, ML_HEADS), heads(v_ml, ML_HEADS),
                                     i_ml.astype(f32) + lp['ml_i_bias'].astype(f32),
                                     f_ml.astype(f32) + lp['ml_f_bias'].astype(f32), c0, n0, m0)
    y_ml = head_norm(h_ml, lp['ml_norm']) * jax.nn.sigmoid(o_ml.astype(f32))

    u, conv1 = causal_conv(xbc.astype(f32), conv0, lp['ssd_conv_w'].astype(f32), lp['ssd_conv_b'].astype(f32))
    xs_, b_, c_ = jnp.split(u, [SSD_WIDTH, SSD_WIDTH + SSD_GROUPS * SSD_STATE], axis=-1)
    xs_ = xs_.reshape(bsz, length, SSD_HEADS, SSD_HEADDIM)
    dt = jax.nn.softplus(dt_raw.astype(f32) + lp['ssd_dt_bias'].astype(f32))
    a = -jnp.exp(lp['ssd_a_log'].astype(f32))
    y_s, ssd1 = ssd_chunked(xs_, dt, a, b_.reshape(bsz, length, SSD_GROUPS, SSD_STATE),
                            c_.reshape(bsz, length, SSD_GROUPS, SSD_STATE), ssd0)
    y_s = y_s + lp['ssd_d'].astype(f32)[:, None] * xs_
    yz = (y_s.reshape(bsz, length, SSD_WIDTH) * jax.nn.silu(z.astype(f32))).reshape(bsz, length, SSD_GROUPS, -1)
    y_s = head_norm(yz, lp['ssd_norm'])

    qr = rotary(heads(q_r, RET_HEADS), pos)
    kr = rotary(heads(k_r, RET_HEADS), pos) * (RET_DH ** -0.5)
    o_r, ret1 = retention_chunked(qr, kr, heads(v_r, RET_HEADS), ret0)
    y_r = head_norm(o_r, lp['ret_norm']) * jax.nn.silu(g_r.astype(f32))

    y = jnp.concatenate([y_ml, y_s, y_r], axis=-1).astype(h.dtype)
    return jnp.einsum('ble,ed->bld', y, lp['w_out']), (c1, n1, m1, conv1, ssd1, ret1)

def memory_kv(mem, g, w_k, w_v):
    mn = rmsnorm(mem, g)
    b = mem.shape[0]
    k = jnp.einsum('bmd,de->bme', mn, w_k).reshape(b, MEM_LEN, CA_HEADS, CA_DH)
    v = jnp.einsum('bmd,de->bme', mn, w_v).reshape(b, MEM_LEN, CA_HEADS, CA_DH)
    return k, v

def cross_attn(h, mem_k, mem_v, w_q, w_o):
    b, length = h.shape[0], h.shape[1]
    q = jnp.einsum('bld,de->ble', h, w_q).reshape(b, length, CA_HEADS, CA_DH)
    s = jnp.einsum('bqhd,bmhd->bhqm', q, mem_k).astype(jnp.float32) * (CA_DH ** -0.5)
    p = jax.nn.softmax(s, axis=-1).astype(mem_v.dtype)
    o = jnp.einsum('bhqm,bmhd->bqhd', p, mem_v).reshape(b, length, D_MODEL)
    return jnp.einsum('bld,de->ble', o.astype(h.dtype), w_o)

def swiglu(h, w_gate, w_up, w_down):
    return (jax.nn.silu(h @ w_gate) * (h @ w_up)) @ w_down

def moe_swiglu(h, w_router, w_gate, w_up, w_down):
    logits = jnp.einsum('bld,de->ble', h, w_router).astype(jnp.float32)
    top_val, top_idx = lax.top_k(logits, TOP_K)
    gate = jax.nn.softmax(top_val, axis=-1)
    combine = jnp.einsum('blk,blke->ble', gate, jax.nn.one_hot(top_idx, N_EXPERTS, dtype=jnp.float32)).astype(h.dtype)
    out = jnp.zeros_like(h)
    for e in range(N_EXPERTS):
        act = jax.nn.silu(h @ w_gate[e]) * (h @ w_up[e])
        out = out + combine[..., e:e + 1] * (act @ w_down[e])
    return out

def run_layer(x, state, mem_k, mem_v, pos, lp, ffn):
    y, new_state = token_mixers(rmsnorm(x, lp['norm_mix']), state, pos, lp)
    x = x + y
    x = x + cross_attn(rmsnorm(x, lp['norm_ca']), mem_k, mem_v, lp['w_ca_q'], lp['w_ca_o'])
    x = x + ffn(rmsnorm(x, lp['norm_ffn']))
    return x, new_state

def setup_inputs(seed: int = 0) -> dict:
    key = jax.random.key(seed)
    keys = jax.random.split(key, 64)
    counter = [0]

    def _next():
        k = keys[counter[0]]
        counter[0] += 1
        return k

    def nrm(shape, scale=1.0):
        return scale * jax.random.normal(_next(), shape, jnp.float32)

    def gain(shape):
        return 1.0 + nrm(shape, 0.01)

    def unif(shape, lo, hi):
        return jax.random.uniform(_next(), shape, jnp.float32, lo, hi)

    dt0 = jnp.exp(unif((DEPTH, SSD_HEADS), math.log(1e-3), math.log(1e-1)))
    a_init = unif((DEPTH, SSD_HEADS), 1.0, 16.0)
    return {
        'x_prompt': nrm((BATCH, SEQ, D_MODEL)),
        'x_sample': nrm((DEC_BATCH, DEC_SEQ, D_MODEL)),
        'state_mlstm_c': nrm((DEPTH, DEC_BATCH, ML_HEADS, ML_DH, ML_DH), 0.5),
        'state_mlstm_n': nrm((DEPTH, DEC_BATCH, ML_HEADS, ML_DH), 0.5),
        'state_mlstm_m': nrm((DEPTH, DEC_BATCH, ML_HEADS)),
        'state_ssd_conv': nrm((DEPTH, DEC_BATCH, CONV_W - 1, SSD_CONV_DIM)),
        'state_ssd': nrm((DEPTH, DEC_BATCH, SSD_HEADS, SSD_HEADDIM, SSD_STATE), 0.5),
        'state_ret': nrm((DEPTH, DEC_BATCH, RET_HEADS, RET_DH, RET_DH), 0.5),
        'cache_mem_k': nrm((DEPTH, DEC_BATCH, MEM_LEN, CA_HEADS, CA_DH)),
        'cache_mem_v': nrm((DEPTH, DEC_BATCH, MEM_LEN, CA_HEADS, CA_DH)),
        'mem_prompt': nrm((BATCH, MEM_LEN, D_MODEL)),
        'norm_mix': gain((DEPTH, D_MODEL)),
        'w_in': nrm((DEPTH, D_MODEL, D_IN_PROJ), D_MODEL ** -0.5),
        'ml_i_bias': nrm((DEPTH, ML_HEADS), 0.1),
        'ml_f_bias': 3.0 + nrm((DEPTH, ML_HEADS), 0.5),
        'ml_norm': gain((DEPTH, ML_WIDTH)),
        'ssd_conv_w': nrm((DEPTH, CONV_W, SSD_CONV_DIM), CONV_W ** -0.5),
        'ssd_conv_b': nrm((DEPTH, SSD_CONV_DIM), 0.01),
        'ssd_dt_bias': dt0 + jnp.log(-jnp.expm1(-dt0)),
        'ssd_a_log': jnp.log(a_init),
        'ssd_d': 1.0 + nrm((DEPTH, SSD_HEADS), 0.1),
        'ssd_norm': gain((DEPTH, SSD_WIDTH)),
        'ret_norm': gain((DEPTH, RET_WIDTH)),
        'w_out': nrm((DEPTH, D_MIX, D_MODEL), D_MIX ** -0.5),
        'norm_ca': gain((DEPTH, D_MODEL)),
        'norm_mem': gain((DEPTH, D_MODEL)),
        'w_ca_q': nrm((DEPTH, D_MODEL, D_MODEL), D_MODEL ** -0.5),
        'w_ca_k': nrm((DEPTH, D_MODEL, D_MODEL), D_MODEL ** -0.5),
        'w_ca_v': nrm((DEPTH, D_MODEL, D_MODEL), D_MODEL ** -0.5),
        'w_ca_o': nrm((DEPTH, D_MODEL, D_MODEL), D_MODEL ** -0.5),
        'norm_ffn': gain((DEPTH, D_MODEL)),
        'ffn_w_gate': nrm((N_DENSE, D_MODEL, D_FF), D_MODEL ** -0.5),
        'ffn_w_up': nrm((N_DENSE, D_MODEL, D_FF), D_MODEL ** -0.5),
        'ffn_w_down': nrm((N_DENSE, D_FF, D_MODEL), D_FF ** -0.5),
        'moe_w_router': nrm((N_MOE, D_MODEL, N_EXPERTS), D_MODEL ** -0.5),
        'moe_w_gate': nrm((N_MOE, N_EXPERTS, D_MODEL, D_EXPERT), D_MODEL ** -0.5),
        'moe_w_up': nrm((N_MOE, N_EXPERTS, D_MODEL, D_EXPERT), D_MODEL ** -0.5),
        'moe_w_down': nrm((N_MOE, N_EXPERTS, D_EXPERT, D_MODEL), D_EXPERT ** -0.5),
        'norm_final': gain((D_MODEL,)),
    }

def reference(x_prompt, x_sample, state_mlstm_c, state_mlstm_n, state_mlstm_m, state_ssd_conv, state_ssd, state_ret,
              cache_mem_k, cache_mem_v, mem_prompt,
              norm_mix, w_in, ml_i_bias, ml_f_bias, ml_norm, ssd_conv_w, ssd_conv_b, ssd_dt_bias, ssd_a_log, ssd_d,
              ssd_norm, ret_norm, w_out, norm_ca, norm_mem, w_ca_q, w_ca_k, w_ca_v, w_ca_o, norm_ffn,
              ffn_w_gate, ffn_w_up, ffn_w_down, moe_w_router, moe_w_gate, moe_w_up, moe_w_down, norm_final):
    f32 = jnp.float32
    bp = x_prompt.shape[0]
    pos_p = jnp.arange(x_prompt.shape[1], dtype=f32)
    pos_s = PAST_LEN + jnp.arange(x_sample.shape[1], dtype=f32)
    zero_p = (jnp.zeros((bp, ML_HEADS, ML_DH, ML_DH), f32), jnp.zeros((bp, ML_HEADS, ML_DH), f32),
              jnp.zeros((bp, ML_HEADS), f32), jnp.zeros((bp, CONV_W - 1, SSD_CONV_DIM), f32),
              jnp.zeros((bp, SSD_HEADS, SSD_HEADDIM, SSD_STATE), f32), jnp.zeros((bp, RET_HEADS, RET_DH, RET_DH), f32))
    sample_states = (state_mlstm_c, state_mlstm_n, state_mlstm_m, state_ssd_conv, state_ssd, state_ret)
    new_p = [[] for _ in range(6)]
    new_s = [[] for _ in range(6)]
    mem_k_p, mem_v_p = [], []
    xp, xs = x_prompt, x_sample
    for l in range(DEPTH):
        lp = {'norm_mix': norm_mix[l], 'w_in': w_in[l], 'ml_i_bias': ml_i_bias[l], 'ml_f_bias': ml_f_bias[l],
              'ml_norm': ml_norm[l], 'ssd_conv_w': ssd_conv_w[l], 'ssd_conv_b': ssd_conv_b[l],
              'ssd_dt_bias': ssd_dt_bias[l], 'ssd_a_log': ssd_a_log[l], 'ssd_d': ssd_d[l], 'ssd_norm': ssd_norm[l],
              'ret_norm': ret_norm[l], 'w_out': w_out[l], 'norm_ca': norm_ca[l], 'w_ca_q': w_ca_q[l],
              'w_ca_o': w_ca_o[l], 'norm_ffn': norm_ffn[l]}
        j = l // 2
        if l % 2 == 0:
            ffn = functools.partial(swiglu, w_gate=ffn_w_gate[j], w_up=ffn_w_up[j], w_down=ffn_w_down[j])
        else:
            ffn = functools.partial(moe_swiglu, w_router=moe_w_router[j], w_gate=moe_w_gate[j],
                                    w_up=moe_w_up[j], w_down=moe_w_down[j])
        mk, mv = memory_kv(mem_prompt, norm_mem[l], w_ca_k[l], w_ca_v[l])
        xp, st_p = run_layer(xp, zero_p, mk, mv, pos_p, lp, ffn)
        mem_k_p.append(mk)
        mem_v_p.append(mv)
        st_in = tuple(a[l].astype(f32) for a in sample_states)
        xs, st_s = run_layer(xs, st_in, cache_mem_k[l], cache_mem_v[l], pos_s, lp, ffn)
        for lst, a in zip(new_p, st_p):
            lst.append(a)
        for lst, a in zip(new_s, st_s):
            lst.append(a)
    y_prompt = rmsnorm(xp, norm_final)
    y_sample = rmsnorm(xs, norm_final)
    return (y_prompt, y_sample,
            jnp.stack(new_p[0]), jnp.stack(new_p[1]), jnp.stack(new_p[2]), jnp.stack(new_p[3]),
            jnp.stack(new_p[4]), jnp.stack(new_p[5]), jnp.stack(mem_k_p), jnp.stack(mem_v_p),
            jnp.stack(new_s[0]), jnp.stack(new_s[1]), jnp.stack(new_s[2]), jnp.stack(new_s[3]),
            jnp.stack(new_s[4]), jnp.stack(new_s[5]))


_drawn_inputs = setup_inputs


def setup_inputs(seed=0):
    import zlib

    import numpy as np

    out = dict(_drawn_inputs(seed))
    spreads = {}
    factors = {'ml_norm': 3.924,
     'ssd_conv_b': 2.85,
     'ssd_norm': 4.422,
     'ret_norm': 4.967,
     'norm_ca': 8.0,
     'norm_mem': 5.177,
     'norm_ffn': 3.009,
     'norm_final': 5.75}
    for name, (base, spread) in spreads.items():
        noise = np.random.default_rng([zlib.crc32(name.encode()), seed]).standard_normal(out[name].shape)
        drawn = base * np.exp(spread * noise) if base else spread * noise
        out[name] = jnp.asarray(drawn.astype(out[name].dtype))
    for name, factor in factors.items():
        out[name] = (out[name] * factor).astype(out[name].dtype)
    return out
```

```python
from contextlib import ExitStack

import numpy as np

import concourse.bass as bass
from concourse import mybir

F32 = mybir.dt.float32
ALU = mybir.AluOpType
ACT = mybir.ActivationFunctionType
AX = mybir.AxisListType

P = 128
D_MODEL, SEQ, DEPTH, NB = 1024, 256, 2, 8
PAST_LEN = 2048
KT = D_MODEL // P
NT = SEQ + NB
NH, SH, RH = 6, 12, 4
SP = SH // 2
NE, TOP_K = 8, 2
MEM, CAH = 256, 4
F_TILES = 11
CONV_T = 10
EPS = 1e-6
MASKED = -30000.0

Q_ML, K_ML, V_ML, O_ML, Z, XBC, Q_R, K_R, V_R, G_R, N_PROJ = 0, 6, 12, 18, 24, 30, 40, 44, 48, 52, 56
B_T, C_T = 6, 8
CA_Q, CA_K, CA_V, CA_O, CA_MEM, CA_MEMN, CA_TMP = 0, 8, 16, 24, 32, 40, 48

SLOTS = 7
BLOCK = 2048
IN_BLOCKS, IN_ITERS = 28, 4
GU_BLOCKS, DOWN_BLOCKS, EXPERT_BLOCKS = F_TILES, KT, 21

G_MIX, G_CA, G_MEM, G_FFN, G_ML, G_SSD, G_RET, CONV_B, CONV_K, D_SKIP = 0, 8, 16, 24, 32, 38, 44, 48, 58, 98
N_PAR = 104
C_ID, C_MASK, C_ONES, C_ROT, C_COS, C_SIN, C_COSK, C_SINK = 0, 128, 256, 384, 512, 776, 1040, 1304
C_RET, C_TIE, C_SEL2, C_EPS, N_CONST = 1568, 1568 + 4 * 384, 1568 + 4 * 384 + 64, 3168 + 768, 3168 + 768 + 2
UNITS = NH + SP + RH
STATE_SLOTS, CACHE_SLOTS = 6, 3


class Steps:

    def __init__(self, eng, sem):
        self.eng, self.sem, self.n, self.i, self.per = eng, sem, 0, None, 0

    def __call__(self, ins):
        self.n += 1
        ins.then_inc(self.sem, 1)
        self.eng.wait_ge(self.sem, self.n if self.i is None else self.i * self.per + self.n)

    def begin(self, i, per):
        self.i, self.per, self.start = i, per, self.n

    def end(self, iters):
        assert self.n - self.start == self.per, (self.n - self.start, self.per)
        self.i, self.n = None, self.start + iters * self.per


class Ring:

    def __init__(self):
        self.used, self.at, self.i = [0] * SLOTS, 0, None

    def take(self):
        s, u = self.at % SLOTS, self.used[self.at % SLOTS]
        self.at, self.used[s] = self.at + 1, u + 1
        return s, (u if self.i is None else self.i * self.per[s] + u)

    def skip(self):
        self.at += 1

    def begin(self, i, blocks, empty=0):
        self.i, self.before = i, list(self.used)
        self.per = [0] * SLOTS
        for b in range(blocks - empty):
            self.per[(self.at + b) % SLOTS] += 1

    def end(self, iters):
        assert [u - b for u, b in zip(self.used, self.before)] == self.per
        self.used = [b + iters * p for b, p in zip(self.before, self.per)]
        self.i = None


def program(nc, t):
    with ExitStack() as ctx:
        def sb(name, cols, rows=P):
            return ctx.enter_context(nc.sbuf_tensor(name, [rows, cols], F32))

        def sem(name):
            return ctx.enter_context(nc.semaphore(name))

        ring = sb("ring", SLOTS * BLOCK)
        xT = sb("xT", KT * NT)
        hT = sb("hT", KT * NT)
        proj = sb("proj", N_PROJ * NT)
        conv = sb("conv", CONV_T * NT)
        tmp = sb("tmp", CONV_T * NT)
        stream = sb("stream", STATE_SLOTS * 1024)
        const = sb("const", N_CONST)
        par = sb("par", DEPTH * N_PAR + KT)
        hpar = sb("hpar", DEPTH * 3)
        wgate = sb("wgate", DEPTH * KT * 76)
        nst = sb("nst", DEPTH * 48)
        cst = sb("cst", DEPTH * CONV_T * 3 * NB)
        m0 = sb("m0", DEPTH * NB, 6)
        alog = sb("alog", DEPTH, 12)
        wrt = sb("wrt", KT * NE)
        rstd = sb("rstd", NT)
        spx = sb("spx", 2 * NT, 12)
        spa, spu, spd, spl = (conv[0:12, 2 * NT * i:2 * NT * (i + 1)] for i in range(4))
        gI, lda = conv[0:6, 8 * NT:9 * NT], conv[0:12, 9 * NT:10 * NT]
        negM, negm = sb("negM", SEQ, 6), sb("negm", SEQ, 6)
        cum_f, run_max, grow, arow = hT[0:6, 600:856], hT[0:6, 860:1116], hT[0:6, 1120:1504], hT[0:12, 1510:1894]
        cum_a = sb("cum_a", SEQ, 12)
        small = sb("small", 40, 12)
        smR = sb("smR", 24, 6)
        gcol = sb("gcol", 54)
        gbc = sb("gbc", 192)
        nnew = sb("nnew", 48)
        rden = sb("rden", 48)
        npr = sb("npr", NH)
        vA = sb("vA", 48)
        xds = sb("xds", 48)
        yT = sb("yT", NB)
        yT2 = sb("yT2", 48)
        cvp = sb("cvp", CONV_T * 3)
        sml = sb("sml", 64)
        ps = ctx.enter_context(nc.psum_tensor("ps", [P, 8 * 512], F32))

        dma_const, dma_small, dma_out = sem("dma_const"), sem("dma_small"), sem("dma_out")
        landed = [sem(f"landed{s}") for s in range(SLOTS)]
        used = [sem(f"used{s}") for s in range(SLOTS)]
        state_in = [sem(f"state_in{s}") for s in range(STATE_SLOTS)]
        state_out = [sem(f"state_out{s}") for s in range(STATE_SLOTS)]
        cache_in = [sem(f"cache_in{s}") for s in range(CACHE_SLOTS)]
        mem_in = sem("mem_in")
        act_step, dve_step = sem("act_step"), sem("dve_step")
        lin_ready, lin_free = sem("lin_ready"), [sem("lin_free0"), sem("lin_free1")]
        sq_ready, ss_ready, rs_ready, h_ready, x_ready = (sem(n) for n in ("sq_ready", "ss_ready", "rs_ready", "h_ready", "x_ready"))
        gate_abs, gate_exp, gate_one, gate_log = (sem(n) for n in ("gate_abs", "gate_exp", "gate_one", "gate_log"))
        gate_rows, gate_cols, gate_cols_in, gate_sexp, gate_bc, gate_bc_in = (sem(n) for n in (
            "gate_rows", "gate_cols", "gate_cols_in", "gate_sexp", "gate_bc", "gate_bc_in"))
        k_scaled, exps_ready, acts_ready, conv_acc, conv_exp, conv_done = (sem(n) for n in (
            "k_scaled", "exps_ready", "acts_ready", "conv_acc", "conv_exp", "conv_done"))
        rot_ready, rot_used, rot_done = sem("rot_ready"), sem("rot_used"), sem("rot_done")
        nq_ready, nden_ready, nden_done = sem("nq_ready"), sem("nden_ready"), sem("nden_done")
        ml_scores, ml_w, ml_weighted, ml_num, ml_h, ml_state = (sem(n) for n in (
            "ml_scores", "ml_w", "ml_weighted", "ml_num", "ml_h", "ml_state"))
        ssd_cb, ssd_dt, ssd_xdt, ssd_L, ssd_w, ssd_S, ssd_y, ssd_h, ssd_state = (sem(n) for n in (
            "ssd_cb", "ssd_dt", "ssd_xdt", "ssd_L", "ssd_w", "ssd_S", "ssd_y", "ssd_h", "ssd_state"))
        ret_scores, ret_vk, ret_weighted, ret_num, ret_h = (sem(n) for n in (
            "ret_scores", "ret_vk", "ret_weighted", "ret_num", "ret_h"))
        dec_diag, dec_bc, dec_S, dec_y = (sem(n) for n in ("dec_diag", "dec_bc", "dec_S", "dec_y"))
        post_sq, post_ss, post_rs, post_y = (sem(n) for n in ("post_sq", "post_ss", "post_rs", "post_y"))
        ca_scores, ca_max, ca_exp, ca_p, ca_pt, ca_ptc, ca_o, ca_oc = (sem(n) for n in (
            "ca_scores", "ca_max", "ca_exp", "ca_p", "ca_pt", "ca_ptc", "ca_o", "ca_oc"))
        cs_k, cs_scores, cs_sc, cs_turn, cs_max, cs_exp, cs_p, cs_back, cs_backc, cs_v, cs_oc = (sem(n) for n in (
            "cs_k", "cs_scores", "cs_sc", "cs_turn", "cs_max", "cs_exp", "cs_p", "cs_back", "cs_backc", "cs_v", "cs_oc"))
        rt_logits, rt_max, rt_exp, rt_comb, rt_turn, rt_combT = (sem(n) for n in (
            "rt_logits", "rt_max", "rt_exp", "rt_comb", "rt_turn", "rt_combT"))
        ex_mask, ex_bc, gu_ready, gu_exp, gu_free, down_ready, down_free = (sem(n) for n in (
            "ex_mask", "ex_bc", "gu_ready", "gu_exp", "gu_free", "down_ready", "down_free"))
        y_out = sem("y_out")

        def bank(b, lo=0, n=512, rows=P, r0=0):
            return ps[r0:r0 + rows, b * 512 + lo:b * 512 + lo + n]

        def tile(buf, i, lo=0, n=NT, rows=P):
            return buf[0:rows, i * NT + lo:i * NT + lo + n]

        def tiles3(buf, i, n, lo=0, w=NT):
            return buf[:, i * NT:(i + n) * NT].rearrange("p (k t) -> p k t", k=n)[:, :, lo:lo + w]

        def c(at, n=P, rows=P):
            return const[0:rows, at:at + n]

        def pcol(l, at):
            return par[:, l * N_PAR + at:l * N_PAR + at + 1]

        def slot(s, lo=0, n=BLOCK):
            return ring[:, s * BLOCK + lo:s * BLOCK + lo + n]

        def state(u):
            return stream[:, (u % STATE_SLOTS) * 1024:(u % STATE_SLOTS + 1) * 1024]

        def cache(i):
            return stream[:, (i % CACHE_SLOTS) * 2048:(i % CACHE_SLOTS + 1) * 2048]

        ident, ones = c(C_ID), c(C_ONES)
        mW, mS, mVK, mKW, mEM, mDN = (hT[:, a:b] for a, b in (
            (0, 384), (384, 768), (768, 1280), (1280, 1536), (1536, 1792), (1792, 2048)))
        sXD, sXT, sS, sXW, sY, sBT = (hT[:, a:b] for a, b in (
            (0, 264), (264, 520), (520, 1288), (1288, 1544), (1544, 1800), (1800, 2056)))
        sL = tmp[:, 0:768]
        dB, dC = tmp[:, 0:1024], tmp[:, 1024:2048]
        caP, caPT = conv[:, 0:512], tmp[:, 0:512]
        csS, csP, csPT = conv[:, 512:576], conv[0:32, 576:832], conv[:, 832:896]
        combT, combM, combB = conv[0:8, 1024:1024 + NT], conv[0:8, 1300:1300 + NT], tmp[:, 1300:1300 + NT]
        sig = [tmp[:, 0:NT], tmp[:, NT:2 * NT]]
        lg = conv[:, 0:24]

        lin_of, n = {}, 0
        for name, k in (("in", 56), ("gates", 1), ("out", KT), ("memk", KT), ("memv", 8), ("q", KT), ("o", KT)):
            lin_of[name] = n
            n += k
        LIN = n
        NORMS = 4
        block = ctx.enter_context(nc.Block())

        @block.sync
        def _(sp):
            r = Ring()

            def load(src, n=BLOCK):
                s, before = r.take()
                if r.i is not None or before > 0:
                    sp.wait_ge(used[s], before)
                sp.dma_start(slot(s, 0, n), src).then_inc(landed[s], 16)

            for dst, name in ((const, "const"), (xT, "x"), (par, "par"), (wgate, "wgate")):
                sp.dma_start(dst[:, :], t[name]).then_inc(dma_const, 16)
            for dst, name in ((hpar, "hpar"), (nst, "nst"), (cst, "cst"), (m0, "m0"), (alog, "alog"), (wrt, "wrt")):
                sp.dma_start(dst[:, :], t[name]).then_inc(dma_small, 16)
            for l in range(DEPTH):
                first = 1 if l == 0 else 0
                if first:
                    for j in range(SLOTS):
                        load(t["w_in"][l, j])
                r.begin(0, SLOTS)
                with sp.Fori(first, IN_ITERS) as i:
                    r.i = i - first if first else i
                    for j in range(SLOTS):
                        load(t["w_in"][l].rearrange("b p n -> p b n")[:, bass.ds(i * SLOTS + j, 1), :])
                r.end(IN_ITERS - first)
                for j in range(KT):
                    load(t["w_out"][l, j])
                for name, blocks in (("w_k", 4), ("w_v", 4), ("w_q", 4), ("w_o", 4)):
                    for j in range(blocks):
                        load(t[name][l, j])
                e0, ne = (0, 2) if l == 0 else (2, NE)
                r.begin(0, EXPERT_BLOCKS, 2)
                with sp.Fori(0, ne) as e:
                    r.i = e
                    for j in range(GU_BLOCKS):
                        load(t["w_gu"].rearrange("e b p n -> p (e b) n")[:, bass.ds((e + e0) * GU_BLOCKS + j, 1), :])
                    for j in range(DOWN_BLOCKS):
                        load(t["w_down"].rearrange("e b p n -> p (e b) n")[
                            :, bass.ds((e + e0) * DOWN_BLOCKS + j, 1), :], F_TILES * P)
                    r.skip()
                    r.skip()
                r.end(ne)
            sp.wait_ge(h_ready, DEPTH * NORMS + 1)
            sp.dma_start(t["y"], hT[:, :]).then_inc(y_out, 16)
            sp.wait_ge(y_out, 16)
            sp.wait_ge(dma_out, 16 * DEPTH * OUTS)
            for s in range(STATE_SLOTS):
                sp.wait_ge(state_out[s], 16 * len([u for u in range(DEPTH * UNITS) if u % UNITS % STATE_SLOTS == s]))

        @block.tensor
        def _(pe):
            r = Ring()
            def block_in():
                s, before = r.take()
                pe.wait_ge(landed[s], before * 16 + 16)
                return s

            def lin_bank(n):
                if n >= 2:
                    pe.wait_ge(lin_free[n % 2], n // 2)
                return n % 2

            def norm_sum(k, src, w=NT, s0=0):
                pe.wait_ge(sq_ready, k + 1)
                for j in range(KT):
                    ins = pe.matmul(bank(6, 0, w), ones, tile(src, s0 + j, 0, w), start=j == 0, stop=j == KT - 1)
                ins.then_inc(ss_ready, 1)

            def in_tiles(s, w, rhs, n):
                for half in range(2):
                    b = lin_bank(n + half)
                    for k in range(KT):
                        ins = pe.matmul(bank(b, 0, w), slot(s, k * 256 + half * P, P), rhs(k), start=k == 0, stop=k == KT - 1)
                    ins.then_inc(lin_ready, 1)

            def free_slot(s):
                pe.matmul(bank(7, 511, 1, 1), ones[0:1, 0:1], ones[0:1, 0:1], start=True, stop=True).then_inc(used[s], 1)

            def causal(dst, h, rows, row):
                sel = ident[0:rows, h:h + 1].to_broadcast([rows, P])
                pe.matmul(dst[:, 0:SEQ], sel, row[:, 0:SEQ], start=True, stop=False, skip_group_check=True)
                pe.matmul(dst[:, 0:P], ident, c(C_MASK), start=False, stop=True, skip_group_check=True)
                pe.matmul(dst[:, SEQ:384], sel, row[:, P:SEQ], start=True, stop=False, skip_group_check=True)
                return pe.matmul(dst[:, SEQ:384], ident, c(C_MASK), start=False, stop=True, skip_group_check=True)

            def blocks3(dst, lhs, rhs):
                pe.matmul(dst[:, 0:P], lhs(0), rhs[:, 0:P], start=True, stop=True, skip_group_check=True)
                pe.matmul(dst[:, P:SEQ], lhs(0), rhs[:, P:SEQ], start=True, stop=False, skip_group_check=True)
                return pe.matmul(dst[:, P:SEQ], lhs(1), rhs[:, SEQ:384], start=False, stop=True, skip_group_check=True)

            pe.wait_ge(dma_const, 64)
            for l in range(DEPTH):
                L0 = l * LIN
                norm_sum(l * NORMS, hT)
                pe.wait_ge(h_ready, l * NORMS + 1)
                n0 = L0 + lin_of["in"]
                first = 1 if l == 0 else 0
                if first:
                    for j in range(SLOTS):
                        s = block_in()
                        in_tiles(s, NT, lambda k: tile(hT, k), n0 + 2 * j)
                        free_slot(s)
                r.begin(0, SLOTS)
                with pe.Fori(first, IN_ITERS) as i:
                    r.i = i - first if first else i
                    for j in range(SLOTS):
                        s = block_in()
                        for half in range(2):
                            n = n0 + 2 * j + half
                            pe.wait_ge(lin_free[n % 2], i * SLOTS + n // 2)
                            for k in range(KT):
                                ins = pe.matmul(bank(n % 2, 0, NT), slot(s, k * 256 + half * P, P), tile(hT, k),
                                                start=k == 0, stop=k == KT - 1)
                            ins.then_inc(lin_ready, 1)
                        free_slot(s)
                r.end(IN_ITERS - first)
                b = lin_bank(L0 + lin_of["gates"])
                for k in range(KT):
                    ins = pe.matmul(bank(b, 0, NT, 76), wgate[:, (l * KT + k) * 76:(l * KT + k + 1) * 76], tile(hT, k),
                                    start=k == 0, stop=k == KT - 1)
                ins.then_inc(lin_ready, 1)
                pe.wait_ge(lin_free[(L0 + 55) % 2], (L0 + 55) // 2 + 1)
                pe.wait_ge(lin_free[(L0 + 54) % 2], (L0 + 54) // 2 + 1)
                for j in range(2 * RH):
                    n = l * 2 * RH + j
                    if j >= 2:
                        pe.wait_ge(rot_used, n - 1)
                    pe.matmul(bank(4 + n % 2, 0, NT), c(C_ROT), tile(proj, Q_R + j), start=True, stop=True).then_inc(rot_ready, 1)
                pe.wait_ge(gate_rows, l + 1)
                for j in range(3):
                    pe.transpose(bank(2, 6 * j, 6), grow[:, j * P:(j + 1) * P], ident[0:6, 0:6])
                for j in range(3):
                    ins = pe.transpose(bank(2, 18 + 12 * j, 12), arow[:, j * P:(j + 1) * P], ident[0:12, 0:12])
                ins.then_inc(gate_cols, 1)
                pe.wait_ge(gate_sexp, l + 1)
                for h in range(NH):
                    pe.matmul(bank(3, 24 * h, 24), ident[0:6, h:h + 1].to_broadcast([6, P]), smR[:, :], start=True, stop=True)
                for j in range(SP):
                    ins = pe.matmul(bank(3, 144 + 8 * j, 8), const[0:12, C_SEL2 + j * P:C_SEL2 + (j + 1) * P], small[:, 8:16],
                                    start=True, stop=True)
                ins.then_inc(gate_bc, 1)
                pe.wait_ge(nq_ready, l + 1)
                pe.matmul(bank(6, 0, 48), ones, yT2[:, :], start=True, stop=True).then_inc(nden_ready, 1)
                pe.wait_ge(k_scaled, l + 1)
                pe.wait_ge(gate_cols_in, l + 1)
                pe.wait_ge(gate_bc_in, l + 1)
                pe.wait_ge(rot_used, (l + 1) * 2 * RH)
                pe.wait_ge(nden_done, l + 1)

                def turn_vk(b, v, k):
                    for st in range(2):
                        pe.transpose(bank(b, st * P, P), tile(proj, v, st * P, P), ident)
                    for st in range(2):
                        ins = pe.transpose(bank(b, SEQ + st * P, P), tile(proj, k, st * P, P), ident)
                    return ins

                def scores(b, k, q):
                    pe.matmul(bank(b, 0, SEQ), tile(proj, k, 0, P), tile(proj, q, 0, SEQ), start=True, stop=True)
                    return pe.matmul(bank(b, SEQ, P), tile(proj, k, P, P), tile(proj, q, P, P), start=True, stop=True)

                def ml_a(h):
                    n = l * NH + h
                    if h:
                        pe.wait_ge(ml_weighted, n)
                        pe.wait_ge(ml_w, n)
                    scores(2, K_ML + h, Q_ML + h)
                    causal(bank(3, 0, 384), h, 6, negM)
                    pe.matmul(bank(4, 0, SEQ), ident[0:6, h:h + 1].to_broadcast([6, P]), negm[:, :], start=True, stop=True)
                    turn_vk(5, V_ML + h, K_ML + h).then_inc(ml_scores, 1)

                def ml_d(h):
                    n = l * NH + h
                    pe.wait_ge(ml_weighted, n + 1)
                    if h:
                        pe.wait_ge(ml_h, n)
                        pe.wait_ge(ml_state, n)
                    blocks3(bank(6, 0, SEQ), lambda st: mVK[:, st * P:(st + 1) * P], mS)
                    blocks3(bank(6, SEQ, SEQ), lambda st: ones, mS)
                    for st in range(2):
                        pe.matmul(bank(7, 0, P), mVK[:, st * P:(st + 1) * P], mKW[:, st * P:(st + 1) * P], start=st == 0, stop=st == 1)
                    for st in range(2):
                        ins = pe.matmul(bank(7, P, 1), mKW[:, st * P:(st + 1) * P], ones[:, 0:1], start=st == 0, stop=st == 1)
                    ins.then_inc(ml_num, 1)

                for h in range(NH):
                    ml_a(h)
                    ml_d(h)
                pe.wait_ge(ml_h, (l + 1) * NH)
                pe.wait_ge(ml_state, (l + 1) * NH)
                pe.wait_ge(conv_done, l + 1)
                for j in range(SP):
                    n, g = l * SP + j, j // 3
                    if j:
                        pe.wait_ge(ssd_h, n)
                        pe.wait_ge(ssd_state, n)
                    if j % 3 == 0:
                        bT, cT = tile(conv, B_T + g), tile(conv, C_T + g)
                        pe.matmul(bank(2, 0, SEQ), bT[:, 0:P], cT[:, 0:SEQ], start=True, stop=True)
                        pe.matmul(bank(2, SEQ, P), bT[:, P:SEQ], cT[:, P:SEQ], start=True, stop=True)
                        for st in range(2):
                            ins = pe.transpose(bank(3, st * P, P), bT[:, st * P:(st + 1) * P], ident)
                        ins.then_inc(ssd_cb, 1)
                    pe.matmul(bank(4, 0, NT), const[0:12, C_SEL2 + j * P:C_SEL2 + (j + 1) * P], spx[:, NT:2 * NT],
                              start=True, stop=True).then_inc(ssd_dt, 1)
                    for hh in range(2):
                        causal(bank(6 + hh, 0, 384), 2 * j + hh, 12, cum_a)
                    pe.wait_ge(ssd_xdt, n + 1)
                    for st in range(2):
                        ins = pe.transpose(bank(5, st * P, P), sXD[:, st * P:(st + 1) * P], ident)
                    ins.then_inc(ssd_L, 1)
                    pe.wait_ge(ssd_S, n + 1)
                    for hh in range(2):
                        dst = ps[64 * hh:64 * hh + 64, 4 * 512:4 * 512 + SEQ]
                        blocks3(dst, lambda st: sXT[:, st * P + 64 * hh:st * P + 64 * hh + 64], sS[:, hh * 384:(hh + 1) * 384])
                    for st in range(2):
                        ins = pe.matmul(bank(5, SEQ, P), sXW[:, st * P:(st + 1) * P], sBT[:, st * P:(st + 1) * P], start=st == 0, stop=st == 1)
                    ins.then_inc(ssd_y, 1)
                pe.wait_ge(ssd_h, (l + 1) * SP)
                pe.wait_ge(ssd_state, (l + 1) * SP)
                pe.wait_ge(rot_done, l + 1)
                for h in range(RH):
                    n = l * RH + h
                    if h:
                        pe.wait_ge(ret_h, n)
                    scores(2, K_R + h, Q_R + h)
                    turn_vk(5, V_R + h, K_R + h).then_inc(ret_scores, 1)
                    pe.wait_ge(ret_weighted, n + 1)
                    pe.wait_ge(ret_vk, n + 1)
                    blocks3(bank(6, 0, SEQ), lambda st: mVK[:, st * P:(st + 1) * P], mS)
                    for st in range(2):
                        ins = pe.matmul(bank(7, 0, P), mKW[:, st * P:(st + 1) * P], mVK[:, st * P:(st + 1) * P], start=st == 0, stop=st == 1)
                    ins.then_inc(ret_num, 1)
                pe.wait_ge(ret_h, (l + 1) * RH)
                for u in range(UNITS):
                    n = l * UNITS + u
                    pe.wait_ge(dec_diag, n + 1)
                    if u:
                        pe.wait_ge(dec_y, n)
                    for half in range(2):
                        ins = pe.matmul(bank(2 + half), ones, dB[:, half * 512:(half + 1) * 512], start=True, stop=True)
                    if u < NH + SP:
                        for half in range(2):
                            ins = pe.matmul(bank(4 + half), ones, dC[:, half * 512:(half + 1) * 512], start=True, stop=True)
                        ins.then_inc(dec_bc, 1)
                    else:
                        h = u - NH - SP
                        ins.then_inc(dec_bc, 1)
                        pe.wait_ge(dec_S, n + 1)
                        for b in range(NB):
                            ins = pe.matmul(bank(6, b, 1), state(u)[:, b * P:(b + 1) * P], tile(proj, Q_R + h, SEQ + b, 1),
                                            start=True, stop=True)
                        ins.then_inc(dec_bc, 1)
                pe.wait_ge(dec_y, (l + 1) * UNITS)
                for k, (n_banks, per) in enumerate(((NH, 1), (2, 3), (RH, 1))):
                    pe.wait_ge(post_sq, 3 * l + k + 1)
                    for g in range(n_banks):
                        for j in range(per):
                            ins = pe.matmul(bank(2 + g, 0, NT), ones, tile(hT, g * per + j), start=j == 0, stop=j == per - 1)
                    ins.then_inc(post_ss, 1)
                pe.wait_ge(post_y, 3 * (l + 1))
                ymap = [Q_ML + h for h in range(NH)] + [Z + j for j in range(SP)] + [Q_R + h for h in range(RH)]
                for j in range(KT):
                    s = block_in()
                    b = lin_bank(L0 + lin_of["out"] + j)
                    for k, y in enumerate(ymap):
                        ins = pe.matmul(bank(b, 0, NT), slot(s, k * P, P), tile(proj, y), start=k == 0, stop=k == 15)
                    ins.then_inc(lin_ready, 1)
                    free_slot(s)
                norm_sum(l * NORMS + 1, proj, MEM, CA_MEMN)
                pe.wait_ge(h_ready, l * NORMS + 2)
                for j in range(4):
                    s = block_in()
                    in_tiles(s, MEM, lambda k: tile(proj, CA_MEMN + k, 0, MEM), L0 + lin_of["memk"] + 2 * j)
                    free_slot(s)
                for j in range(4):
                    s = block_in()
                    for mt in range(2):
                        b = lin_bank(L0 + lin_of["memv"] + 2 * j + mt)
                        for k in range(KT):
                            ins = pe.matmul(bank(b, 0, 256), tile(proj, CA_MEMN + k, mt * P, P), slot(s, k * 256, 256),
                                            start=k == 0, stop=k == KT - 1)
                        ins.then_inc(lin_ready, 1)
                    free_slot(s)
                norm_sum(l * NORMS + 2, hT)
                pe.wait_ge(h_ready, l * NORMS + 3)
                for j in range(4):
                    s = block_in()
                    in_tiles(s, NT, lambda k: tile(hT, k), L0 + lin_of["q"] + 2 * j)
                    free_slot(s)
                for n in (L0 + lin_of["q"] + 6, L0 + lin_of["q"] + 7):
                    pe.wait_ge(lin_free[n % 2], n // 2 + 1)
                for h in range(CAH):
                    n = l * CAH + h
                    if h:
                        pe.wait_ge(ca_oc, n)
                    for qt in range(2):
                        for kk in range(2):
                            ins = pe.matmul(bank(2, qt * MEM, MEM), tile(proj, CA_Q + 2 * h + kk, qt * P, P),
                                            tile(proj, CA_K + 2 * h + kk, 0, MEM), start=kk == 0, stop=kk == 1)
                    ins.then_inc(ca_scores, 1)
                    pe.wait_ge(ca_p, n + 1)
                    for mt in range(2):
                        for qt in range(2):
                            ins = pe.transpose(bank(3, mt * SEQ + qt * P, P), caP[:, qt * MEM + mt * P:qt * MEM + (mt + 1) * P], ident)
                    ins.then_inc(ca_pt, 1)
                    pe.wait_ge(ca_ptc, n + 1)
                    for dt in range(2):
                        for mt in range(2):
                            v0 = CA_V * NT + mt * D_MODEL + (2 * h + dt) * P
                            ins = pe.matmul(bank(4, dt * SEQ, SEQ), proj[:, v0:v0 + P], caPT[:, mt * SEQ:(mt + 1) * SEQ],
                                            start=mt == 0, stop=mt == 1)
                    ins.then_inc(ca_o, 1)
                for b in range(NB):
                    pe.wait_ge(cache_in[b % CACHE_SLOTS], 16 * cache_count(l, b))
                    kc = cache(b)
                    for mt in range(2):
                        for h in range(CAH):
                            for kk in range(2):
                                ins = pe.matmul(bank(5, mt * 32 + h * NB + b, 1), kc[:, (2 * h + kk) * MEM + mt * P:(2 * h + kk) * MEM + (mt + 1) * P],
                                                tile(proj, CA_Q + 2 * h + kk, SEQ + b, 1), start=kk == 0, stop=kk == 1)
                    ins.then_inc(cs_k, 1)
                pe.wait_ge(cs_sc, l + 1)
                for mt in range(2):
                    ins = pe.transpose(bank(6, mt * P, P, 32), csS[:, mt * 32:(mt + 1) * 32], ident)
                ins.then_inc(cs_turn, 1)
                pe.wait_ge(cs_p, l + 1)
                for mt in range(2):
                    ins = pe.transpose(bank(7, mt * 32, 32), csP[:, mt * P:(mt + 1) * P], ident[0:32, 0:32])
                ins.then_inc(cs_back, 1)
                pe.wait_ge(cs_backc, l + 1)
                for b in range(NB):
                    pe.wait_ge(cache_in[(NB + b) % CACHE_SLOTS], 16 * cache_count(l, NB + b))
                    vc = cache(NB + b)
                    for d in range(KT):
                        for mt in range(2):
                            ins = pe.matmul(bank(5, 128 + d * NB + b, 1), vc[:, mt * D_MODEL + d * P:mt * D_MODEL + (d + 1) * P],
                                            csPT[:, mt * 32 + (d // 2) * NB + b:mt * 32 + (d // 2) * NB + b + 1], start=mt == 0, stop=mt == 1)
                    ins.then_inc(cs_v, 1)
                pe.wait_ge(ca_oc, (l + 1) * CAH)
                pe.wait_ge(cs_oc, l + 1)
                for j in range(4):
                    s = block_in()
                    in_tiles(s, NT, lambda k: tile(proj, CA_O + k), L0 + lin_of["o"] + 2 * j)
                    free_slot(s)
                norm_sum(l * NORMS + 3, hT)
                pe.wait_ge(h_ready, l * NORMS + 4)
                moe = l % 2 == 1
                if moe:
                    for tt, (lo, w) in enumerate(((0, P), (P, P), (SEQ, NB))):
                        for k in range(KT):
                            ins = pe.matmul(bank(7, tt * NE, NE, w), tile(hT, k, lo, w), wrt[:, k * NE:(k + 1) * NE],
                                            start=k == 0, stop=k == KT - 1)
                    ins.then_inc(rt_logits, 1)
                    pe.wait_ge(rt_comb, 1)
                    for tt, (lo, w) in enumerate(((0, P), (P, P), (SEQ, NB))):
                        ins = pe.transpose(bank(7, 64 + lo, w, NE), lg[0:w, tt * NE:(tt + 1) * NE], ident[0:w, 0:w])
                    ins.then_inc(rt_turn, 1)
                    pe.wait_ge(rt_combT, 1)
                gu0, dn0, ne = (0, 0, 2) if l == 0 else (2 * F_TILES, 2 * KT, NE)
                for n in (L0 + LIN - 2, L0 + LIN - 1):
                    pe.wait_ge(lin_free[n % 2], n // 2 + 1)
                r.begin(0, EXPERT_BLOCKS, 2)
                with pe.Fori(0, ne) as e:
                    r.i = e
                    for f in range(F_TILES):
                        s = block_in()
                        if f >= 2:
                            pe.wait_ge(gu_free, e * F_TILES + (gu0 + f - 1))
                        for g in range(2):
                            for k in range(KT):
                                ins = pe.matmul(bank(2 * g + f % 2, 0, NT), slot(s, k * 256 + g * P, P), tile(hT, k),
                                                start=k == 0, stop=k == KT - 1)
                        ins.then_inc(gu_ready, 1)
                        free_slot(s)
                        if moe and f == 0:
                            pe.wait_ge(ex_mask, e + 1)
                            pe.matmul(bank(6, 0, NT), ones[0:NE, :], combM, start=True, stop=True).then_inc(ex_bc, 1)
                    pe.wait_ge(gu_free, e * F_TILES + (gu0 + F_TILES))
                    for j in range(KT):
                        s = block_in()
                        if j >= 2:
                            pe.wait_ge(down_free, e * KT + (dn0 + j - 1))
                        for k in range(F_TILES):
                            ins = pe.matmul(bank(4 + j % 2, 0, NT), slot(s, k * P, P), tile(proj, k), start=k == 0, stop=k == F_TILES - 1)
                        ins.then_inc(down_ready, 1)
                        free_slot(s)
                    r.skip()
                    r.skip()
                r.end(ne)
            norm_sum(DEPTH * NORMS, hT)

        @block.scalar
        def _(act):
            act.preload_act_table_set("natural_log_exp_and_others")
            st = Steps(act, act_step)
            act.wait_ge(dma_const, 64)
            act.wait_ge(dma_small, 96)
            eps = c(C_EPS, 1)

            def norm(k, src, sq, w=NT, s0=0, q0=0):
                act.activation(tiles3(sq, q0, KT, 0, w), tiles3(src, s0, KT, 0, w), ACT.Square).then_inc(sq_ready, 1)
                act.wait_ge(ss_ready, k + 1)
                st(act.activation(rstd[:, 0:w], bank(6, 0, w), ACT.Ln, bias=eps, scale=1.0 / D_MODEL))
                act.activation(rstd[:, 0:w], rstd[:, 0:w], ACT.Exp, scale=-0.5).then_inc(rs_ready, 1)

            def take(n, dst, src):
                act.wait_ge(lin_ready, n + 1)
                act.activation(dst, src, ACT.Copy).then_inc(lin_free[n % 2], 1)

            for l in range(DEPTH):
                L0 = l * LIN
                if l:
                    act.wait_ge(x_ready, 3 * l)
                norm(l * NORMS, xT, hT)
                with act.Fori(0, IN_ITERS) as i:
                    for j in range(2 * SLOTS):
                        n = L0 + j
                        act.wait_ge(lin_ready, i * (2 * SLOTS) + (n + 1))
                        act.activation(proj[:, bass.ds(i * (2 * SLOTS * NT) + j * NT, NT)], bank(n % 2, 0, NT), ACT.Copy).then_inc(lin_free[n % 2], 1)
                act.wait_ge(lin_free[(L0 + 55) % 2], (L0 + 55) // 2 + 1)
                act.wait_ge(lin_free[(L0 + 54) % 2], (L0 + 54) // 2 + 1)
                act.activation(proj[:, K_ML * NT:V_ML * NT], proj[:, K_ML * NT:V_ML * NT], ACT.Copy, scale=P ** -0.5).then_inc(k_scaled, 1)
                act.activation(proj[:, O_ML * NT:Z * NT], proj[:, O_ML * NT:Z * NT], ACT.Exp, scale=-1.0)
                act.activation(tmp[:, 0:6 * NT], proj[:, Z * NT:XBC * NT], ACT.Exp, scale=-1.0)
                act.activation(tmp[:, 6 * NT:10 * NT], proj[:, G_R * NT:N_PROJ * NT], ACT.Exp, scale=-1.0).then_inc(exps_ready, 1)
                act.wait_ge(gate_abs, l + 1)
                act.activation(spu[:, :], spa[:, :], ACT.Exp, scale=-1.0).then_inc(gate_exp, 1)
                act.activation(small[:, 0:1], alog[:, l:l + 1], ACT.Exp)
                act.wait_ge(gate_one, l + 1)
                act.activation(spl[:, :], spa[:, :], ACT.Ln).then_inc(gate_log, 1)
                act.wait_ge(gate_rows, l + 1)
                act.activation(smR[:, :], smR[:, :], ACT.Exp)
                act.activation(small[:, 8:16], lda[:, SEQ:NT], ACT.Exp).then_inc(gate_sexp, 1)
                act.wait_ge(conv_acc, l + 1)
                act.activation(tmp[:, :], conv[:, :], ACT.Exp, scale=-1.0).then_inc(conv_exp, 1)
                act.wait_ge(gate_cols_in, l + 1)
                for h in range(NH):
                    n = l * NH + h
                    act.wait_ge(ml_scores, n + 1)
                    if h:
                        act.wait_ge(ml_h, n)
                    for q, (lo, hi) in enumerate(((0, P), (P, SEQ), (SEQ, 384))):
                        act.activation(mW[:, lo:hi], bank(3, lo, hi - lo), ACT.Exp, bias=gcol[:, 6 * q + h:6 * q + h + 1])
                    act.activation(mEM, bank(4, 0, SEQ), ACT.Exp)
                    act.activation(mVK, bank(5), ACT.Copy).then_inc(ml_w, 1)
                    act.wait_ge(ml_num, n + 1)
                    act.activation(tile(proj, K_ML + h, 0, P), bank(7, 0, P), ACT.Copy)
                    act.activation(npr[:, h:h + 1], bank(7, P, 1), ACT.Copy).then_inc(ml_state, 1)
                for j in range(SP):
                    n = l * SP + j
                    if j % 3 == 0:
                        act.wait_ge(ssd_cb, 2 * l + j // 3 + 1)
                        act.activation(sBT, bank(3, 0, SEQ), ACT.Copy)
                    act.wait_ge(ssd_L, n + 1)
                    act.activation(sXT, bank(5, 0, SEQ), ACT.Copy)
                    for hh in range(2):
                        for q, (lo, hi) in enumerate(((0, P), (P, SEQ), (SEQ, 384))):
                            col = 18 + 12 * q + 2 * j + hh
                            ins = act.activation(sL[:, hh * 384 + lo:hh * 384 + hi], bank(6 + hh, lo, hi - lo), ACT.Exp, bias=gcol[:, col:col + 1])
                    ins.then_inc(ssd_w, 1)
                    act.wait_ge(ssd_y, n + 1)
                    act.activation(tile(proj, V_ML + j, 0, P), bank(5, SEQ, P), ACT.Copy).then_inc(ssd_state, 1)
                for h in range(RH):
                    n = l * RH + h
                    act.wait_ge(ret_scores, n + 1)
                    act.activation(mVK, bank(5), ACT.Copy).then_inc(ret_vk, 1)
                    act.wait_ge(ret_num, n + 1)
                    act.activation(tile(proj, Q_R + h, 0, SEQ), bank(6, 0, SEQ), ACT.Copy)
                    act.activation(tile(proj, K_R + h, 0, P), bank(7, 0, P), ACT.Copy).then_inc(ret_h, 1)
                act.wait_ge(dec_y, (l + 1) * UNITS)
                for k, (y0, nt, n_banks, width) in enumerate(((Q_ML, NH, NH, P), (Z, SP, 2, 3 * P), (Q_R, RH, RH, P))):
                    if k:
                        act.wait_ge(post_y, 3 * l + k)
                    act.activation(hT[:, 0:nt * NT], proj[:, y0 * NT:(y0 + nt) * NT], ACT.Square).then_inc(post_sq, 1)
                    act.wait_ge(post_ss, 3 * l + k + 1)
                    for g in range(n_banks):
                        ins = act.activation(tile(tmp, g), bank(2 + g, 0, NT), ACT.Ln, bias=eps, scale=1.0 / width)
                    st(ins)
                    act.activation(tmp[:, 0:n_banks * NT], tmp[:, 0:n_banks * NT], ACT.Exp, scale=-0.5).then_inc(post_rs, 1)
                act.wait_ge(mem_in, 16 * (l + 1))
                norm(l * NORMS + 1, proj, proj, MEM, CA_MEM, CA_MEMN)
                for j in range(KT):
                    n = L0 + lin_of["memk"] + j
                    take(n, tile(proj, CA_K + j, 0, MEM), bank(n % 2, 0, MEM))
                for j in range(8):
                    n = L0 + lin_of["memv"] + j
                    v0 = CA_V * NT + (j % 2) * D_MODEL + (j // 2) * 256
                    take(n, proj[:, v0:v0 + 256], bank(n % 2, 0, 256))
                act.wait_ge(x_ready, 3 * l + 1)
                norm(l * NORMS + 2, xT, hT)
                for j in range(KT):
                    n = L0 + lin_of["q"] + j
                    take(n, tile(proj, CA_Q + j), bank(n % 2, 0, NT))
                for h in range(CAH):
                    n = l * CAH + h
                    act.wait_ge(ca_max, n + 1)
                    for qt in range(2):
                        ins = act.activation(caP[:, qt * MEM:(qt + 1) * MEM], bank(2, qt * MEM, MEM), ACT.Exp, bias=sml[:, qt:qt + 1],
                                             scale=1.0 / 16, accum_out=sml[:, 2 + qt:3 + qt])
                    ins.then_inc(ca_exp, 1)
                    act.wait_ge(ca_pt, n + 1)
                    act.activation(caPT, bank(3), ACT.Copy).then_inc(ca_ptc, 1)
                    act.wait_ge(ca_o, n + 1)
                    act.activation(tiles3(proj, CA_O + 2 * h, 2, 0, SEQ), bank(4).rearrange("p (a t) -> p a t", a=2), ACT.Copy).then_inc(ca_oc, 1)
                act.wait_ge(cs_k, (l + 1) * NB)
                act.activation(csS, bank(5, 0, 64), ACT.Copy).then_inc(cs_sc, 1)
                act.wait_ge(cs_max, l + 1)
                act.activation(csP, bank(6, 0, MEM, 32), ACT.Exp, bias=sml[0:32, 8:9], scale=1.0 / 16, accum_out=sml[0:32, 9:10]).then_inc(cs_exp, 1)
                act.wait_ge(cs_back, l + 1)
                act.activation(csPT, bank(7, 0, 64), ACT.Copy).then_inc(cs_backc, 1)
                act.wait_ge(cs_v, (l + 1) * NB)
                act.activation(tiles3(proj, CA_O, KT, SEQ, NB), bank(5, 128, 64).rearrange("p (a t) -> p a t", a=KT), ACT.Copy).then_inc(cs_oc, 1)
                act.wait_ge(x_ready, 3 * l + 2)
                norm(l * NORMS + 3, xT, hT)
                if l % 2 == 1:
                    act.wait_ge(rt_max, 1)
                    act.activation(conv[:, 24:48], conv[:, 24:48], ACT.Exp).then_inc(rt_exp, 1)
                gu0, ne = (0, 2) if l == 0 else (2 * F_TILES, NE)
                with act.Fori(0, ne) as e:
                    for f in range(F_TILES):
                        act.wait_ge(gu_ready, e * F_TILES + (gu0 + f + 1))
                        if f >= 2:
                            act.wait_ge(gu_free, e * F_TILES + (gu0 + f - 1))
                        act.activation(sig[f % 2], bank(f % 2, 0, NT), ACT.Exp, scale=-1.0).then_inc(gu_exp, 1)
            act.wait_ge(x_ready, 3 * DEPTH)
            norm(DEPTH * NORMS, xT, hT)

        @block.vector
        def _(dve):
            st = Steps(dve, dve_step)
            st(dve.memset(spx[:, :], 0.0))
            dve.wait_ge(dma_const, 64)
            dve.wait_ge(dma_small, 96)

            def norm(k, src, dst, gain, w=NT, s0=0, d0=0):
                dve.wait_ge(rs_ready, k + 1)
                for j in range(KT):
                    ins = dve.scalar_tensor_tensor(out=tile(dst, d0 + j, 0, w), in0=tile(src, s0 + j, 0, w), scalar=gain(j),
                                                   in1=rstd[:, 0:w], op0=ALU.mult, op1=ALU.mult)
                ins.then_inc(h_ready, 1)

            def add_to_x(n, j, last):
                dve.wait_ge(lin_ready, n + 1)
                dve.tensor_tensor(tile(xT, j), bank(n % 2, 0, NT), tile(xT, j), ALU.add).then_inc(lin_free[n % 2], 1)
                if last:
                    for k in (n - 1, n):
                        dve.wait_ge(lin_free[k % 2], k // 2 + 1)
                    dve.sem_inc(x_ready, 1)

            for l in range(DEPTH):
                L0 = l * LIN
                norm(l * NORMS, xT, hT, lambda j: pcol(l, G_MIX + j))
                n = L0 + lin_of["gates"]
                dve.wait_ge(lin_ready, n + 1)
                b = n % 2
                dve.tensor_scalar(gI[:, :], bank(b, 0, NT, 6), hpar[0:6, 3 * l:3 * l + 1], None, ALU.add)
                dve.tensor_scalar(spx[0:6, 0:NT], bank(b, 0, NT, 6, 32), hpar[32:38, 3 * l:3 * l + 1], -1.0, ALU.add, ALU.mult)
                dve.tensor_scalar(spx[:, NT:2 * NT], bank(b, 0, NT, 12, 64), hpar[64:76, 3 * l:3 * l + 1], None, ALU.add).then_inc(lin_free[b], 1)
                dve.wait_ge(lin_free[b], n // 2 + 1)
                dve.scalar_tensor_tensor(out=spa[:, :], in0=spx[:, :], scalar=-1.0, in1=spx[:, :], op0=ALU.mult, op1=ALU.max).then_inc(gate_abs, 1)
                dve.wait_ge(gate_exp, l + 1)
                st(dve.tensor_scalar(spd[:, :], spu[:, :], 1.0, -1.0, ALU.add, ALU.add))
                dve.tensor_scalar(spa[:, :], spu[:, :], 1.0, None, ALU.add).then_inc(gate_one, 1)
                dve.wait_ge(gate_log, l + 1)
                st(dve.tensor_scalar(spa[:, :], spd[:, :], 0.0, None, ALU.is_equal))
                st(dve.tensor_tensor(spd[:, :], spd[:, :], spa[:, :], ALU.add))
                st(dve.tensor_tensor(spl[:, :], spl[:, :], spa[:, :], ALU.add))
                st(dve.reciprocal(spd[:, :], spd[:, :]))
                st(dve.tensor_tensor(spl[:, :], spl[:, :], spd[:, :], ALU.mult))
                st(dve.tensor_tensor(spl[:, :], spl[:, :], spu[:, :], ALU.mult))
                st(dve.scalar_tensor_tensor(out=spx[:, :], in0=spx[:, :], scalar=0.0, in1=spl[:, :], op0=ALU.max, op1=ALU.add))
                on = const[0:12, C_ONES:C_ONES + P]
                for ch in range(2):
                    a, z = ch * P, (ch + 1) * P
                    st(dve.tensor_tensor_scan(cum_f[:, a:z], on[0:6, :], spx[0:6, a:z], 0.0, ALU.mult, ALU.subtract))
                g0, g1 = grow[:, 0:P], grow[:, SEQ:384]
                st(dve.tensor_tensor(g0, gI[:, 0:P], cum_f[:, 0:P], ALU.subtract))
                st(dve.tensor_tensor(g1, gI[:, P:SEQ], cum_f[:, P:SEQ], ALU.subtract))
                st(dve.tensor_tensor_scan(run_max[:, 0:P], g0, g0, 0.0, ALU.max, ALU.max))
                st(dve.tensor_tensor(small[0:6, 1:2], cum_f[:, P - 1:P], run_max[:, P - 1:P], ALU.add))
                st(dve.tensor_tensor_scan(run_max[:, P:SEQ], g1, g1, small[0:6, 1:2], ALU.max, ALU.max))
                st(dve.tensor_scalar(negM[:, :], run_max[:, :], -1.0, None, ALU.mult))
                st(dve.scalar_tensor_tensor(out=negm[:, :], in0=cum_f[:, :], scalar=-1.0, in1=run_max[:, :], op0=ALU.mult, op1=ALU.subtract))
                st(dve.tensor_scalar(grow[:, P:SEQ], g0, cum_f[:, P - 1:P], None, ALU.add))
                st(dve.tensor_scalar(small[0:6, 2:3], negm[:, SEQ - 1:SEQ], -1.0, None, ALU.mult))
                st(dve.tensor_tensor(small[0:6, 16:24], m0[:, l * NB:(l + 1) * NB], spx[0:6, SEQ:NT], ALU.subtract))
                st(dve.tensor_tensor(small[0:6, 24:32], small[0:6, 16:24], gI[:, SEQ:NT], ALU.max))
                st(dve.tensor_tensor(smR[:, 0:8], gI[:, SEQ:NT], small[0:6, 24:32], ALU.subtract))
                st(dve.tensor_tensor(smR[:, 8:16], small[0:6, 16:24], small[0:6, 24:32], ALU.subtract))
                st(dve.tensor_scalar(smR[:, 16:24], small[0:6, 24:32], -1.0, None, ALU.mult))
                st(dve.tensor_scalar(lda[:, :], spx[:, NT:2 * NT], small[:, 0:1], -1.0, ALU.mult, ALU.mult))
                for ch in range(2):
                    a, z = ch * P, (ch + 1) * P
                    st(dve.tensor_tensor_scan(cum_a[:, a:z], on, lda[:, a:z], 0.0, ALU.mult, ALU.add))
                    st(dve.tensor_scalar(arow[:, 2 * a:2 * a + P], cum_a[:, a:z], -1.0, None, ALU.mult))
                dve.tensor_scalar(arow[:, P:SEQ], arow[:, 0:P], cum_a[:, P - 1:P], None, ALU.add).then_inc(gate_rows, 1)
                for j in range(2 * RH):
                    n = l * 2 * RH + j
                    cs, sn = (C_COS, C_SIN) if j < RH else (C_COSK, C_SINK)
                    dve.wait_ge(rot_ready, n + 1)
                    dve.tensor_tensor(tile(hT, j % 2), bank(4 + n % 2, 0, NT), c(sn, NT), ALU.mult).then_inc(rot_used, 1)
                    dve.wait_ge(rot_used, n + 1)
                    st(dve.tensor_tensor(tile(proj, Q_R + j), tile(proj, Q_R + j), c(cs, NT), ALU.mult))
                    ins = dve.tensor_tensor(tile(proj, Q_R + j), tile(proj, Q_R + j), tile(hT, j % 2), ALU.add)
                ins.then_inc(rot_done, 1)
                dve.wait_ge(exps_ready, l + 1)
                o3 = proj[:, O_ML * NT:Z * NT]
                st(dve.tensor_scalar(o3, o3, 1.0, None, ALU.add))
                st(dve.reciprocal(o3, o3))
                st(dve.tensor_scalar(tmp[:, :], tmp[:, :], 1.0, None, ALU.add))
                st(dve.reciprocal(tmp[:, :], tmp[:, :]))
                z3, g3 = proj[:, Z * NT:XBC * NT], proj[:, G_R * NT:N_PROJ * NT]
                st(dve.tensor_tensor(z3, z3, tmp[:, 0:6 * NT], ALU.mult))
                st(dve.tensor_tensor(g3, g3, tmp[:, 6 * NT:], ALU.mult))
                dve.wait_ge(gate_cols, l + 1)
                dve.tensor_copy(gcol[:, :], bank(2, 0, 54)).then_inc(gate_cols_in, 1)
                dve.wait_ge(gate_bc, l + 1)
                dve.tensor_copy(gbc[:, :], bank(3, 0, 192)).then_inc(gate_bc_in, 1)
                dve.wait_ge(gate_bc_in, l + 1)
                gb = gbc[:, 0:144].rearrange("p (h q b) -> p h q b", h=NH, q=3)
                dve.wait_ge(k_scaled, l + 1)

                def r3(buf, n=6):
                    return buf.rearrange("p (h b) -> p h b", h=n)

                nn, vv = r3(nnew[:, :]), r3(vA[:, :])
                st(dve.tensor_tensor(nn, r3(nst[:, l * 48:(l + 1) * 48]), gb[:, :, 1, :], ALU.mult))
                st(dve.tensor_tensor(r3(yT2[:, :]), tiles3(proj, K_ML, NH, SEQ, NB), gb[:, :, 0, :], ALU.mult))
                st(dve.tensor_tensor(nn, nn, r3(yT2[:, :]), ALU.add))
                st(dve.tensor_tensor(vv, tiles3(proj, V_ML, NH, SEQ, NB), gb[:, :, 0, :], ALU.mult))
                dve.tensor_tensor(r3(yT2[:, :]), nn, tiles3(proj, Q_ML, NH, SEQ, NB), ALU.mult).then_inc(nq_ready, 1)
                dve.wait_ge(nden_ready, l + 1)
                st(dve.scalar_tensor_tensor(out=r3(rden[:, :]), in0=r3(bank(6, 0, 48)), scalar=-1.0, in1=gb[:, :, 2, :], op0=ALU.mult, op1=ALU.max))
                st(dve.tensor_tensor(rden[:, :], bank(6, 0, 48), rden[:, :], ALU.max))
                dve.reciprocal(rden[:, :], rden[:, :]).then_inc(nden_done, 1)
                for k in range(CONV_T):
                    u, y = tile(proj, XBC + k), tile(conv, k)

                    def tap(i):
                        return pcol(l, CONV_K + 4 * k + i)
                    st(dve.tensor_scalar(y, u, tap(3), pcol(l, CONV_B + k), ALU.mult, ALU.add))
                    for d in range(1, 4):
                        w = cst[:, ((l * CONV_T + k) * 3 + 3 - d) * NB:((l * CONV_T + k) * 3 + 4 - d) * NB]
                        dve.scalar_tensor_tensor(out=y[:, d:SEQ], in0=u[:, 0:SEQ - d], scalar=tap(3 - d), in1=y[:, d:SEQ], op0=ALU.mult, op1=ALU.add)
                        st(dve.scalar_tensor_tensor(out=y[:, SEQ:NT], in0=w, scalar=tap(3 - d), in1=y[:, SEQ:NT], op0=ALU.mult, op1=ALU.add))
                st(dve.tensor_copy(cvp[:, :].rearrange("p (c i) -> p c i", i=3), tiles3(proj, XBC, CONV_T, SEQ - 3, 3)))
                old = cst[:, l * CONV_T * 24:(l + 1) * CONV_T * 24].rearrange("p (c i b) -> p c i b", c=CONV_T, i=3)
                for i in range(2):
                    st(dve.tensor_copy(old[:, :, i, :], old[:, :, i + 1, :]))
                st(dve.tensor_copy(old[:, :, 2, :], tiles3(proj, XBC, CONV_T, SEQ, NB)))
                dve.sem_inc(conv_acc, 1)
                dve.wait_ge(conv_exp, l + 1)
                st(dve.tensor_scalar(tmp[:, :], tmp[:, :], 1.0, None, ALU.add))
                st(dve.reciprocal(tmp[:, :], tmp[:, :]))
                dve.tensor_tensor(conv[:, :], conv[:, :], tmp[:, :], ALU.mult).then_inc(conv_done, 1)
                dve.wait_ge(conv_done, l + 1)
                for h in range(NH):
                    n = l * NH + h
                    dve.wait_ge(ml_w, n + 1)
                    dve.tensor_tensor(mS, mW, bank(2, 0, 384), ALU.mult)
                    dve.tensor_scalar(mKW[:, 0:P], mVK[:, SEQ:384], mW[:, SEQ - 1:SEQ], None, ALU.mult)
                    dve.tensor_scalar(mKW[:, P:SEQ], mVK[:, 384:512], mW[:, 383:384], None, ALU.mult).then_inc(ml_weighted, 1)
                    dve.wait_ge(ml_num, n + 1)
                    st(dve.scalar_tensor_tensor(out=mDN, in0=bank(6, SEQ, SEQ), scalar=-1.0, in1=mEM, op0=ALU.mult, op1=ALU.max))
                    st(dve.tensor_tensor(mDN, bank(6, SEQ, SEQ), mDN, ALU.max))
                    st(dve.reciprocal(mDN, mDN))
                    dve.tensor_tensor(tile(proj, Q_ML + h, 0, SEQ), bank(6, 0, SEQ), mDN, ALU.mult).then_inc(ml_h, 1)
                dve.wait_ge(ml_h, (l + 1) * NH)
                for j in range(SP):
                    n, g = l * SP + j, j // 3
                    dve.wait_ge(ssd_dt, n + 1)
                    dve.tensor_tensor(sXD, tile(conv, j), bank(4, 0, NT), ALU.mult).then_inc(ssd_xdt, 1)
                    dve.wait_ge(ssd_xdt, n + 1)
                    dve.tensor_copy(xds[:, j * NB:(j + 1) * NB], sXD[:, SEQ:NT])
                    dve.wait_ge(ssd_w, n + 1)
                    for hh in range(2):
                        dve.tensor_tensor(sS[:, hh * 384:(hh + 1) * 384], sL[:, hh * 384:(hh + 1) * 384], bank(2, 0, 384), ALU.mult)
                        for s_, at in ((0, SEQ - 1), (1, 383)):
                            ins = dve.tensor_scalar(sXW[:, s_ * P + 64 * hh:s_ * P + 64 * hh + 64], sXT[:, s_ * P + 64 * hh:s_ * P + 64 * hh + 64],
                                                    sL[:, hh * 384 + at:hh * 384 + at + 1], None, ALU.mult)
                    ins.then_inc(ssd_S, 1)
                    dve.wait_ge(ssd_y, n + 1)
                    st(dve.scalar_tensor_tensor(out=sY, in0=tile(conv, j, 0, SEQ), scalar=pcol(l, D_SKIP + j), in1=bank(4, 0, SEQ), op0=ALU.mult, op1=ALU.add))
                    dve.tensor_tensor(tile(proj, Z + j, 0, SEQ), tile(proj, Z + j, 0, SEQ), sY, ALU.mult).then_inc(ssd_h, 1)
                for h in range(RH):
                    n = l * RH + h
                    dve.wait_ge(ret_scores, n + 1)
                    if h == 0:
                        dve.wait_ge(ssd_state, (l + 1) * SP)
                    w0 = C_RET + h * 384
                    dve.tensor_tensor(mS, bank(2, 0, 384), c(w0, 384), ALU.mult)
                    dve.wait_ge(ret_vk, n + 1)
                    dve.tensor_scalar(mKW[:, 0:P], mVK[:, SEQ:384], c(w0 + SEQ - 1, 1), None, ALU.mult)
                    dve.tensor_scalar(mKW[:, P:SEQ], mVK[:, 384:512], c(w0 + 383, 1), None, ALU.mult).then_inc(ret_weighted, 1)
                dve.wait_ge(ret_h, (l + 1) * RH)
                for u in range(UNITS):
                    n = l * UNITS + u
                    S = state(u)
                    S3 = S.rearrange("p (b f) -> p b f", b=NB)
                    dve.wait_ge(state_in[u % STATE_SLOTS], 16 * state_count(l, u))
                    if u < NH:
                        dec, a = gb[:, u, 1, :], vA[:, u * NB:(u + 1) * NB]
                    elif u < NH + SP:
                        j = u - NH
                        dec, a = gbc[:, 144 + j * NB:144 + (j + 1) * NB], xds[:, j * NB:(j + 1) * NB]
                    else:
                        h = u - NH - SP
                        dec, a = None, tile(proj, K_R + h, SEQ, NB)
                    if dec is None:
                        gamma = float(np.float32(1.0) - np.float32(2.0) ** np.float32(-5.0 - h))
                        st(dve.tensor_scalar(S, S, gamma, None, ALU.mult))
                    else:
                        st(dve.tensor_tensor(S3, S3, dec.unsqueeze(2).to_broadcast([P, NB, P]), ALU.mult))
                    bcs = n + sum(1 for q in range(n) if q % UNITS >= NH + SP)
                    dve.wait_ge(dec_bc, bcs + 1)
                    for b in range(NB):
                        ins = dve.scalar_tensor_tensor(out=S[:, b * P:(b + 1) * P], in0=bank(2, b * P, P), scalar=a[:, b:b + 1],
                                                       in1=S[:, b * P:(b + 1) * P], op0=ALU.mult, op1=ALU.add)
                    ins.then_inc(dec_S, 1)
                    dve.wait_ge(dec_S, n + 1)
                    if u < NH + SP:
                        st(dve.tensor_tensor(dB, S, ps[:, 4 * 512:6 * 512], ALU.mult))
                        st(dve.tensor_reduce(yT[:, :], dB.rearrange("p (b f) -> p b f", b=NB), AX.X, ALU.add))
                    if u < NH:
                        dve.tensor_tensor(tile(proj, Q_ML + u, SEQ, NB), yT[:, :], rden[:, u * NB:(u + 1) * NB], ALU.mult).then_inc(dec_y, 1)
                    elif u < NH + SP:
                        st(dve.scalar_tensor_tensor(out=yT[:, :], in0=tile(conv, j, SEQ, NB), scalar=pcol(l, D_SKIP + j), in1=yT[:, :], op0=ALU.mult, op1=ALU.add))
                        dve.tensor_tensor(tile(proj, Z + j, SEQ, NB), tile(proj, Z + j, SEQ, NB), yT[:, :], ALU.mult).then_inc(dec_y, 1)
                    else:
                        dve.wait_ge(dec_bc, bcs + 2)
                        dve.tensor_copy(tile(proj, Q_R + h, SEQ, NB), bank(6, 0, NB)).then_inc(dec_y, 1)
                for k, (y0, nt, per, g0_) in enumerate(((Q_ML, NH, 1, G_ML), (Z, SP, 3, G_SSD), (Q_R, RH, 1, G_RET))):
                    dve.wait_ge(post_rs, 3 * l + k + 1)
                    for j in range(nt):
                        ins = dve.scalar_tensor_tensor(out=tile(proj, y0 + j), in0=tile(proj, y0 + j), scalar=pcol(l, g0_ + j), in1=tile(tmp, j // per),
                                                       op0=ALU.mult, op1=ALU.mult)
                    gate = {0: o3, 2: g3}.get(k)
                    if gate is None:
                        ins.then_inc(post_y, 1)
                    else:
                        st(ins)
                        ys = proj[:, y0 * NT:(y0 + nt) * NT]
                        dve.tensor_tensor(ys, ys, gate, ALU.mult).then_inc(post_y, 1)
                for j in range(KT):
                    add_to_x(L0 + lin_of["out"] + j, j, j == KT - 1)
                norm(l * NORMS + 1, proj, proj, lambda j: pcol(l, G_MEM + j), MEM, CA_MEM, CA_MEMN)
                norm(l * NORMS + 2, xT, hT, lambda j: pcol(l, G_CA + j))
                for h in range(CAH):
                    n = l * CAH + h
                    dve.wait_ge(ca_scores, n + 1)
                    st(dve.tensor_reduce(sml[:, 4:6], bank(2).rearrange("p (a m) -> p a m", a=2), AX.X, ALU.max))
                    dve.tensor_scalar(sml[:, 0:2], sml[:, 4:6], -1.0 / 16, None, ALU.mult).then_inc(ca_max, 1)
                    dve.wait_ge(ca_exp, n + 1)
                    st(dve.reciprocal(sml[:, 6:8], sml[:, 2:4]))
                    for qt in range(2):
                        ins = dve.tensor_scalar(caP[:, qt * MEM:(qt + 1) * MEM], caP[:, qt * MEM:(qt + 1) * MEM], sml[:, 6 + qt:7 + qt], None, ALU.mult)
                    ins.then_inc(ca_p, 1)
                dve.wait_ge(cs_turn, l + 1)
                st(dve.tensor_reduce(sml[0:32, 10:11], bank(6, 0, MEM, 32), AX.X, ALU.max))
                dve.tensor_scalar(sml[0:32, 8:9], sml[0:32, 10:11], -1.0 / 16, None, ALU.mult).then_inc(cs_max, 1)
                dve.wait_ge(cs_exp, l + 1)
                st(dve.reciprocal(sml[0:32, 11:12], sml[0:32, 9:10]))
                dve.tensor_scalar(csP, csP, sml[0:32, 11:12], None, ALU.mult).then_inc(cs_p, 1)
                for j in range(KT):
                    add_to_x(L0 + lin_of["o"] + j, j, j == KT - 1)
                norm(l * NORMS + 3, xT, hT, lambda j: pcol(l, G_FFN + j))
                moe = l % 2 == 1
                if moe:
                    T3 = 3 * NE
                    st(dve.memset(conv[:, 0:T3], 0.0))
                    dve.wait_ge(rt_logits, 1)
                    dve.tensor_copy(conv[:, 0:2 * NE], bank(7, 0, 2 * NE))
                    st(dve.tensor_copy(conv[0:NB, 2 * NE:T3], bank(7, 2 * NE, NE, NB)))
                    l3 = conv[:, 0:T3].rearrange("p (t e) -> p t e", t=3)
                    x3 = conv[:, 24:48].rearrange("p (t e) -> p t e", t=3)
                    st(dve.tensor_reduce(conv[:, 48:51], l3, AX.X, ALU.max))
                    dve.tensor_tensor(x3, l3, conv[:, 48:51].unsqueeze(2).to_broadcast([P, 3, NE]), ALU.subtract).then_inc(rt_max, 1)
                    gt, eq = conv[:, 64:64 + 192], conv[:, 256:256 + 192]
                    tie = c(C_TIE, 64).rearrange("p (e j) -> p e j", e=NE)
                    for tt in range(3):
                        other = conv[:, tt * NE:(tt + 1) * NE].unsqueeze(1).to_broadcast([P, NE, NE])
                        own = conv[:, tt * NE:(tt + 1) * NE].unsqueeze(2).to_broadcast([P, NE, NE])
                        g_ = gt[:, tt * 64:(tt + 1) * 64].rearrange("p (e j) -> p e j", e=NE)
                        e_ = eq[:, tt * 64:(tt + 1) * 64].rearrange("p (e j) -> p e j", e=NE)
                        st(dve.tensor_tensor(g_, other, own, ALU.is_gt))
                        st(dve.tensor_tensor(e_, other, own, ALU.is_equal))
                        st(dve.tensor_tensor(e_, e_, tie, ALU.mult))
                        st(dve.tensor_tensor(g_, g_, e_, ALU.add))
                    st(dve.tensor_reduce(conv[:, 512:536], gt.rearrange("p (t j) -> p t j", j=NE), AX.X, ALU.add))
                    st(dve.tensor_scalar(conv[:, 512:536], conv[:, 512:536], TOP_K - 0.5, None, ALU.is_lt))
                    dve.wait_ge(rt_exp, 1)
                    st(dve.tensor_tensor(conv[:, 512:536], conv[:, 512:536], conv[:, 24:48], ALU.mult))
                    w3 = conv[:, 512:536].rearrange("p (t e) -> p t e", t=3)
                    st(dve.tensor_reduce(conv[:, 48:51], w3, AX.X, ALU.add))
                    st(dve.reciprocal(conv[:, 48:51], conv[:, 48:51]))
                    dve.tensor_tensor(l3, w3, conv[:, 48:51].unsqueeze(2).to_broadcast([P, 3, NE]), ALU.mult).then_inc(rt_comb, 1)
                    dve.wait_ge(rt_turn, 1)
                    dve.tensor_copy(combT, bank(7, 64, NT, NE)).then_inc(rt_combT, 1)
                    dve.wait_ge(rt_combT, 1)
                dve.wait_ge(dma_out, 16 * OUTS * (l + 1))
                gu0, dn0, ne = (0, 0, 2) if l == 0 else (2 * F_TILES, 2 * KT, NE)
                with dve.Fori(0, ne) as e:
                    st.begin(e, F_TILES * (4 if moe else 3) + (1 if moe else 0))
                    if moe:
                        dve.tensor_scalar(combM, combT, const[0:NE, bass.ds(e + C_ID, 1)], None, ALU.mult).then_inc(ex_mask, 1)
                        dve.wait_ge(ex_bc, e + 1)
                        st(dve.tensor_copy(combB, bank(6, 0, NT)))
                    for f in range(F_TILES):
                        dve.wait_ge(gu_exp, e * F_TILES + (gu0 + f + 1))
                        sg = sig[f % 2]
                        st(dve.tensor_scalar(sg, sg, 1.0, None, ALU.add))
                        st(dve.reciprocal(sg, sg))
                        if moe:
                            st(dve.tensor_tensor(sg, sg, combB, ALU.mult))
                        st(dve.tensor_tensor(sg, sg, bank(f % 2, 0, NT), ALU.mult))
                        dve.tensor_tensor(tile(proj, f), sg, bank(2 + f % 2, 0, NT), ALU.mult).then_inc(gu_free, 1)
                    for j in range(KT):
                        dve.wait_ge(down_ready, e * KT + (dn0 + j + 1))
                        dve.tensor_tensor(tile(xT, j), tile(xT, j), bank(4 + j % 2, 0, NT), ALU.add).then_inc(down_free, 1)
                    st.end(ne)
                dve.wait_ge(down_free, dn0 + ne * KT)
                dve.sem_inc(x_ready, 1)
            norm(DEPTH * NORMS, xT, hT, lambda j: par[:, DEPTH * N_PAR + j:DEPTH * N_PAR + j + 1])

        def store_state(pool, l, u):
            pool.wait_ge(dec_S, l * UNITS + u + 1)
            pool.dma_start(t["o_states"][l, u], state(u)).then_inc(state_out[u % STATE_SLOTS], 16)

        @block.gpsimd
        def _(pool):
            pool.wait_ge(dma_const, 64)

            def load_state(l, u):
                pool.dma_start(state(u), t["states"][l, u]).then_inc(state_in[u % STATE_SLOTS], 16)

            for l in range(DEPTH):
                if l:
                    pool.wait_ge(cs_v, l * NB)
                for u in range(STATE_SLOTS):
                    load_state(l, u)
                pool.wait_ge(gate_rows, l + 1)
                pool.dma_start(t["o_mp"][l], small[0:6, 2:3]).then_inc(dma_out, 16)
                pool.dma_start(t["o_ms"][l], small[0:6, 24:32]).then_inc(dma_out, 16)
                pool.wait_ge(conv_acc, l + 1)
                pool.dma_start(t["o_cvp"][l], cvp[:, :]).then_inc(dma_out, 16)
                pool.dma_start(t["o_cvs"][l], cst[:, l * CONV_T * 24:(l + 1) * CONV_T * 24]).then_inc(dma_out, 16)
                pool.wait_ge(nden_done, l + 1)
                pool.dma_start(t["o_ns"][l], nnew[:, :]).then_inc(dma_out, 16)
                pool.wait_ge(ml_state, (l + 1) * NH)
                pool.dma_start(t["o_np"][l], npr[:, :]).then_inc(dma_out, 16)
                pool.dma_start(t["o_pst"][l, :, 0:NH, :], tiles3(proj, K_ML, NH, 0, P)).then_inc(dma_out, 16)
                pool.wait_ge(ssd_state, (l + 1) * SP)
                pool.dma_start(t["o_pst"][l, :, NH:NH + SP, :], tiles3(proj, V_ML, SP, 0, P)).then_inc(dma_out, 16)
                pool.wait_ge(ret_h, (l + 1) * RH)
                pool.dma_start(t["o_pst"][l, :, NH + SP:UNITS, :], tiles3(proj, K_R, RH, 0, P)).then_inc(dma_out, 16)
                for u in range(UNITS):
                    n = l * UNITS + u
                    if u < NH:
                        bcol, ccol = tile(proj, K_ML + u, SEQ, NB), tile(proj, Q_ML + u, SEQ, NB)
                    elif u < NH + SP:
                        g = (u - NH) // 3
                        bcol, ccol = tile(conv, B_T + g, SEQ, NB), tile(conv, C_T + g, SEQ, NB)
                    else:
                        bcol, ccol = tile(proj, V_R + u - NH - SP, SEQ, NB), None
                    if u:
                        pool.wait_ge(dec_y, n)
                    for dst, col in ((dB, bcol), (dC, ccol)):
                        if col is not None:
                            ins = pool.tensor_tensor(dst.rearrange("p (b f) -> p b f", b=NB), ident.unsqueeze(1).to_broadcast([P, NB, P]),
                                                     col.unsqueeze(2).to_broadcast([P, NB, P]), ALU.mult)
                    ins.then_inc(dec_diag, 1)
                    if u:
                        store_state(pool, l, u - 1)
                        if u - 1 + STATE_SLOTS < UNITS:
                            pool.wait_ge(state_out[(u - 1) % STATE_SLOTS], 16 * state_count(l, u - 1))
                            load_state(l, u - 1 + STATE_SLOTS)
                pool.wait_ge(dec_y, (l + 1) * UNITS)
                store_state(pool, l, UNITS - 1)
                pool.wait_ge(lin_ready, l * LIN + lin_of["out"] + KT)
                pool.dma_start(tiles3(proj, CA_MEM, KT, 0, MEM), t["mem"]).then_inc(mem_in, 16)
                for s in range(STATE_SLOTS):
                    pool.wait_ge(state_out[s], 16 * state_count(l, UNITS - 1 - (UNITS - 1 - s) % STATE_SLOTS))
                for i in range(2 * NB):
                    if i >= CACHE_SLOTS:
                        k = i - CACHE_SLOTS
                        pool.wait_ge(*((cs_k, l * NB + k + 1) if k < NB else (cs_v, l * NB + k - NB + 1)))
                    pool.dma_start(cache(i), t["kc" if i < NB else "vc"][l, i % NB]).then_inc(cache_in[i % CACHE_SLOTS], 16)
                pool.wait_ge(h_ready, l * NORMS + 3)
                for n in (l * LIN + lin_of["memv"] + 6, l * LIN + lin_of["memv"] + 7):
                    pool.wait_ge(lin_free[n % 2], n // 2 + 1)
                pool.dma_start(t["o_mk"][l], tiles3(proj, CA_K, KT, 0, MEM)).then_inc(dma_out, 16)
                pool.dma_start(t["o_mv"][l], proj[:, CA_V * NT:CA_V * NT + 2048]).then_inc(dma_out, 16)
                pool.wait_ge(dma_out, 16 * OUTS * (l + 1))


OUTS = 11


def state_count(l, u):
    s = u % STATE_SLOTS
    per = len([q for q in range(UNITS) if q % STATE_SLOTS == s])
    return l * per + u // STATE_SLOTS + 1


def cache_count(l, i):
    s = i % CACHE_SLOTS
    per = len([q for q in range(2 * NB) if q % CACHE_SLOTS == s])
    return l * per + i // CACHE_SLOTS + 1


def constants():
    f = np.float32
    k = np.zeros((P, N_CONST), f)
    idx = np.arange(P)
    k[:, C_ID:C_ID + P] = np.eye(P, dtype=f)
    k[:, C_MASK:C_MASK + P] = np.where(idx[:, None] <= idx[None, :], 0.0, MASKED)
    k[:, C_ONES:C_ONES + P] = 1.0
    for m in range(64):
        k[m + 64, C_ROT + m] = -1.0
        k[m, C_ROT + m + 64] = 1.0
    inv = (f(10000.0) ** (-np.arange(64, dtype=f) / f(64))).astype(f)
    pos = np.concatenate([np.arange(SEQ, dtype=f), np.full(NB, PAST_LEN, f)])
    ang = (np.concatenate([inv, inv])[:, None] * pos[None, :]).astype(f)
    scale = f(P ** -0.5)
    for at, v in ((C_COS, np.cos(ang)), (C_SIN, np.sin(ang)), (C_COSK, np.cos(ang) * scale), (C_SINK, np.sin(ang) * scale)):
        k[:, at:at + NT] = v
    for h in range(RH):
        log_g = np.log1p(-np.exp2(-5.0 - h))
        rel = np.arange(SEQ)[None, :] - idx[:, None]
        w = np.where(rel >= 0, np.exp(np.maximum(rel, 0) * log_g), 0.0)
        k[:, C_RET + h * 384:C_RET + h * 384 + SEQ] = w
        k[:, C_RET + h * 384 + SEQ:C_RET + (h + 1) * 384] = w[:, 0:P]
    tie = np.arange(NE)[None, :] < np.arange(NE)[:, None]
    k[:, C_TIE:C_TIE + 64] = tie.reshape(1, 64)
    for j in range(SP):
        k[2 * j, C_SEL2 + j * P:C_SEL2 + j * P + 64] = 1.0
        k[2 * j + 1, C_SEL2 + j * P + 64:C_SEL2 + (j + 1) * P] = 1.0
    k[:, C_EPS] = EPS
    return k


def lay_out(a):
    f = np.float32

    def cols(v):
        return np.asarray(v).reshape(-1, P).T

    def fm(x):
        return np.asarray(x).T.reshape(-1, P, x.shape[0]).transpose(1, 0, 2)

    def blocks(w, width=256):
        kk, n = w.shape
        return np.asarray(w).reshape(kk // P, P, n // width, width).transpose(2, 1, 0, 3)

    o = {"const": constants()}
    x = np.concatenate([np.asarray(a["x_prompt"])[0], np.asarray(a["x_sample"])[:, 0]], 0)
    o["x"] = fm(x).reshape(P, -1)
    par = np.zeros((P, DEPTH * N_PAR + KT), f)
    for l in range(DEPTH):
        def put(at, v):
            par[:, l * N_PAR + at:l * N_PAR + at + v.shape[1]] = v
        for at, name in ((G_MIX, "norm_mix"), (G_CA, "norm_ca"), (G_MEM, "norm_mem"), (G_FFN, "norm_ffn"), (G_ML, "ml_norm"),
                         (G_SSD, "ssd_norm"), (G_RET, "ret_norm"), (CONV_B, "ssd_conv_b")):
            put(at, cols(a[name][l]))
        put(CONV_K, np.asarray(a["ssd_conv_w"][l]).reshape(4, CONV_T, P).transpose(2, 1, 0).reshape(P, -1))
        put(D_SKIP, cols(np.repeat(np.asarray(a["ssd_d"][l]), 64)))
    par[:, DEPTH * N_PAR:] = cols(a["norm_final"])
    o["par"] = par
    w_in = np.asarray(a["w_in"])
    i0 = 24 * P
    dt0 = i0 + 12 + 16 * P
    wg = np.zeros((P, DEPTH, KT, 76), f)
    hp = np.zeros((P, DEPTH, 3), f)
    w_main = []
    for l in range(DEPTH):
        w = w_in[l]
        w3 = w.reshape(KT, P, -1).transpose(1, 0, 2)
        wg[:, l, :, 0:6] = w3[:, :, i0:i0 + 6]
        wg[:, l, :, 32:38] = w3[:, :, i0 + 6:i0 + 12]
        wg[:, l, :, 64:76] = w3[:, :, dt0:dt0 + 12]
        hp[0:6, l, 0] = a["ml_i_bias"][l]
        hp[32:38, l, 0] = a["ml_f_bias"][l]
        hp[64:76, l, 0] = a["ssd_dt_bias"][l]
        main = np.concatenate([w[:, :i0], w[:, i0 + 12:dt0], w[:, dt0 + 12:]], 1)
        w_main.append(blocks(main).reshape(IN_BLOCKS, P, BLOCK))
    o["wgate"], o["hpar"], o["w_in"] = wg.reshape(P, -1), hp.reshape(P, -1), np.stack(w_main)
    o["alog"] = np.asarray(a["ssd_a_log"]).T
    o["m0"] = np.asarray(a["state_mlstm_m"]).transpose(2, 0, 1).reshape(NH, -1)
    o["nst"] = np.asarray(a["state_mlstm_n"]).transpose(3, 0, 2, 1).reshape(P, -1)
    o["cst"] = np.asarray(a["state_ssd_conv"]).reshape(DEPTH, NB, 3, CONV_T, P).transpose(4, 0, 3, 2, 1).reshape(P, -1)
    o["wrt"] = np.asarray(a["moe_w_router"])[0].reshape(KT, P, NE).transpose(1, 0, 2).reshape(P, -1)
    ml = np.asarray(a["state_mlstm_c"]).transpose(0, 2, 3, 1, 4)
    sd = np.asarray(a["state_ssd"]).reshape(DEPTH, NB, SP, P, P).transpose(0, 2, 3, 1, 4)
    rt = np.asarray(a["state_ret"]).transpose(0, 2, 3, 1, 4)
    o["states"] = np.concatenate([ml, sd, rt], 1).reshape(DEPTH, UNITS, P, NB * P)
    o["kc"] = np.asarray(a["cache_mem_k"]).reshape(DEPTH, NB, MEM, KT, P).transpose(0, 1, 4, 3, 2).reshape(DEPTH, NB, P, -1)
    o["vc"] = np.asarray(a["cache_mem_v"]).reshape(DEPTH, NB, 2, P, D_MODEL).transpose(0, 1, 3, 2, 4).reshape(DEPTH, NB, P, -1)
    o["mem"] = fm(np.asarray(a["mem_prompt"])[0])
    o["w_out"] = np.stack([blocks(w, P).reshape(KT, P, BLOCK) for w in np.asarray(a["w_out"])])
    for name, src in (("w_q", "w_ca_q"), ("w_k", "w_ca_k"), ("w_v", "w_ca_v"), ("w_o", "w_ca_o")):
        o[name] = np.stack([blocks(w).reshape(4, P, BLOCK) for w in np.asarray(a[src])])
    ff = F_TILES * P
    experts = []
    for h in range(2):
        experts.append([np.asarray(a[n])[0][:, h * ff:(h + 1) * ff] for n in ("ffn_w_gate", "ffn_w_up")]
                       + [np.asarray(a["ffn_w_down"])[0][h * ff:(h + 1) * ff]])
    for e in range(NE):
        experts.append([np.asarray(a[n])[0, e] for n in ("moe_w_gate", "moe_w_up", "moe_w_down")])
    o["w_gu"] = np.stack([np.stack([blocks(g, P), blocks(u, P)], 3).reshape(F_TILES, P, BLOCK) for g, u, _ in experts])
    o["w_down"] = np.stack([blocks(d, P).reshape(KT, P, ff) for _, _, d in experts])
    return {k: np.ascontiguousarray(v, dtype=f) for k, v in o.items()}


OUT_SHAPES = {
    "y": (P, KT * NT), "o_mp": (DEPTH, NH, 1), "o_ms": (DEPTH, NH, NB), "o_cvp": (DEPTH, P, CONV_T * 3), "o_cvs": (DEPTH, P, CONV_T * 3 * NB),
    "o_ns": (DEPTH, P, 48), "o_np": (DEPTH, P, NH), "o_pst": (DEPTH, P, UNITS, P), "o_states": (DEPTH, UNITS, P, NB * P),
    "o_mk": (DEPTH, P, KT, MEM), "o_mv": (DEPTH, P, 2 * D_MODEL),
}


def kernel(**inputs):
    from concourse import bacc
    from concourse.bass_utils import run_bass_kernel_spmd

    arrays = lay_out(inputs)
    nc = bacc.Bacc("TRN2", target_bir_lowering=False, num_devices=1)
    t = {k: nc.dram_tensor(f"{k}_dram", v.shape, F32, kind="ExternalInput").ap() for k, v in arrays.items()}
    t.update({k: nc.dram_tensor(f"{k}_dram", s, F32, kind="ExternalOutput").ap() for k, s in OUT_SHAPES.items()})
    program(nc, t)
    r = run_bass_kernel_spmd(nc, [{f"{k}_dram": v for k, v in arrays.items()}], core_ids=[0])
    o = {k: r.results[0][f"{k}_dram"] for k in OUT_SHAPES}

    y = o["y"].reshape(P, KT, NT).transpose(2, 1, 0).reshape(NT, D_MODEL)
    pst = o["o_pst"].transpose(0, 2, 1, 3)
    s = o["o_states"].reshape(DEPTH, UNITS, P, NB, P).transpose(0, 3, 1, 2, 4)
    cv = o["o_cvs"].reshape(DEPTH, P, CONV_T, 3, NB).transpose(0, 4, 3, 2, 1).reshape(DEPTH, NB, 3, -1)
    cvp = o["o_cvp"].reshape(DEPTH, P, CONV_T, 3).transpose(0, 3, 2, 1).reshape(DEPTH, 1, 3, -1)
    mk = o["o_mk"].transpose(0, 3, 2, 1).reshape(DEPTH, 1, MEM, CAH, 2 * P)
    mv = o["o_mv"].reshape(DEPTH, P, 2, D_MODEL).transpose(0, 2, 1, 3).reshape(DEPTH, 1, MEM, CAH, 2 * P)
    out = (
        y[:SEQ][None], y[SEQ:][:, None],
        pst[:, None, 0:NH], o["o_np"].transpose(0, 2, 1)[:, None], o["o_mp"][:, None, :, 0], cvp,
        pst[:, NH:NH + SP].reshape(DEPTH, 1, SH, 64, P), pst[:, None, NH + SP:], mk, mv,
        s[:, :, 0:NH], o["o_ns"].reshape(DEPTH, P, NH, NB).transpose(0, 3, 2, 1), o["o_ms"].transpose(0, 2, 1), cv,
        s[:, :, NH:NH + SP].reshape(DEPTH, NB, SH, 64, P), s[:, :, NH + SP:],
    )
    return tuple(np.ascontiguousarray(v) for v in out)
```

```python
from contextlib import ExitStack

import numpy as np

import concourse.bass as bass
from concourse import mybir

F32 = mybir.dt.float32
F32R = mybir.dt.float32r
ALU = mybir.AluOpType
ACT = mybir.ActivationFunctionType
AX = mybir.AxisListType

P = 128
D_MODEL, SEQ, DEPTH, NB = 1024, 256, 2, 8
PAST_LEN = 2048
KT = D_MODEL // P
NT = SEQ + NB
NH, SH, RH = 6, 12, 4
SP = SH // 2
NE, TOP_K = 8, 2
MEM, CAH = 256, 4
F_TILES = 11
CONV_T = 10
EPS = 1e-6
MASKED = -30000.0

Q_ML, K_ML, V_ML, O_ML, Z, XBC, Q_R, K_R, V_R, G_R, N_PROJ = 0, 6, 12, 18, 24, 30, 40, 44, 48, 52, 56
B_T, C_T = 6, 8
CA_Q, CA_K, CA_VT, CA_V, CA_O, CA_MEM, CA_MEMN, CA_MEMH = 0, 8, 16, 24, 32, 32, 40, 48
CA_OH, FF_H, FF_L = 40, 0, 11
Y_HI = (K_ML, XBC, K_R)

SLOTS = 4
BLOCK = 2048
PIECE, BUFS, AHEAD = BLOCK // 2, 4, 3
IN_BLOCKS, IN_ITERS = 28, 7
GU_BLOCKS, DOWN_BLOCKS = F_TILES, KT
PAIR_BLOCKS, PAIR_EMPTY = 2 * (GU_BLOCKS + DOWN_BLOCKS), 2
PAIR_PIECES = 2 * PAIR_BLOCKS
DOWN_REST = (F_TILES - KT) * P

G_MIX, G_CA, G_MEM, G_FFN, G_ML, G_SSD, G_RET, CONV_B, CONV_K, D_SKIP = 0, 8, 16, 24, 32, 38, 44, 48, 58, 98
N_PAR = 104
C_ID, C_MASK, C_ONES, C_ROT, C_COS, C_SIN = 0, 128, 256, 384, 512, 776
C_RET, C_TIE, C_SEL2, C_EPS, N_CONST = 1040, 1040 + 4 * 384, 1040 + 4 * 384 + 64, 2640 + 768, 2640 + 768 + 2
UNITS = NH + SP + RH
STATE_SLOTS = 3


class Steps:

    def __init__(self, eng, sem):
        self.eng, self.sem, self.n, self.i, self.per = eng, sem, 0, None, 0

    def __call__(self, ins):
        self.n += 1
        ins.then_inc(self.sem, 1)
        self.eng.wait_ge(self.sem, self.n if self.i is None else self.i * self.per + self.n)

    def begin(self, i, per):
        self.i, self.per, self.start = i, per, self.n

    def end(self, iters):
        assert self.n - self.start == self.per, (self.n - self.start, self.per)
        self.i, self.n = None, self.start + iters * self.per


class Ring:

    def __init__(self):
        self.used, self.at, self.piece, self.i, self.half = [0] * SLOTS, 0, 0, None, 0

    def block(self):
        if self.at in EMPTY_PLACES:
            self.at += PAIR_EMPTY
        s = self.at % SLOTS
        self.at, self.used[s] = self.at + 1, self.used[s] + 1
        return s, self.before(s)

    def before(self, s):
        return self.used[s] - 1 if self.i is None else self.i * self.per[s] + (self.used[s] - 1)

    def next_piece(self):
        if self.half == 0:
            if self.at in CACHE_PLACES:
                self.at, self.used = self.at + 2 * NB, [u + 2 * NB // SLOTS for u in self.used]
            self.s, _ = self.block()
        q = self.piece if self.i is None else self.i * self.pieces + self.piece
        out = self.s, self.before(self.s), self.half, q, self.piece % BUFS
        self.half, self.piece = 1 - self.half, self.piece + 1
        return out

    def begin(self, blocks):
        self.pieces, self.per, self.first, self.start = 2 * blocks, slot_uses(blocks), list(self.used), self.piece

    def end(self, iters):
        self.used = [b + iters * (u - b) for b, u in zip(self.first, self.used)]
        self.piece = self.start + iters * self.pieces
        self.i = None


def slot_uses(blocks):
    return [len([b for b in range(blocks) if b % SLOTS == s]) for s in range(SLOTS)]


LAYER_PLACES = [SLOTS * (2 - l) + KT + 3 * 4 + 2 * NB + 4 + PAIR_BLOCKS + PAIR_EMPTY for l in range(DEPTH)]
CACHE_PLACES = [sum(LAYER_PLACES[0:l]) + SLOTS * (2 - l) + KT + 3 * 4 for l in range(DEPTH)]
EMPTY_PLACES = [sum(LAYER_PLACES[0:l + 1]) - PAIR_EMPTY for l in range(DEPTH)]
ROUNDS = [1, NE // 2]


def rounds(eng, r, l, expert, st=None, steps=0):
    if ROUNDS[l] == 1:
        for ee in range(2):
            expert(None, ee)
    else:
        r.begin(PAIR_BLOCKS)
        with eng.Fori(0, ROUNDS[l]) as i:
            r.i = i
            if st:
                st.begin(i, steps)
            for ee in range(2):
                expert(i, ee)
        r.end(ROUNDS[l])
        if st:
            st.end(ROUNDS[l])


def program(nc, t):
    with ExitStack() as ctx:
        def sb(name, cols, rows=P, dt=F32):
            return ctx.enter_context(nc.sbuf_tensor(name, [rows, cols], dt))

        def view(name, cols, dt, offset):
            return nc.alloc_sbuf_tensor_at(name, [P, cols], dt, offset=offset)

        def sem(name):
            return ctx.enter_context(nc.semaphore(name))

        base = (nc.sbuf_base + 31) // 32 * 32
        arena = sb("arena", (KT + N_PROJ) * NT + 8)
        hT, hH = view("hT", KT * NT, F32, base), view("hH", KT * NT, F32R, base)
        proj, projR = (view(n_, N_PROJ * NT, dt, base + 4 * KT * NT) for n_, dt in (("proj", F32), ("projR", F32R)))
        hL = sb("hL", KT * NT, dt=F32R)
        wH, wL = sb("wH", BUFS * PIECE, dt=F32R), sb("wL", BUFS * PIECE, dt=F32R)
        ring = sb("ring", SLOTS * BLOCK)
        xT = sb("xT", KT * NT)
        conv = sb("conv", CONV_T * NT)
        tmp = sb("tmp", KT * NT)
        stream = sb("stream", STATE_SLOTS * 1024)
        const = sb("const", N_CONST)
        par = sb("par", DEPTH * N_PAR + KT)
        hpar = sb("hpar", DEPTH * 3)
        wgate = sb("wgate", DEPTH * KT * 76)
        nst = sb("nst", DEPTH * 48)
        cst = sb("cst", DEPTH * CONV_T * 3 * NB)
        m0 = sb("m0", DEPTH * NB, 6)
        alog = sb("alog", DEPTH, 12)
        wrt = sb("wrt", KT * NE)
        rstd = sb("rstd", NT)
        spx = sb("spx", 2 * NT, 12)
        spa, spu, spd, spl = (conv[0:12, 2 * NT * i:2 * NT * (i + 1)] for i in range(4))
        gI, lda = conv[0:6, 8 * NT:9 * NT], conv[0:12, 9 * NT:10 * NT]
        negM, negm = sb("negM", SEQ, 6), sb("negm", SEQ, 6)
        cum_f, run_max, grow, arow = hT[0:6, 600:856], hT[0:6, 860:1116], hT[0:6, 1120:1504], hT[0:12, 1510:1894]
        cum_a = sb("cum_a", SEQ, 12)
        small = sb("small", 40, 12)
        smR = sb("smR", 24, 6)
        gcol = sb("gcol", 54)
        gbc = sb("gbc", 192)
        nnew = sb("nnew", 48)
        rden = sb("rden", 48)
        npr = sb("npr", NH)
        vA = sb("vA", 48)
        xds = sb("xds", 48)
        yT = sb("yT", NB)
        yT2 = sb("yT2", 48)
        cvp = sb("cvp", CONV_T * 3)
        sml = sb("sml", 64)
        ps = ctx.enter_context(nc.psum_tensor("ps", [P, 8 * 512], F32))

        dma_const, dma_small, dma_out = sem("dma_const"), sem("dma_small"), sem("dma_out")
        landed = [sem(f"landed{s}") for s in range(SLOTS)]
        hi_ready, lo_ready = sem("hi_ready"), sem("lo_ready")
        piece_done = sem("piece_done")
        state_in = [sem(f"state_in{s}") for s in range(STATE_SLOTS)]
        state_out = [sem(f"state_out{s}") for s in range(STATE_SLOTS)]
        mem_in = sem("mem_in")
        act_step, dve_step = sem("act_step"), sem("dve_step")
        gate_sum, lin_free = sem("gate_sum"), [sem("lin_free0"), sem("lin_free1")]
        sq_ready, ss_ready, rs_ready, h_full, h_high, h_ready, x_ready = (sem(n) for n in (
            "sq_ready", "ss_ready", "rs_ready", "h_full", "h_high", "h_ready", "x_ready"))
        gate_abs, gate_exp, gate_one, gate_log = (sem(n) for n in ("gate_abs", "gate_exp", "gate_one", "gate_log"))
        gate_rows, gate_cols, gate_cols_in, gate_sexp, gate_bc, gate_bc_in = (sem(n) for n in (
            "gate_rows", "gate_cols", "gate_cols_in", "gate_sexp", "gate_bc", "gate_bc_in"))
        k_scaled, gates_done, conv_acc, conv_done = (sem(n) for n in ("k_scaled", "gates_done", "conv_acc", "conv_done"))
        rot_ready, rot_used, rot_done = sem("rot_ready"), sem("rot_used"), sem("rot_done")
        nq_ready, nden_ready, nden_done = sem("nq_ready"), sem("nden_ready"), sem("nden_done")
        ml_scores, ml_w, ml_weighted, ml_num, ml_h, ml_state = (sem(n) for n in (
            "ml_scores", "ml_w", "ml_weighted", "ml_num", "ml_h", "ml_state"))
        ssd_cb, ssd_dt, ssd_xdt, ssd_L, ssd_w, ssd_S, ssd_y, ssd_h, ssd_state = (sem(n) for n in (
            "ssd_cb", "ssd_dt", "ssd_xdt", "ssd_L", "ssd_w", "ssd_S", "ssd_y", "ssd_h", "ssd_state"))
        ret_scores, ret_vk, ret_weighted, ret_num, ret_h = (sem(n) for n in (
            "ret_scores", "ret_vk", "ret_weighted", "ret_num", "ret_h"))
        dec_bc, dec_S, dec_read, dec_y = (sem(n) for n in ("dec_bc", "dec_S", "dec_read", "dec_y"))
        post_sq, post_ss, post_rs, post_y, post_high, post_low = (sem(n) for n in (
            "post_sq", "post_ss", "post_rs", "post_y", "post_high", "post_low"))
        mem_full, mem_high, mem_low, v_turn, v_turned = (sem(n) for n in ("mem_full", "mem_high", "mem_low", "v_turn", "v_turned"))
        o_high, o_low = sem("o_high"), sem("o_low")
        ca_scores, ca_max, ca_exp, ca_p, ca_pt, ca_ptc, ca_o, ca_oc = (sem(n) for n in (
            "ca_scores", "ca_max", "ca_exp", "ca_p", "ca_pt", "ca_ptc", "ca_o", "ca_oc"))
        cs_zero, cs_q, cs_k, cs_max, cs_exp, cs_p, cs_back, cs_backc, cs_v, cs_o, cs_turn, cs_oc = (sem(n) for n in (
            "cs_zero", "cs_q", "cs_k", "cs_max", "cs_exp", "cs_p", "cs_back", "cs_backc", "cs_v", "cs_o", "cs_turn", "cs_oc"))
        rt_logits, rt_max, rt_exp, rt_comb, rt_turn, rt_combT = (sem(n) for n in (
            "rt_logits", "rt_max", "rt_exp", "rt_comb", "rt_turn", "rt_combT"))
        ex_mask, ex_bc, gu_silu, gu_full, gu_high, gu_low, down_free = (sem(n) for n in (
            "ex_mask", "ex_bc", "gu_silu", "gu_full", "gu_high", "gu_low", "down_free"))
        y_out = sem("y_out")

        def bank(b, lo=0, n=512, rows=P, r0=0):
            return ps[r0:r0 + rows, b * 512 + lo:b * 512 + lo + n]

        def tile(buf, i, lo=0, n=NT, rows=P):
            return buf[0:rows, i * NT + lo:i * NT + lo + n]

        def tiles3(buf, i, n, lo=0, w=NT):
            return buf[:, i * NT:(i + n) * NT].rearrange("p (k t) -> p k t", k=n)[:, :, lo:lo + w]

        def c(at, n=P, rows=P):
            return const[0:rows, at:at + n]

        def pcol(l, at):
            return par[:, l * N_PAR + at:l * N_PAR + at + 1]

        def slot(s, lo=0, n=BLOCK):
            return ring[:, s * BLOCK + lo:s * BLOCK + lo + n]

        def state(u):
            return stream[:, (u % STATE_SLOTS) * 1024:(u % STATE_SLOTS + 1) * 1024]

        def unit_bc(u):
            if u < NH:
                tiles = (proj, K_ML + u), (proj, Q_ML + u)
            elif u < NH + SP:
                g = (u - NH) // 3
                tiles = (conv, B_T + g), (conv, C_T + g)
            else:
                tiles = (proj, K_R + u - NH - SP), (proj, Q_R + u - NH - SP)
            return [tile(buf, i, SEQ, NB) for buf, i in tiles]

        def f32(ap):
            return ap.bitcast(F32)

        def split_high(act, r):
            s, landed_before, half, q, buf = r.next_piece()
            act.wait_ge(landed[s], landed_before * 16 + 16)
            if r.i is not None or q >= BUFS:
                act.wait_ge(piece_done, q + (1 - BUFS))
            act.activation(wH[:, buf * PIECE:(buf + 1) * PIECE], slot(s, half * PIECE, PIECE), ACT.Copy).then_inc(hi_ready, 1)

        def split_low(dve, r):
            s, _, half, q, buf = r.next_piece()
            dve.wait_ge(hi_ready, q + 1)
            dve.tensor_tensor(wL[:, buf * PIECE:(buf + 1) * PIECE], slot(s, half * PIECE, PIECE),
                              f32(wH[:, buf * PIECE:(buf + 1) * PIECE]), ALU.subtract).then_inc(lo_ready, 1)

        ident, ones = c(C_ID), c(C_ONES)
        mW, mS, mVK, mKW, mEM, mDN = (hT[:, a:b] for a, b in (
            (0, 384), (384, 768), (768, 1280), (1280, 1536), (1536, 1792), (1792, 2048)))
        sXD, sXT, sS, sXW, sY, sBT = (hT[:, a:b] for a, b in (
            (0, 264), (264, 520), (520, 1288), (1288, 1544), (1544, 1800), (1800, 2056)))
        sL = tmp[:, 0:768]
        dP = tmp[:, 1024:1536]
        caP, caPT = conv[:, 0:512], conv[:, 1024:1536]
        csQ, csPM, csP, csO = tmp[:, 0:2 * 1024], conv[:, 1800:2312], conv[0:32, 1536:1792], tmp[0:NB, 0:D_MODEL]
        combT, combM, combB = conv[0:8, 1024:1024 + NT], conv[0:8, 1300:1300 + NT], conv[:, 1600:1600 + NT]
        sig, full = [tile(tmp, i) for i in range(2)], [tile(tmp, 2 + i) for i in range(2)]
        lg = conv[:, 0:24]

        lin_of, piece_of, n, q = {}, {}, 0, 0
        for name, k, pieces in (("in", 56, 1), ("gates", 1, 0), ("out", KT, 2), ("memk", KT, 1), ("memv", KT, 1), ("q", KT, 1), ("o", KT, 1)):
            lin_of[name], piece_of[name] = n, q
            n, q = n + k, q + k * pieces
        LIN, piece_of["ffn"] = n, q
        LAYER_PIECE = [0, q + ROUNDS[0] * PAIR_PIECES]
        NORMS = 4
        block = ctx.enter_context(nc.Block())

        @block.sync
        def _(sp):
            r = Ring()
            free = [None] * SLOTS

            def load(src, n=BLOCK, by=None, wrap=0):
                q = r.piece
                s, _ = r.block()
                if r.i is None:
                    if free[s]:
                        sp.wait_ge(*free[s])
                    value = q + 2
                else:
                    sp.wait_ge(lo_ready, r.i * r.pieces + max(free[s][1], wrap))
                    value = q + 2
                free[s] = by or (lo_ready, value)
                if by is None:
                    r.piece += 2
                sp.dma_start(slot(s, 0, n), src).then_inc(landed[s], 16)

            for dst, name in ((const, "const"), (xT, "x"), (par, "par"), (wgate, "wgate")):
                sp.dma_start(dst[:, :], t[name]).then_inc(dma_const, 16)
            for dst, name in ((hpar, "hpar"), (nst, "nst"), (cst, "cst"), (m0, "m0"), (alog, "alog"), (wrt, "wrt")):
                sp.dma_start(dst[:, :], t[name]).then_inc(dma_small, 16)

            def expert(e, first):
                gu, down = (t[k].rearrange("e b p n -> p (e b) n") for k in ("w_gu", "w_down"))
                for j in range(GU_BLOCKS):
                    load(gu[:, bass.ds(e * GU_BLOCKS + j, 1), :], wrap=wraps[j] if first and j < SLOTS else 0)
                for j in range(DOWN_BLOCKS):
                    load(down[:, bass.ds(e * DOWN_BLOCKS + j, 1), :], F_TILES * P)

            for l in range(DEPTH):
                w_in = t["w_in"][l].rearrange("b p n -> p b n")
                if l == 0:
                    for j in range(SLOTS):
                        load(t["w_in"][l, j])
                peel = 1 - l
                r.begin(SLOTS)
                with sp.Fori(peel, IN_ITERS) as i:
                    r.i = i - peel if peel else i
                    for j in range(SLOTS):
                        load(w_in[:, bass.ds(i * SLOTS + j, 1), :], wrap=r.start - 2 * SLOTS + 2 * j + 2)
                r.end(IN_ITERS - peel)
                free = [(lo_ready, r.piece - 2 * SLOTS + 2 * j + 2) for j in range(SLOTS)]
                for j in range(KT):
                    load(t["w_out"][l, j])
                for name in ("w_k", "w_v", "w_q"):
                    for j in range(4):
                        load(t[name][l, j])
                for b in range(NB):
                    load(t["kc"][l, b], by=(cs_k, l * NB + b + 1))
                for b in range(NB):
                    load(t["vc"][l, b], by=(cs_v, l * NB + b + 1))
                for j in range(4):
                    load(t["w_o"][l, j])
                first_piece = r.piece
                wraps = []
                for j in range(SLOTS):
                    place = j + PAIR_BLOCKS + PAIR_EMPTY - SLOTS
                    while place >= PAIR_BLOCKS:
                        place -= SLOTS
                    wraps.append(first_piece + 2 * (place - PAIR_BLOCKS) + 2)
                if l == 0:
                    for e in range(2):
                        expert(e, e == 0)
                else:
                    r.begin(PAIR_BLOCKS)
                    with sp.Fori(0, ROUNDS[l]) as i:
                        r.i = i
                        for e in range(2):
                            expert(i * 2 + (2 + e), e == 0)
                    shift = (ROUNDS[l] - 1) * PAIR_PIECES
                    free = [(lo_ready, f[1] + shift) for f in free]
                    r.end(ROUNDS[l])
            for j in range(2):
                load(t["w_in"][0, j])
            sp.wait_ge(h_full, (3 * DEPTH + 1) * KT)
            sp.dma_start(t["y"], tmp[:, :]).then_inc(y_out, 16)
            sp.wait_ge(y_out, 16)
            sp.wait_ge(dma_out, 16 * DEPTH * OUTS)
            for s in range(STATE_SLOTS):
                sp.wait_ge(state_out[s], 16 * DEPTH * len([u for u in range(UNITS) if u % STATE_SLOTS == s]))
            for s in range(SLOTS):
                sp.wait_ge(landed[s], 16 * r.used[s])

        @block.tensor
        def _(pe):
            r = Ring()

            def lin_bank(n):
                if n >= 2:
                    pe.wait_ge(lin_free[n % 2], n // 2)
                return n % 2

            def norm_sum(k, src, w=NT, s0=0):
                pe.wait_ge(sq_ready, k + 1)
                for j in range(KT):
                    ins = pe.matmul(bank(6, 0, w), ones, tile(src, s0 + j, 0, w), start=j == 0, stop=j == KT - 1)
                ins.then_inc(ss_ready, 1)

            def product(dst, high, low, kts=KT, k0=0, k_all=KT):
                _, _, _, q, buf = r.next_piece()
                pe.wait_ge(lo_ready, q + 1)
                for k in range(kts):
                    wh, wl = (w[:, buf * PIECE + k * P:buf * PIECE + (k + 1) * P] for w in (wH, wL))
                    pe.matmul(dst, wh, high(k0 + k), start=k0 + k == 0, stop=False)
                    pe.matmul(dst, wh, low(k0 + k), start=False, stop=False)
                    ins = pe.matmul(dst, wl, high(k0 + k), start=False, stop=k0 + k == k_all - 1)
                ins.then_inc(piece_done, 1)

            def tiles_out(name, l, n_tiles, high, low, w=NT, halves=1):
                for j in range(n_tiles):
                    b = lin_bank(l * LIN + lin_of[name] + j)
                    for half in range(halves):
                        product(bank(b, 0, w), high, low, k0=half * KT, k_all=halves * KT)

            def causal(dst, h, rows, row):
                sel = ident[0:rows, h:h + 1].to_broadcast([rows, P])
                pe.matmul(dst[:, 0:SEQ], sel, row[:, 0:SEQ], start=True, stop=False, skip_group_check=True)
                pe.matmul(dst[:, 0:P], ident, c(C_MASK), start=False, stop=True, skip_group_check=True)
                pe.matmul(dst[:, SEQ:384], sel, row[:, P:SEQ], start=True, stop=False, skip_group_check=True)
                return pe.matmul(dst[:, SEQ:384], ident, c(C_MASK), start=False, stop=True, skip_group_check=True)

            def blocks3(dst, lhs, rhs):
                pe.matmul(dst[:, 0:P], lhs(0), rhs[:, 0:P], start=True, stop=True, skip_group_check=True)
                pe.matmul(dst[:, P:SEQ], lhs(0), rhs[:, P:SEQ], start=True, stop=False, skip_group_check=True)
                return pe.matmul(dst[:, P:SEQ], lhs(1), rhs[:, SEQ:384], start=False, stop=True, skip_group_check=True)

            pe.wait_ge(dma_const, 64)
            for l in range(DEPTH):
                L0 = l * LIN
                norm_sum(l * NORMS, hT)
                pe.wait_ge(h_ready, (3 * l + 1) * KT)

                def h_high_part(k):
                    return tile(hH, k)

                def h_low_part(k):
                    return tile(hL, k)

                n0 = L0 + lin_of["in"]
                peel = 1 - l
                per = 2 * SLOTS
                if peel:
                    tiles_out("in", l, per, h_high_part, h_low_part)
                r.begin(SLOTS)
                with pe.Fori(peel, IN_ITERS) as i:
                    r.i = i - peel if peel else i
                    for j in range(per):
                        n = n0 + j
                        pe.wait_ge(lin_free[n % 2], i * (per // 2) + n // 2)
                        product(bank(n % 2, 0, NT), h_high_part, h_low_part)
                r.end(IN_ITERS - peel)
                b = lin_bank(L0 + lin_of["gates"])
                for k in range(KT):
                    for part in (hH, hL):
                        ins = pe.matmul(bank(b, 0, NT, 76), wgate[:, (l * KT + k) * 76:(l * KT + k + 1) * 76], f32(tile(part, k)),
                                        start=k == 0 and part is hH, stop=k == KT - 1 and part is hL)
                ins.then_inc(gate_sum, 1)
                pe.wait_ge(k_scaled, l + 1)
                for j in range(2 * RH):
                    n = l * 2 * RH + j
                    if j >= 2:
                        pe.wait_ge(rot_used, n - 1)
                    pe.matmul(bank(4 + n % 2, 0, NT), c(C_ROT), tile(proj, Q_R + j), start=True, stop=True).then_inc(rot_ready, 1)
                pe.wait_ge(gate_rows, l + 1)
                for j in range(3):
                    pe.transpose(bank(2, 6 * j, 6), grow[:, j * P:(j + 1) * P], ident[0:6, 0:6])
                for j in range(3):
                    ins = pe.transpose(bank(2, 18 + 12 * j, 12), arow[:, j * P:(j + 1) * P], ident[0:12, 0:12])
                ins.then_inc(gate_cols, 1)
                pe.wait_ge(gate_sexp, l + 1)
                for h in range(NH):
                    pe.matmul(bank(3, 24 * h, 24), ident[0:6, h:h + 1].to_broadcast([6, P]), smR[:, :], start=True, stop=True)
                for j in range(SP):
                    ins = pe.matmul(bank(3, 144 + 8 * j, 8), const[0:12, C_SEL2 + j * P:C_SEL2 + (j + 1) * P], small[:, 8:16],
                                    start=True, stop=True)
                ins.then_inc(gate_bc, 1)
                pe.wait_ge(nq_ready, l + 1)
                pe.matmul(bank(6, 0, 48), ones, yT2[:, :], start=True, stop=True).then_inc(nden_ready, 1)
                for n in (L0 + lin_of["gates"] - 1, L0 + lin_of["gates"]):
                    pe.wait_ge(lin_free[n % 2], n // 2 + 1)

                def spread(u, half):
                    n = 2 * (l * UNITS + u) + half
                    if n > 2 * l * UNITS:
                        pe.wait_ge(dec_read, n)
                    for bk, col in enumerate(unit_bc(u)):
                        for b in range(NB // 2):
                            at = half * (NB // 2) + b
                            ins = pe.matmul(bank(bk, b * P, P), col[:, at:at + 1].to_broadcast([P, P]), ident, start=True, stop=True)
                    ins.then_inc(dec_bc, 1)

                pe.wait_ge(k_scaled, l + 1)
                pe.wait_ge(gate_cols_in, l + 1)
                pe.wait_ge(gate_bc_in, l + 1)
                pe.wait_ge(rot_used, (l + 1) * 2 * RH)
                pe.wait_ge(nden_done, l + 1)

                def turn_vk(b, v, k):
                    for st in range(2):
                        pe.transpose(bank(b, st * P, P), tile(proj, v, st * P, P), ident)
                    for st in range(2):
                        ins = pe.transpose(bank(b, SEQ + st * P, P), tile(proj, k, st * P, P), ident)
                    return ins

                def scores(b, k, q):
                    pe.matmul(bank(b, 0, SEQ), tile(proj, k, 0, P), tile(proj, q, 0, SEQ), start=True, stop=True)
                    return pe.matmul(bank(b, SEQ, P), tile(proj, k, P, P), tile(proj, q, P, P), start=True, stop=True)

                def ml_a(h):
                    n = l * NH + h
                    if h:
                        pe.wait_ge(ml_weighted, n)
                        pe.wait_ge(ml_w, n)
                    scores(2, K_ML + h, Q_ML + h)
                    causal(bank(3, 0, 384), h, 6, negM)
                    pe.matmul(bank(4, 0, SEQ), ident[0:6, h:h + 1].to_broadcast([6, P]), negm[:, :], start=True, stop=True)
                    turn_vk(5, V_ML + h, K_ML + h).then_inc(ml_scores, 1)

                def ml_d(h):
                    n = l * NH + h
                    pe.wait_ge(ml_weighted, n + 1)
                    if h:
                        pe.wait_ge(ml_h, n)
                        pe.wait_ge(ml_state, n)
                    blocks3(bank(6, 0, SEQ), lambda st: mVK[:, st * P:(st + 1) * P], mS)
                    blocks3(bank(6, SEQ, SEQ), lambda st: ones, mS)
                    for st in range(2):
                        pe.matmul(bank(7, 0, P), mVK[:, st * P:(st + 1) * P], mKW[:, st * P:(st + 1) * P], start=st == 0, stop=st == 1)
                    for st in range(2):
                        ins = pe.matmul(bank(7, P, 1), mKW[:, st * P:(st + 1) * P], ones[:, 0:1], start=st == 0, stop=st == 1)
                    ins.then_inc(ml_num, 1)

                for h in range(NH):
                    ml_a(h)
                    spread(h, 0)
                    ml_d(h)
                    spread(h, 1)
                pe.wait_ge(ml_h, (l + 1) * NH)
                pe.wait_ge(ml_state, (l + 1) * NH)
                pe.wait_ge(conv_done, l + 1)
                for j in range(SP):
                    n, g = l * SP + j, j // 3
                    if j:
                        pe.wait_ge(ssd_h, n)
                        pe.wait_ge(ssd_state, n)
                    if j % 3 == 0:
                        bT, cT = tile(conv, B_T + g), tile(conv, C_T + g)
                        pe.matmul(bank(2, 0, SEQ), bT[:, 0:P], cT[:, 0:SEQ], start=True, stop=True)
                        pe.matmul(bank(2, SEQ, P), bT[:, P:SEQ], cT[:, P:SEQ], start=True, stop=True)
                        for st in range(2):
                            ins = pe.transpose(bank(3, st * P, P), bT[:, st * P:(st + 1) * P], ident)
                        ins.then_inc(ssd_cb, 1)
                    pe.matmul(bank(4, 0, NT), const[0:12, C_SEL2 + j * P:C_SEL2 + (j + 1) * P], spx[:, NT:2 * NT],
                              start=True, stop=True).then_inc(ssd_dt, 1)
                    for hh in range(2):
                        causal(bank(6 + hh, 0, 384), 2 * j + hh, 12, cum_a)
                    pe.wait_ge(ssd_xdt, n + 1)
                    for st in range(2):
                        ins = pe.transpose(bank(5, st * P, P), sXD[:, st * P:(st + 1) * P], ident)
                    ins.then_inc(ssd_L, 1)
                    spread(NH + j, 0)
                    pe.wait_ge(ssd_S, n + 1)
                    for hh in range(2):
                        dst = ps[64 * hh:64 * hh + 64, 4 * 512:4 * 512 + SEQ]
                        blocks3(dst, lambda st: sXT[:, st * P + 64 * hh:st * P + 64 * hh + 64], sS[:, hh * 384:(hh + 1) * 384])
                    for st in range(2):
                        ins = pe.matmul(bank(5, SEQ, P), sXW[:, st * P:(st + 1) * P], sBT[:, st * P:(st + 1) * P], start=st == 0, stop=st == 1)
                    ins.then_inc(ssd_y, 1)
                    spread(NH + j, 1)
                pe.wait_ge(ssd_h, (l + 1) * SP)
                pe.wait_ge(ssd_state, (l + 1) * SP)
                pe.wait_ge(rot_done, l + 1)
                for h in range(RH):
                    n = l * RH + h
                    if h:
                        pe.wait_ge(ret_h, n)
                    scores(2, K_R + h, Q_R + h)
                    turn_vk(5, V_R + h, K_R + h).then_inc(ret_scores, 1)
                    spread(NH + SP + h, 0)
                    pe.wait_ge(ret_weighted, n + 1)
                    pe.wait_ge(ret_vk, n + 1)
                    blocks3(bank(6, 0, SEQ), lambda st: mVK[:, st * P:(st + 1) * P], mS)
                    for st in range(2):
                        ins = pe.matmul(bank(7, 0, P), mKW[:, st * P:(st + 1) * P], mVK[:, st * P:(st + 1) * P], start=st == 0, stop=st == 1)
                    ins.then_inc(ret_num, 1)
                    spread(NH + SP + h, 1)
                pe.wait_ge(ret_h, (l + 1) * RH)
                pe.wait_ge(dec_y, (l + 1) * UNITS)
                for k, (n_banks, per) in enumerate(((NH, 1), (2, 3), (RH, 1))):
                    pe.wait_ge(post_sq, 3 * l + k + 1)
                    for g in range(n_banks):
                        for j in range(per):
                            ins = pe.matmul(bank(2 + g, 0, NT), ones, tile(hT, g * per + j), start=j == 0, stop=j == per - 1)
                    ins.then_inc(post_ss, 1)
                pe.wait_ge(post_low, 3 * (l + 1))
                lows = [Q_ML + h for h in range(NH)] + [Z + j for j in range(SP)] + [Q_R + h for h in range(RH)]
                highs = [Y_HI[0] + h for h in range(NH)] + [Y_HI[1] + j for j in range(SP)] + [Y_HI[2] + h for h in range(RH)]
                tiles_out("out", l, KT, lambda k: tile(projR, highs[k]), lambda k: tile(projR, lows[k]), halves=2)
                norm_sum(l * NORMS + 1, proj, MEM, CA_MEMN)
                pe.wait_ge(mem_low, l + 1)
                for name in ("memk", "memv"):
                    tiles_out(name, l, KT, lambda k: tile(projR, CA_MEMH + k, 0, MEM), lambda k: tile(projR, CA_MEMN + k, 0, MEM), MEM)
                for n in (L0 + lin_of["memv"] + 6, L0 + lin_of["memv"] + 7):
                    pe.wait_ge(lin_free[n % 2], n // 2 + 1)
                for mt in range(2):
                    for k in range(KT):
                        ins = pe.transpose(bank(2 + 2 * mt + k // 4, k % 4 * P, P), tile(proj, CA_VT + k, mt * P, P), ident)
                ins.then_inc(v_turn, 1)
                norm_sum(l * NORMS + 2, hT)
                pe.wait_ge(h_ready, (3 * l + 2) * KT)
                tiles_out("q", l, KT, h_high_part, h_low_part)
                for n in (L0 + lin_of["q"] + 6, L0 + lin_of["q"] + 7):
                    pe.wait_ge(lin_free[n % 2], n // 2 + 1)
                pe.wait_ge(v_turned, l + 1)
                for h in range(CAH):
                    n = l * CAH + h
                    if h:
                        pe.wait_ge(ca_oc, n)
                    for qt in range(2):
                        for kk in range(2):
                            ins = pe.matmul(bank(2, qt * MEM, MEM), tile(proj, CA_Q + 2 * h + kk, qt * P, P),
                                            tile(proj, CA_K + 2 * h + kk, 0, MEM), start=kk == 0, stop=kk == 1)
                    ins.then_inc(ca_scores, 1)
                    pe.wait_ge(ca_p, n + 1)
                    for mt in range(2):
                        for qt in range(2):
                            ins = pe.transpose(bank(3, mt * SEQ + qt * P, P), caP[:, qt * MEM + mt * P:qt * MEM + (mt + 1) * P], ident)
                    ins.then_inc(ca_pt, 1)
                    pe.wait_ge(ca_ptc, n + 1)
                    for dt in range(2):
                        for mt in range(2):
                            v0 = CA_V * NT + mt * D_MODEL + (2 * h + dt) * P
                            ins = pe.matmul(bank(4, dt * SEQ, SEQ), proj[:, v0:v0 + P], caPT[:, mt * SEQ:(mt + 1) * SEQ],
                                            start=mt == 0, stop=mt == 1)
                    ins.then_inc(ca_o, 1)
                pe.wait_ge(cs_q, l + 1)
                for b in range(NB):
                    s, before = r.block()
                    pe.wait_ge(landed[s], 16 * before + 16)
                    kc = slot(s)
                    for h in range(CAH):
                        for kk in range(2):
                            q0 = kk * 1024 + (h * NB + b) * CAH * NB
                            ins = pe.matmul(bank(5, 0, MEM, CAH * NB), csQ[:, q0:q0 + CAH * NB], kc[:, (2 * h + kk) * MEM:(2 * h + kk + 1) * MEM],
                                            start=(b, h, kk) == (0, 0, 0), stop=(b, h, kk) == (NB - 1, CAH - 1, 1))
                    ins.then_inc(cs_k, 1)
                pe.wait_ge(cs_p, l + 1)
                for mt in range(2):
                    ins = pe.transpose(bank(7, mt * 32, 32), csP[:, mt * P:(mt + 1) * P], ident[0:32, 0:32])
                ins.then_inc(cs_back, 1)
                pe.wait_ge(cs_backc, l + 1)
                pe.wait_ge(ca_oc, (l + 1) * CAH)
                for b in range(NB):
                    s, before = r.block()
                    pe.wait_ge(landed[s], 16 * before + 16)
                    vc = slot(s)
                    for h in range(CAH):
                        for mt in range(2):
                            p0 = ((mt * CAH + h) * NB + b) * NB
                            ins = pe.matmul(bank(2 + h, 0, 2 * P, NB), csPM[:, p0:p0 + NB], vc[:, mt * D_MODEL + 2 * h * P:mt * D_MODEL + (2 * h + 2) * P],
                                            start=(b, mt) == (0, 0), stop=(b, mt) == (NB - 1, 1))
                    ins.then_inc(cs_v, 1)
                pe.wait_ge(cs_o, l + 1)
                for d in range(KT):
                    ins = pe.transpose(bank(7, 64 + d * NB, NB), csO[:, d * P:(d + 1) * P], ident[0:NB, 0:NB])
                ins.then_inc(cs_turn, 1)
                pe.wait_ge(o_low, l + 1)
                tiles_out("o", l, KT, lambda k: tile(projR, CA_OH + k), lambda k: tile(projR, CA_O + k))
                norm_sum(l * NORMS + 3, hT)
                pe.wait_ge(h_ready, (3 * l + 3) * KT)
                moe = l % 2 == 1
                if moe:
                    for tt, (lo, w) in enumerate(((0, P), (P, P), (SEQ, NB))):
                        for k in range(KT):
                            for part in (hH, hL):
                                ins = pe.matmul(bank(7, tt * NE, NE, w), f32(tile(part, k, lo, w)), wrt[:, k * NE:(k + 1) * NE],
                                                start=k == 0 and part is hH, stop=k == KT - 1 and part is hL)
                    ins.then_inc(rt_logits, 1)
                    pe.wait_ge(rt_comb, 1)
                    for tt, (lo, w) in enumerate(((0, P), (P, P), (SEQ, NB))):
                        ins = pe.transpose(bank(7, 64 + lo, w, NE), lg[0:w, tt * NE:(tt + 1) * NE], ident[0:w, 0:w])
                    ins.then_inc(rt_turn, 1)
                    pe.wait_ge(rt_combT, 1)
                for n in (L0 + LIN - 2, L0 + LIN - 1):
                    pe.wait_ge(lin_free[n % 2], n // 2 + 1)

                def expert(i, ee):
                    def at(per, n):
                        return n if i is None else i * (2 * per) + n
                    gu0, dn0 = l * 2 * F_TILES + ee * F_TILES, l * 2 * KT + ee * KT
                    for f in range(F_TILES):
                        if f >= 2:
                            pe.wait_ge(gu_full, at(F_TILES, gu0 + f - 1))
                        for g in range(2):
                            product(bank(2 * g + f % 2, 0, NT), h_high_part, h_low_part)
                        if moe and f == 0:
                            pe.wait_ge(ex_mask, at(1, ee + 1))
                            pe.matmul(bank(6, 0, NT), ones[0:NE, :], combM, start=True, stop=True).then_inc(ex_bc, 1)
                    for j in range(KT):
                        if j >= 2:
                            pe.wait_ge(down_free, at(KT, dn0 + j - 1))
                        dst = bank(4 + j % 2, 0, NT)
                        if j == 0:
                            pe.wait_ge(gu_low, at(F_TILES, gu0 + F_TILES))
                        product(dst, lambda k: tile(projR, FF_H + k), lambda k: tile(projR, FF_L + k), k_all=F_TILES)
                        product(dst, lambda k: tile(projR, FF_H + k), lambda k: tile(projR, FF_L + k), F_TILES - KT, KT, F_TILES)

                rounds(pe, r, l, expert)
            norm_sum(DEPTH * NORMS, hT)

        @block.scalar
        def _(act):
            act.preload_act_table_set("natural_log_exp_and_others")
            st = Steps(act, act_step)
            act.wait_ge(dma_const, 64)
            act.wait_ge(dma_small, 96)
            eps = c(C_EPS, 1)

            r = Ring()

            def norm(k, src, sq, w=NT, s0=0, q0=0):
                act.activation(tiles3(sq, q0, KT, 0, w), tiles3(src, s0, KT, 0, w), ACT.Square).then_inc(sq_ready, 1)
                act.wait_ge(ss_ready, k + 1)
                st(act.activation(rstd[:, 0:w], bank(6, 0, w), ACT.Ln, bias=eps, scale=1.0 / D_MODEL))
                act.activation(rstd[:, 0:w], rstd[:, 0:w], ACT.Exp, scale=-0.5).then_inc(rs_ready, 1)

            def high(k):
                for j in range(KT):
                    act.wait_ge(h_full, k * KT + j + 1)
                    act.activation(tile(hH, j), tile(tmp, j), ACT.Copy).then_inc(h_high, 1)

            def take(n, q, dst, src, ahead=True):
                if ahead:
                    split_high(act, r)
                act.wait_ge(piece_done, q + 1)
                act.activation(dst, src, ACT.Copy).then_inc(lin_free[n % 2], 1)

            for _ in range(AHEAD):
                split_high(act, r)

            for l in range(DEPTH):
                L0 = l * LIN
                Q0 = LAYER_PIECE[l]
                if l:
                    act.wait_ge(x_ready, 3 * l)
                norm(l * NORMS, xT, hT)
                high(3 * l)
                peel = 1 - l
                for j in range(2 * SLOTS * peel):
                    take(L0 + j, Q0 + j, tile(proj, j), bank((L0 + j) % 2, 0, NT))
                r.begin(SLOTS)
                with act.Fori(peel, IN_ITERS) as i:
                    r.i = i - peel if peel else i
                    for j in range(2 * SLOTS):
                        n = L0 + j
                        split_high(act, r)
                        act.wait_ge(piece_done, i * (2 * SLOTS) + (Q0 + j + 1))
                        act.activation(proj[:, bass.ds(i * (2 * SLOTS * NT) + j * NT, NT)], bank(n % 2, 0, NT), ACT.Copy).then_inc(lin_free[n % 2], 1)
                r.end(IN_ITERS - peel)
                act.wait_ge(lin_free[(L0 + 55) % 2], (L0 + 55) // 2 + 1)
                act.wait_ge(lin_free[(L0 + 54) % 2], (L0 + 54) // 2 + 1)
                act.activation(proj[:, K_ML * NT:V_ML * NT], proj[:, K_ML * NT:V_ML * NT], ACT.Copy, scale=P ** -0.5)
                act.activation(proj[:, K_R * NT:V_R * NT], proj[:, K_R * NT:V_R * NT], ACT.Copy, scale=P ** -0.5).then_inc(k_scaled, 1)
                act.wait_ge(gate_abs, l + 1)
                act.activation(spu[:, :], spa[:, :], ACT.Exp, scale=-1.0).then_inc(gate_exp, 1)
                act.activation(small[:, 0:1], alog[:, l:l + 1], ACT.Exp)
                act.wait_ge(gate_one, l + 1)
                act.activation(spl[:, :], spa[:, :], ACT.Ln).then_inc(gate_log, 1)
                act.wait_ge(gate_rows, l + 1)
                act.activation(smR[:, :], smR[:, :], ACT.Exp)
                act.activation(small[:, 8:16], lda[:, SEQ:NT], ACT.Exp).then_inc(gate_sexp, 1)
                act.activation(proj[:, O_ML * NT:Z * NT], proj[:, O_ML * NT:Z * NT], ACT.Sigmoid)
                act.activation(proj[:, Z * NT:XBC * NT], proj[:, Z * NT:XBC * NT], ACT.Silu)
                act.activation(proj[:, G_R * NT:N_PROJ * NT], proj[:, G_R * NT:N_PROJ * NT], ACT.Silu).then_inc(gates_done, 1)
                act.wait_ge(conv_acc, l + 1)
                act.activation(conv[:, :], conv[:, :], ACT.Silu).then_inc(conv_done, 1)
                act.wait_ge(gate_cols_in, l + 1)
                for h in range(NH):
                    n = l * NH + h
                    act.wait_ge(ml_scores, n + 1)
                    if h:
                        act.wait_ge(ml_h, n)
                    for q, (lo, hi) in enumerate(((0, P), (P, SEQ), (SEQ, 384))):
                        act.activation(mW[:, lo:hi], bank(3, lo, hi - lo), ACT.Exp, bias=gcol[:, 6 * q + h:6 * q + h + 1])
                    act.activation(mEM, bank(4, 0, SEQ), ACT.Exp)
                    act.activation(mVK, bank(5), ACT.Copy).then_inc(ml_w, 1)
                    act.wait_ge(ml_num, n + 1)
                    act.activation(tile(proj, K_ML + h, 0, P), bank(7, 0, P), ACT.Copy)
                    act.activation(npr[:, h:h + 1], bank(7, P, 1), ACT.Copy).then_inc(ml_state, 1)
                for j in range(SP):
                    n = l * SP + j
                    if j % 3 == 0:
                        act.wait_ge(ssd_cb, 2 * l + j // 3 + 1)
                        act.activation(sBT, bank(3, 0, SEQ), ACT.Copy)
                    act.wait_ge(ssd_L, n + 1)
                    act.activation(sXT, bank(5, 0, SEQ), ACT.Copy)
                    for hh in range(2):
                        for q, (lo, hi) in enumerate(((0, P), (P, SEQ), (SEQ, 384))):
                            col = 18 + 12 * q + 2 * j + hh
                            ins = act.activation(sL[:, hh * 384 + lo:hh * 384 + hi], bank(6 + hh, lo, hi - lo), ACT.Exp, bias=gcol[:, col:col + 1])
                    ins.then_inc(ssd_w, 1)
                    act.wait_ge(ssd_y, n + 1)
                    act.activation(tile(proj, V_ML + j, 0, P), bank(5, SEQ, P), ACT.Copy).then_inc(ssd_state, 1)
                for h in range(RH):
                    n = l * RH + h
                    act.wait_ge(ret_scores, n + 1)
                    act.activation(mVK, bank(5), ACT.Copy).then_inc(ret_vk, 1)
                    act.wait_ge(ret_num, n + 1)
                    act.activation(tile(proj, Q_R + h, 0, SEQ), bank(6, 0, SEQ), ACT.Copy)
                    act.activation(tile(proj, K_R + h, 0, P), bank(7, 0, P), ACT.Copy).then_inc(ret_h, 1)
                act.wait_ge(dec_y, (l + 1) * UNITS)
                for k, (y0, nt, n_banks, width) in enumerate(((Q_ML, NH, NH, P), (Z, SP, 2, 3 * P), (Q_R, RH, RH, P))):
                    if k:
                        act.wait_ge(post_y, 3 * l + k)
                    act.activation(hT[:, 0:nt * NT], proj[:, y0 * NT:(y0 + nt) * NT], ACT.Square).then_inc(post_sq, 1)
                    act.wait_ge(post_ss, 3 * l + k + 1)
                    for g in range(n_banks):
                        ins = act.activation(tile(tmp, g), bank(2 + g, 0, NT), ACT.Ln, bias=eps, scale=1.0 / width)
                    st(ins)
                    act.activation(tmp[:, 0:n_banks * NT], tmp[:, 0:n_banks * NT], ACT.Exp, scale=-0.5).then_inc(post_rs, 1)
                    if k == 0:
                        act.wait_ge(dma_out, 16 * (OUTS * l + OUTS - 2))
                    act.wait_ge(post_y, 3 * l + k + 1)
                    act.activation(projR[:, Y_HI[k] * NT:(Y_HI[k] + nt) * NT], proj[:, y0 * NT:(y0 + nt) * NT], ACT.Copy).then_inc(post_high, 1)
                for j in range(2 * KT):
                    split_high(act, r)
                act.wait_ge(mem_in, 16 * (l + 1))
                norm(l * NORMS + 1, proj, proj, MEM, CA_MEM, CA_MEMN)
                act.wait_ge(mem_full, l + 1)
                act.activation(tiles3(projR, CA_MEMH, KT, 0, MEM), tiles3(proj, CA_MEMN, KT, 0, MEM), ACT.Copy).then_inc(mem_high, 1)
                for name, at in (("memk", CA_K), ("memv", CA_VT)):
                    for j in range(KT):
                        n = L0 + lin_of[name] + j
                        take(n, Q0 + piece_of[name] + j, tile(proj, at + j, 0, MEM), bank(n % 2, 0, MEM))
                act.wait_ge(v_turn, l + 1)
                for mt in range(2):
                    v0 = CA_V * NT + mt * D_MODEL
                    ins = act.activation(proj[:, v0:v0 + D_MODEL], ps[:, (2 + 2 * mt) * 512:(4 + 2 * mt) * 512], ACT.Copy)
                ins.then_inc(v_turned, 1)
                act.wait_ge(x_ready, 3 * l + 1)
                norm(l * NORMS + 2, xT, hT)
                high(3 * l + 1)
                for j in range(KT):
                    n = L0 + lin_of["q"] + j
                    take(n, Q0 + piece_of["q"] + j, tile(proj, CA_Q + j), bank(n % 2, 0, NT), j < KT - AHEAD)
                for h in range(CAH):
                    n = l * CAH + h
                    act.wait_ge(ca_max, n + 1)
                    for qt in range(2):
                        ins = act.activation(caP[:, qt * MEM:(qt + 1) * MEM], bank(2, qt * MEM, MEM), ACT.Exp, bias=sml[:, qt:qt + 1],
                                             scale=1.0 / 16, accum_out=sml[:, 2 + qt:3 + qt])
                    ins.then_inc(ca_exp, 1)
                    act.wait_ge(ca_pt, n + 1)
                    act.activation(caPT, bank(3), ACT.Copy).then_inc(ca_ptc, 1)
                    act.wait_ge(ca_o, n + 1)
                    act.activation(tiles3(proj, CA_O + 2 * h, 2, 0, SEQ), bank(4).rearrange("p (a t) -> p a t", a=2), ACT.Copy).then_inc(ca_oc, 1)
                act.wait_ge(cs_max, l + 1)
                act.activation(csP, bank(5, 0, MEM, 32), ACT.Exp, bias=sml[0:32, 8:9], scale=1.0 / 16, accum_out=sml[0:32, 9:10]).then_inc(cs_exp, 1)
                act.wait_ge(cs_back, l + 1)
                act.wait_ge(cs_zero, 2 * (l + 1))
                act.activation(csPM.rearrange("p (a c) -> p a c", a=2 * CAH)[:, :, 0:NB * NB:NB + 1],
                               bank(7, 0, 64).rearrange("p (a b) -> p a b", a=2 * CAH), ACT.Copy).then_inc(cs_backc, 1)
                for _ in range(AHEAD):
                    split_high(act, r)
                act.wait_ge(cs_v, (l + 1) * NB)
                act.activation(csO.rearrange("p (h d) -> p h d", h=CAH), bank(2, 0, CAH * 512, NB).rearrange("p (h d) -> p h d", h=CAH)[:, :, 0:2 * P],
                               ACT.Copy).then_inc(cs_o, 1)
                act.wait_ge(cs_turn, l + 1)
                act.activation(tiles3(proj, CA_O, KT, SEQ, NB), bank(7, 64, 64).rearrange("p (a t) -> p a t", a=KT), ACT.Copy).then_inc(cs_oc, 1)
                act.wait_ge(cs_oc, l + 1)
                act.wait_ge(ca_oc, (l + 1) * CAH)
                act.activation(projR[:, CA_OH * NT:(CA_OH + KT) * NT], proj[:, CA_O * NT:(CA_O + KT) * NT], ACT.Copy).then_inc(o_high, 1)
                for j in range(KT):
                    split_high(act, r)
                act.wait_ge(x_ready, 3 * l + 2)
                norm(l * NORMS + 3, xT, hT)
                high(3 * l + 2)
                if l % 2 == 1:
                    act.wait_ge(rt_max, 1)
                    act.activation(conv[:, 24:48], conv[:, 24:48], ACT.Exp).then_inc(rt_exp, 1)
                act.wait_ge(dma_out, 16 * OUTS * (l + 1))

                def expert(i, ee):
                    def at(per, n):
                        return n if i is None else i * (2 * per) + n
                    gu0 = l * 2 * F_TILES + ee * F_TILES
                    q0 = Q0 + piece_of["ffn"] + ee * (PAIR_PIECES // 2)
                    for f in range(F_TILES):
                        split_high(act, r)
                        split_high(act, r)
                        if f >= 2:
                            act.wait_ge(gu_full, at(F_TILES, gu0 + f - 1))
                        act.wait_ge(piece_done, at(PAIR_PIECES // 2, q0 + 2 * f + 2))
                        act.activation(sig[f % 2], bank(f % 2, 0, NT), ACT.Silu).then_inc(gu_silu, 1)
                        act.wait_ge(gu_full, at(F_TILES, gu0 + f + 1))
                        act.activation(tile(projR, FF_H + f), full[f % 2], ACT.Copy).then_inc(gu_high, 1)
                    for j in range(KT):
                        for _ in range(2):
                            split_high(act, r)

                rounds(act, r, l, expert)
            act.wait_ge(x_ready, 3 * DEPTH)
            norm(DEPTH * NORMS, xT, hT)

        @block.vector
        def _(dve):
            st = Steps(dve, dve_step)
            st(dve.memset(spx[:, :], 0.0))
            dve.wait_ge(dma_const, 64)
            dve.wait_ge(dma_small, 96)

            r = Ring()

            def scale(k, src, dst, gain, w=NT, s0=0, d0=0):
                dve.wait_ge(rs_ready, k + 1)
                for j in range(KT):
                    yield dve.scalar_tensor_tensor(out=tile(dst, d0 + j, 0, w), in0=tile(src, s0 + j, 0, w), scalar=gain(j),
                                                   in1=rstd[:, 0:w], op0=ALU.mult, op1=ALU.mult)

            def norm(k, k_h, gain):
                for ins in scale(k, xT, tmp, gain):
                    ins.then_inc(h_full, 1)
                if k < DEPTH * NORMS:
                    for j in range(KT):
                        dve.wait_ge(h_high, k_h * KT + j + 1)
                        dve.tensor_tensor(tile(hL, j), tile(tmp, j), f32(tile(hH, j)), ALU.subtract).then_inc(h_ready, 1)

            def add_to_x(n, q, j, pieces):
                for _ in range(pieces):
                    split_low(dve, r)
                dve.wait_ge(piece_done, q + 1)
                dve.tensor_tensor(tile(xT, j), bank(n % 2, 0, NT), tile(xT, j), ALU.add).then_inc(lin_free[n % 2], 1)
                if j == KT - 1:
                    for k in (n - 1, n):
                        dve.wait_ge(lin_free[k % 2], k // 2 + 1)
                    dve.sem_inc(x_ready, 1)

            for _ in range(AHEAD):
                split_low(dve, r)
            for l in range(DEPTH):
                L0 = l * LIN
                Q0 = LAYER_PIECE[l]
                norm(l * NORMS, 3 * l, lambda j: pcol(l, G_MIX + j))
                peel = 1 - l
                for j in range(2 * SLOTS * peel):
                    split_low(dve, r)
                r.begin(SLOTS)
                with dve.Fori(peel, IN_ITERS) as i:
                    r.i = i - peel if peel else i
                    for j in range(2 * SLOTS):
                        split_low(dve, r)
                r.end(IN_ITERS - peel)
                n = L0 + lin_of["gates"]
                dve.wait_ge(gate_sum, l + 1)
                b = n % 2
                dve.tensor_scalar(gI[:, :], bank(b, 0, NT, 6), hpar[0:6, 3 * l:3 * l + 1], None, ALU.add)
                dve.tensor_scalar(spx[0:6, 0:NT], bank(b, 0, NT, 6, 32), hpar[32:38, 3 * l:3 * l + 1], -1.0, ALU.add, ALU.mult)
                dve.tensor_scalar(spx[:, NT:2 * NT], bank(b, 0, NT, 12, 64), hpar[64:76, 3 * l:3 * l + 1], None, ALU.add).then_inc(lin_free[b], 1)
                dve.wait_ge(lin_free[b], n // 2 + 1)
                dve.scalar_tensor_tensor(out=spa[:, :], in0=spx[:, :], scalar=-1.0, in1=spx[:, :], op0=ALU.mult, op1=ALU.max).then_inc(gate_abs, 1)
                dve.wait_ge(gate_exp, l + 1)
                st(dve.tensor_scalar(spd[:, :], spu[:, :], 1.0, -1.0, ALU.add, ALU.add))
                dve.tensor_scalar(spa[:, :], spu[:, :], 1.0, None, ALU.add).then_inc(gate_one, 1)
                dve.wait_ge(gate_log, l + 1)
                st(dve.tensor_scalar(spa[:, :], spd[:, :], 0.0, None, ALU.is_equal))
                st(dve.tensor_tensor(spd[:, :], spd[:, :], spa[:, :], ALU.add))
                st(dve.tensor_tensor(spl[:, :], spl[:, :], spa[:, :], ALU.add))
                st(dve.reciprocal(spd[:, :], spd[:, :]))
                st(dve.tensor_tensor(spl[:, :], spl[:, :], spd[:, :], ALU.mult))
                st(dve.tensor_tensor(spl[:, :], spl[:, :], spu[:, :], ALU.mult))
                st(dve.scalar_tensor_tensor(out=spx[:, :], in0=spx[:, :], scalar=0.0, in1=spl[:, :], op0=ALU.max, op1=ALU.add))
                on = const[0:12, C_ONES:C_ONES + P]
                for ch in range(2):
                    a, z = ch * P, (ch + 1) * P
                    st(dve.tensor_tensor_scan(cum_f[:, a:z], on[0:6, :], spx[0:6, a:z], 0.0, ALU.mult, ALU.subtract))
                g0, g1 = grow[:, 0:P], grow[:, SEQ:384]
                st(dve.tensor_tensor(g0, gI[:, 0:P], cum_f[:, 0:P], ALU.subtract))
                st(dve.tensor_tensor(g1, gI[:, P:SEQ], cum_f[:, P:SEQ], ALU.subtract))
                st(dve.tensor_tensor_scan(run_max[:, 0:P], g0, g0, 0.0, ALU.max, ALU.max))
                st(dve.tensor_tensor(small[0:6, 1:2], cum_f[:, P - 1:P], run_max[:, P - 1:P], ALU.add))
                st(dve.tensor_tensor_scan(run_max[:, P:SEQ], g1, g1, small[0:6, 1:2], ALU.max, ALU.max))
                st(dve.tensor_scalar(negM[:, :], run_max[:, :], -1.0, None, ALU.mult))
                st(dve.scalar_tensor_tensor(out=negm[:, :], in0=cum_f[:, :], scalar=-1.0, in1=run_max[:, :], op0=ALU.mult, op1=ALU.subtract))
                st(dve.tensor_scalar(grow[:, P:SEQ], g0, cum_f[:, P - 1:P], None, ALU.add))
                st(dve.tensor_scalar(small[0:6, 2:3], negm[:, SEQ - 1:SEQ], -1.0, None, ALU.mult))
                st(dve.tensor_tensor(small[0:6, 16:24], m0[:, l * NB:(l + 1) * NB], spx[0:6, SEQ:NT], ALU.subtract))
                st(dve.tensor_tensor(small[0:6, 24:32], small[0:6, 16:24], gI[:, SEQ:NT], ALU.max))
                st(dve.tensor_tensor(smR[:, 0:8], gI[:, SEQ:NT], small[0:6, 24:32], ALU.subtract))
                st(dve.tensor_tensor(smR[:, 8:16], small[0:6, 16:24], small[0:6, 24:32], ALU.subtract))
                st(dve.tensor_scalar(smR[:, 16:24], small[0:6, 24:32], -1.0, None, ALU.mult))
                st(dve.tensor_scalar(lda[:, :], spx[:, NT:2 * NT], small[:, 0:1], -1.0, ALU.mult, ALU.mult))
                for ch in range(2):
                    a, z = ch * P, (ch + 1) * P
                    st(dve.tensor_tensor_scan(cum_a[:, a:z], on, lda[:, a:z], 0.0, ALU.mult, ALU.add))
                    st(dve.tensor_scalar(arow[:, 2 * a:2 * a + P], cum_a[:, a:z], -1.0, None, ALU.mult))
                dve.tensor_scalar(arow[:, P:SEQ], arow[:, 0:P], cum_a[:, P - 1:P], None, ALU.add).then_inc(gate_rows, 1)
                dve.wait_ge(k_scaled, l + 1)
                for j in range(2 * RH):
                    n = l * 2 * RH + j
                    cs, sn = C_COS, C_SIN
                    dve.wait_ge(rot_ready, n + 1)
                    dve.tensor_tensor(tile(hT, j % 2), bank(4 + n % 2, 0, NT), c(sn, NT), ALU.mult).then_inc(rot_used, 1)
                    dve.wait_ge(rot_used, n + 1)
                    st(dve.tensor_tensor(tile(proj, Q_R + j), tile(proj, Q_R + j), c(cs, NT), ALU.mult))
                    ins = dve.tensor_tensor(tile(proj, Q_R + j), tile(proj, Q_R + j), tile(hT, j % 2), ALU.add)
                ins.then_inc(rot_done, 1)
                o3, g3 = proj[:, O_ML * NT:Z * NT], proj[:, G_R * NT:N_PROJ * NT]
                dve.wait_ge(gate_cols, l + 1)
                dve.tensor_copy(gcol[:, :], bank(2, 0, 54)).then_inc(gate_cols_in, 1)
                dve.wait_ge(gate_bc, l + 1)
                dve.tensor_copy(gbc[:, :], bank(3, 0, 192)).then_inc(gate_bc_in, 1)
                dve.wait_ge(gate_bc_in, l + 1)
                gb = gbc[:, 0:144].rearrange("p (h q b) -> p h q b", h=NH, q=3)
                dve.wait_ge(k_scaled, l + 1)

                def r3(buf, n=6):
                    return buf.rearrange("p (h b) -> p h b", h=n)

                nn, vv = r3(nnew[:, :]), r3(vA[:, :])
                st(dve.tensor_tensor(nn, r3(nst[:, l * 48:(l + 1) * 48]), gb[:, :, 1, :], ALU.mult))
                st(dve.tensor_tensor(r3(yT2[:, :]), tiles3(proj, K_ML, NH, SEQ, NB), gb[:, :, 0, :], ALU.mult))
                st(dve.tensor_tensor(nn, nn, r3(yT2[:, :]), ALU.add))
                st(dve.tensor_tensor(vv, tiles3(proj, V_ML, NH, SEQ, NB), gb[:, :, 0, :], ALU.mult))
                dve.tensor_tensor(r3(yT2[:, :]), nn, tiles3(proj, Q_ML, NH, SEQ, NB), ALU.mult).then_inc(nq_ready, 1)
                dve.wait_ge(nden_ready, l + 1)
                st(dve.scalar_tensor_tensor(out=r3(rden[:, :]), in0=r3(bank(6, 0, 48)), scalar=-1.0, in1=gb[:, :, 2, :], op0=ALU.mult, op1=ALU.max))
                st(dve.tensor_tensor(rden[:, :], bank(6, 0, 48), rden[:, :], ALU.max))
                dve.reciprocal(rden[:, :], rden[:, :]).then_inc(nden_done, 1)
                for k in range(CONV_T):
                    u, y = tile(proj, XBC + k), tile(conv, k)

                    def tap(i):
                        return pcol(l, CONV_K + 4 * k + i)
                    st(dve.tensor_scalar(y, u, tap(3), pcol(l, CONV_B + k), ALU.mult, ALU.add))
                    for d in range(1, 4):
                        w = cst[:, ((l * CONV_T + k) * 3 + 3 - d) * NB:((l * CONV_T + k) * 3 + 4 - d) * NB]
                        dve.scalar_tensor_tensor(out=y[:, d:SEQ], in0=u[:, 0:SEQ - d], scalar=tap(3 - d), in1=y[:, d:SEQ], op0=ALU.mult, op1=ALU.add)
                        st(dve.scalar_tensor_tensor(out=y[:, SEQ:NT], in0=w, scalar=tap(3 - d), in1=y[:, SEQ:NT], op0=ALU.mult, op1=ALU.add))
                st(dve.tensor_copy(cvp[:, :].rearrange("p (c i) -> p c i", i=3), tiles3(proj, XBC, CONV_T, SEQ - 3, 3)))
                old = cst[:, l * CONV_T * 24:(l + 1) * CONV_T * 24].rearrange("p (c i b) -> p c i b", c=CONV_T, i=3)
                for i in range(2):
                    st(dve.tensor_copy(old[:, :, i, :], old[:, :, i + 1, :]))
                st(dve.tensor_copy(old[:, :, 2, :], tiles3(proj, XBC, CONV_T, SEQ, NB)))
                dve.sem_inc(conv_acc, 1)
                dve.wait_ge(conv_done, l + 1)
                dve.wait_ge(gates_done, l + 1)
                def unit_decay(u):
                    S = state(u)
                    S3 = S.rearrange("p (b f) -> p b f", b=NB)
                    dve.wait_ge(state_in[u % STATE_SLOTS], 16 * state_count(l, u))
                    if u < NH + SP:
                        dec = gb[:, u, 1, :] if u < NH else gbc[:, 144 + (u - NH) * NB:144 + (u - NH + 1) * NB]
                        st(dve.tensor_tensor(S3, S3, dec.unsqueeze(2).to_broadcast([P, NB, P]), ALU.mult))
                    else:
                        gamma = float(np.float32(1.0) - np.float32(2.0) ** np.float32(-5.0 - (u - NH - SP)))
                        st(dve.tensor_scalar(S, S, gamma, None, ALU.mult))

                def unit_half(u, half):
                    n = l * UNITS + u
                    S = state(u)[:, half * 512:(half + 1) * 512]
                    if u < NH:
                        a = vA[:, u * NB:(u + 1) * NB]
                    elif u < NH + SP:
                        a = xds[:, (u - NH) * NB:(u - NH + 1) * NB]
                    else:
                        a = tile(proj, V_R + u - NH - SP, SEQ, NB)
                    dve.wait_ge(dec_bc, 2 * n + half + 1)
                    for b in range(NB // 2):
                        at = half * (NB // 2) + b
                        ins = dve.scalar_tensor_tensor(out=S[:, b * P:(b + 1) * P], in0=bank(0, b * P, P), scalar=a[:, at:at + 1],
                                                       in1=S[:, b * P:(b + 1) * P], op0=ALU.mult, op1=ALU.add)
                    ins.then_inc(dec_S, 1)
                    dve.wait_ge(dec_S, 2 * n + half + 1)
                    dve.tensor_tensor(dP, S, bank(1), ALU.mult).then_inc(dec_read, 1)
                    dve.wait_ge(dec_read, 2 * n + half + 1)
                    st(dve.tensor_reduce(yT[:, half * (NB // 2):(half + 1) * (NB // 2)], dP.rearrange("p (b f) -> p b f", b=NB // 2), AX.X, ALU.add))
                    if half == 0:
                        return
                    if u < NH:
                        ins = dve.tensor_tensor(tile(proj, Q_ML + u, SEQ, NB), yT[:, :], rden[:, u * NB:(u + 1) * NB], ALU.mult)
                    elif u < NH + SP:
                        j = u - NH
                        st(dve.scalar_tensor_tensor(out=yT[:, :], in0=tile(conv, j, SEQ, NB), scalar=pcol(l, D_SKIP + j), in1=yT[:, :], op0=ALU.mult, op1=ALU.add))
                        ins = dve.tensor_tensor(tile(proj, Z + j, SEQ, NB), tile(proj, Z + j, SEQ, NB), yT[:, :], ALU.mult)
                    else:
                        ins = dve.tensor_copy(tile(proj, Q_R + u - NH - SP, SEQ, NB), yT[:, :])
                    ins.then_inc(dec_y, 1)
                    dve.wait_ge(dec_y, n + 1)

                for h in range(NH):
                    n = l * NH + h
                    unit_decay(h)
                    dve.wait_ge(ml_w, n + 1)
                    dve.tensor_tensor(mS, mW, bank(2, 0, 384), ALU.mult)
                    dve.tensor_scalar(mKW[:, 0:P], mVK[:, SEQ:384], mW[:, SEQ - 1:SEQ], None, ALU.mult)
                    dve.tensor_scalar(mKW[:, P:SEQ], mVK[:, 384:512], mW[:, 383:384], None, ALU.mult).then_inc(ml_weighted, 1)
                    unit_half(h, 0)
                    dve.wait_ge(ml_num, n + 1)
                    st(dve.scalar_tensor_tensor(out=mDN, in0=bank(6, SEQ, SEQ), scalar=-1.0, in1=mEM, op0=ALU.mult, op1=ALU.max))
                    st(dve.tensor_tensor(mDN, bank(6, SEQ, SEQ), mDN, ALU.max))
                    st(dve.reciprocal(mDN, mDN))
                    dve.tensor_tensor(tile(proj, Q_ML + h, 0, SEQ), bank(6, 0, SEQ), mDN, ALU.mult).then_inc(ml_h, 1)
                    unit_half(h, 1)
                dve.wait_ge(ml_h, (l + 1) * NH)
                for j in range(SP):
                    n, g = l * SP + j, j // 3
                    dve.wait_ge(ssd_dt, n + 1)
                    dve.tensor_tensor(sXD, tile(conv, j), bank(4, 0, NT), ALU.mult).then_inc(ssd_xdt, 1)
                    dve.wait_ge(ssd_xdt, n + 1)
                    st(dve.tensor_copy(xds[:, j * NB:(j + 1) * NB], sXD[:, SEQ:NT]))
                    unit_decay(NH + j)
                    dve.wait_ge(ssd_w, n + 1)
                    for hh in range(2):
                        dve.tensor_tensor(sS[:, hh * 384:(hh + 1) * 384], sL[:, hh * 384:(hh + 1) * 384], bank(2, 0, 384), ALU.mult)
                        for s_, at in ((0, SEQ - 1), (1, 383)):
                            ins = dve.tensor_scalar(sXW[:, s_ * P + 64 * hh:s_ * P + 64 * hh + 64], sXT[:, s_ * P + 64 * hh:s_ * P + 64 * hh + 64],
                                                    sL[:, hh * 384 + at:hh * 384 + at + 1], None, ALU.mult)
                    ins.then_inc(ssd_S, 1)
                    unit_half(NH + j, 0)
                    dve.wait_ge(ssd_y, n + 1)
                    st(dve.scalar_tensor_tensor(out=sY, in0=tile(conv, j, 0, SEQ), scalar=pcol(l, D_SKIP + j), in1=bank(4, 0, SEQ), op0=ALU.mult, op1=ALU.add))
                    dve.tensor_tensor(tile(proj, Z + j, 0, SEQ), tile(proj, Z + j, 0, SEQ), sY, ALU.mult).then_inc(ssd_h, 1)
                    unit_half(NH + j, 1)
                for h in range(RH):
                    n = l * RH + h
                    dve.wait_ge(ret_scores, n + 1)
                    if h == 0:
                        dve.wait_ge(ssd_state, (l + 1) * SP)
                    w0 = C_RET + h * 384
                    dve.tensor_tensor(mS, bank(2, 0, 384), c(w0, 384), ALU.mult)
                    unit_decay(NH + SP + h)
                    dve.wait_ge(ret_vk, n + 1)
                    dve.tensor_scalar(mKW[:, 0:P], mVK[:, SEQ:384], c(w0 + SEQ - 1, 1), None, ALU.mult)
                    dve.tensor_scalar(mKW[:, P:SEQ], mVK[:, 384:512], c(w0 + 383, 1), None, ALU.mult).then_inc(ret_weighted, 1)
                    for half in range(2):
                        unit_half(NH + SP + h, half)
                dve.wait_ge(ret_h, (l + 1) * RH)
                for k, (y0, nt, per, g0_) in enumerate(((Q_ML, NH, 1, G_ML), (Z, SP, 3, G_SSD), (Q_R, RH, 1, G_RET))):
                    dve.wait_ge(post_rs, 3 * l + k + 1)
                    for j in range(nt):
                        ins = dve.scalar_tensor_tensor(out=tile(proj, y0 + j), in0=tile(proj, y0 + j), scalar=pcol(l, g0_ + j), in1=tile(tmp, j // per),
                                                       op0=ALU.mult, op1=ALU.mult)
                    gate = {0: o3, 2: g3}.get(k)
                    if gate is None:
                        ins.then_inc(post_y, 1)
                    else:
                        st(ins)
                        ys = proj[:, y0 * NT:(y0 + nt) * NT]
                        dve.tensor_tensor(ys, ys, gate, ALU.mult).then_inc(post_y, 1)
                    dve.wait_ge(post_high, 3 * l + k + 1)
                    a, z = y0 * NT, (y0 + nt) * NT
                    dve.tensor_tensor(projR[:, a:z], proj[:, a:z], f32(projR[:, Y_HI[k] * NT:(Y_HI[k] + nt) * NT]), ALU.subtract).then_inc(post_low, 1)
                for j in range(KT):
                    add_to_x(L0 + lin_of["out"] + j, Q0 + piece_of["out"] + 2 * j + 1, j, 2)
                for ins in scale(l * NORMS + 1, proj, proj, lambda j: pcol(l, G_MEM + j), MEM, CA_MEM, CA_MEMN):
                    last = ins
                last.then_inc(mem_full, 1)
                dve.wait_ge(mem_high, l + 1)
                dve.tensor_tensor(tiles3(projR, CA_MEMN, KT, 0, MEM), tiles3(proj, CA_MEMN, KT, 0, MEM),
                                  f32(tiles3(projR, CA_MEMH, KT, 0, MEM)), ALU.subtract).then_inc(mem_low, 1)
                for j in range(2 * KT):
                    split_low(dve, r)
                norm(l * NORMS + 2, 3 * l + 1, lambda j: pcol(l, G_CA + j))
                for j in range(KT - AHEAD):
                    split_low(dve, r)
                for h in range(CAH):
                    n = l * CAH + h
                    dve.wait_ge(ca_scores, n + 1)
                    st(dve.tensor_reduce(sml[:, 4:6], bank(2).rearrange("p (a m) -> p a m", a=2), AX.X, ALU.max))
                    dve.tensor_scalar(sml[:, 0:2], sml[:, 4:6], -1.0 / 16, None, ALU.mult).then_inc(ca_max, 1)
                    dve.wait_ge(ca_exp, n + 1)
                    st(dve.reciprocal(sml[:, 6:8], sml[:, 2:4]))
                    for qt in range(2):
                        ins = dve.tensor_scalar(caP[:, qt * MEM:(qt + 1) * MEM], caP[:, qt * MEM:(qt + 1) * MEM], sml[:, 6 + qt:7 + qt], None, ALU.mult)
                    ins.then_inc(ca_p, 1)
                dve.wait_ge(cs_k, (l + 1) * NB)
                st(dve.tensor_reduce(sml[0:32, 10:11], bank(5, 0, MEM, 32), AX.X, ALU.max))
                dve.tensor_scalar(sml[0:32, 8:9], sml[0:32, 10:11], -1.0 / 16, None, ALU.mult).then_inc(cs_max, 1)
                dve.wait_ge(cs_exp, l + 1)
                st(dve.reciprocal(sml[0:32, 11:12], sml[0:32, 9:10]))
                dve.tensor_scalar(csP, csP, sml[0:32, 11:12], None, ALU.mult).then_inc(cs_p, 1)
                for _ in range(AHEAD):
                    split_low(dve, r)
                dve.wait_ge(o_high, l + 1)
                a, z = CA_O * NT, (CA_O + KT) * NT
                dve.tensor_tensor(projR[:, a:z], proj[:, a:z], f32(projR[:, CA_OH * NT:(CA_OH + KT) * NT]), ALU.subtract).then_inc(o_low, 1)
                for j in range(KT):
                    add_to_x(L0 + lin_of["o"] + j, Q0 + piece_of["o"] + j, j, 1)
                norm(l * NORMS + 3, 3 * l + 2, lambda j: pcol(l, G_FFN + j))
                moe = l % 2 == 1
                if moe:
                    T3 = 3 * NE
                    st(dve.memset(conv[:, 0:T3], 0.0))
                    dve.wait_ge(rt_logits, 1)
                    dve.tensor_copy(conv[:, 0:2 * NE], bank(7, 0, 2 * NE))
                    st(dve.tensor_copy(conv[0:NB, 2 * NE:T3], bank(7, 2 * NE, NE, NB)))
                    l3 = conv[:, 0:T3].rearrange("p (t e) -> p t e", t=3)
                    x3 = conv[:, 24:48].rearrange("p (t e) -> p t e", t=3)
                    st(dve.tensor_reduce(conv[:, 48:51], l3, AX.X, ALU.max))
                    dve.tensor_tensor(x3, l3, conv[:, 48:51].unsqueeze(2).to_broadcast([P, 3, NE]), ALU.subtract).then_inc(rt_max, 1)
                    gt, eq = conv[:, 64:64 + 192], conv[:, 256:256 + 192]
                    tie = c(C_TIE, 64).rearrange("p (e j) -> p e j", e=NE)
                    for tt in range(3):
                        other = conv[:, tt * NE:(tt + 1) * NE].unsqueeze(1).to_broadcast([P, NE, NE])
                        own = conv[:, tt * NE:(tt + 1) * NE].unsqueeze(2).to_broadcast([P, NE, NE])
                        g_ = gt[:, tt * 64:(tt + 1) * 64].rearrange("p (e j) -> p e j", e=NE)
                        e_ = eq[:, tt * 64:(tt + 1) * 64].rearrange("p (e j) -> p e j", e=NE)
                        st(dve.tensor_tensor(g_, other, own, ALU.is_gt))
                        st(dve.tensor_tensor(e_, other, own, ALU.is_equal))
                        st(dve.tensor_tensor(e_, e_, tie, ALU.mult))
                        st(dve.tensor_tensor(g_, g_, e_, ALU.add))
                    st(dve.tensor_reduce(conv[:, 512:536], gt.rearrange("p (t j) -> p t j", j=NE), AX.X, ALU.add))
                    st(dve.tensor_scalar(conv[:, 512:536], conv[:, 512:536], TOP_K - 0.5, None, ALU.is_lt))
                    dve.wait_ge(rt_exp, 1)
                    st(dve.tensor_tensor(conv[:, 512:536], conv[:, 512:536], conv[:, 24:48], ALU.mult))
                    w3 = conv[:, 512:536].rearrange("p (t e) -> p t e", t=3)
                    st(dve.tensor_reduce(conv[:, 48:51], w3, AX.X, ALU.add))
                    st(dve.reciprocal(conv[:, 48:51], conv[:, 48:51]))
                    dve.tensor_tensor(l3, w3, conv[:, 48:51].unsqueeze(2).to_broadcast([P, 3, NE]), ALU.mult).then_inc(rt_comb, 1)
                    dve.wait_ge(rt_turn, 1)
                    dve.tensor_copy(combT, bank(7, 64, NT, NE)).then_inc(rt_combT, 1)
                    dve.wait_ge(rt_combT, 1)
                dve.wait_ge(dma_out, 16 * OUTS * (l + 1))

                def expert(i, ee):
                    def at(per, n):
                        return n if i is None else i * (2 * per) + n
                    gu0, q0 = l * 2 * F_TILES + ee * F_TILES, Q0 + piece_of["ffn"] + ee * (PAIR_PIECES // 2)
                    if moe:
                        dve.tensor_scalar(combM, combT, const[0:NE, bass.ds(i * 2 + (C_ID + ee), 1)], None, ALU.mult).then_inc(ex_mask, 1)
                    for f in range(F_TILES):
                        split_low(dve, r)
                        split_low(dve, r)
                        if moe and f == 0:
                            dve.wait_ge(ex_bc, at(1, ee + 1))
                            st(dve.tensor_copy(combB, bank(6, 0, NT)))
                        dve.wait_ge(gu_silu, at(F_TILES, gu0 + f + 1))
                        sg = sig[f % 2]
                        if moe:
                            st(dve.tensor_tensor(sg, sg, combB, ALU.mult))
                        dve.tensor_tensor(full[f % 2], sg, bank(2 + f % 2, 0, NT), ALU.mult).then_inc(gu_full, 1)
                        dve.wait_ge(gu_high, at(F_TILES, gu0 + f + 1))
                        dve.tensor_tensor(tile(projR, FF_L + f), full[f % 2], f32(tile(projR, FF_H + f)), ALU.subtract).then_inc(gu_low, 1)
                    for j in range(KT):
                        for _ in range(2):
                            split_low(dve, r)
                        dve.wait_ge(piece_done, at(PAIR_PIECES // 2, q0 + 2 * F_TILES + 2 * j + 2))
                        dve.tensor_tensor(tile(xT, j), tile(xT, j), bank(4 + j % 2, 0, NT), ALU.add).then_inc(down_free, 1)

                rounds(dve, r, l, expert, st, 2 * (F_TILES + 1))
                dve.wait_ge(down_free, (2 * KT, 2 * KT + NE * KT)[l])
                dve.sem_inc(x_ready, 1)
            norm(DEPTH * NORMS, 3 * DEPTH, lambda j: par[:, DEPTH * N_PAR + j:DEPTH * N_PAR + j + 1])

        @block.gpsimd
        def _(pool):
            pool.wait_ge(dma_const, 64)

            def load_state(l, u):
                pool.dma_start(state(u), t["states"][l, u]).then_inc(state_in[u % STATE_SLOTS], 16)

            for l in range(DEPTH):
                for u in range(STATE_SLOTS):
                    if l:
                        pool.wait_ge(state_out[u], 16 * (state_count(l, u) - 1))
                        pool.wait_ge(dec_read, 2 * l * UNITS)
                    load_state(l, u)
                pool.wait_ge(gate_rows, l + 1)
                pool.dma_start(t["o_mp"][l], small[0:6, 2:3]).then_inc(dma_out, 16)
                pool.dma_start(t["o_ms"][l], small[0:6, 24:32]).then_inc(dma_out, 16)
                pool.wait_ge(conv_acc, l + 1)
                pool.dma_start(t["o_cvp"][l], cvp[:, :]).then_inc(dma_out, 16)
                pool.dma_start(t["o_cvs"][l], cst[:, l * CONV_T * 24:(l + 1) * CONV_T * 24]).then_inc(dma_out, 16)
                pool.wait_ge(nden_done, l + 1)
                pool.dma_start(t["o_ns"][l], nnew[:, :]).then_inc(dma_out, 16)
                for u in range(UNITS):
                    pool.wait_ge(dec_S, 2 * (l * UNITS + u + 1))
                    pool.dma_start(t["o_states"][l, u], state(u)).then_inc(state_out[u % STATE_SLOTS], 16)
                    if u + STATE_SLOTS < UNITS:
                        pool.wait_ge(state_out[u % STATE_SLOTS], 16 * state_count(l, u))
                        pool.wait_ge(dec_read, 2 * (l * UNITS + u + 1))
                        load_state(l, u + STATE_SLOTS)
                    if u == NH:
                        pool.wait_ge(ml_state, (l + 1) * NH)
                        pool.dma_start(t["o_np"][l], npr[:, :]).then_inc(dma_out, 16)
                        pool.dma_start(t["o_pst"][l, :, 0:NH, :], tiles3(proj, K_ML, NH, 0, P)).then_inc(dma_out, 16)
                    if u == NH + SP:
                        pool.wait_ge(ssd_state, (l + 1) * SP)
                        pool.dma_start(t["o_pst"][l, :, NH:NH + SP, :], tiles3(proj, V_ML, SP, 0, P)).then_inc(dma_out, 16)
                pool.wait_ge(ret_h, (l + 1) * RH)
                pool.dma_start(t["o_pst"][l, :, NH + SP:UNITS, :], tiles3(proj, K_R, RH, 0, P)).then_inc(dma_out, 16)
                pool.wait_ge(piece_done, LAYER_PIECE[l] + piece_of["memk"])
                pool.dma_start(tiles3(proj, CA_MEM, KT, 0, MEM), t["mem"]).then_inc(mem_in, 16)
                pool.wait_ge(v_turn, l + 1)
                pool.dma_start(t["o_mk"][l], tiles3(proj, CA_K, KT, 0, MEM)).then_inc(dma_out, 16)
                pool.dma_start(t["o_mv"][l], tiles3(proj, CA_VT, KT, 0, MEM)).then_inc(dma_out, 16)
                pool.wait_ge(h_ready, (3 * l + 2) * KT)
                pool.memset(csQ, 0.0).then_inc(cs_zero, 1)
                pool.memset(csPM, 0.0).then_inc(cs_zero, 1)
                pool.wait_ge(cs_zero, 2 * (l + 1))
                for n in (l * LIN + lin_of["q"] + 6, l * LIN + lin_of["q"] + 7):
                    pool.wait_ge(lin_free[n % 2], n // 2 + 1)
                qs = tiles3(proj, CA_Q, KT, SEQ, NB).rearrange("p (h k) b -> p k h b", k=2)
                for kk in range(2):
                    at = csQ[:, kk * 1024:(kk + 1) * 1024][:, 0:1024:CAH * NB + 1].rearrange("p (h b) -> p h b", h=CAH)
                    ins = pool.tensor_copy(at, qs[:, kk])
                ins.then_inc(cs_q, 1)
                pool.wait_ge(dma_out, 16 * OUTS * (l + 1))


OUTS = 11


def state_count(l, u):
    s = u % STATE_SLOTS
    per = len([q for q in range(UNITS) if q % STATE_SLOTS == s])
    return l * per + u // STATE_SLOTS + 1


def constants():
    f = np.float32
    k = np.zeros((P, N_CONST), f)
    idx = np.arange(P)
    k[:, C_ID:C_ID + P] = np.eye(P, dtype=f)
    k[:, C_MASK:C_MASK + P] = np.where(idx[:, None] <= idx[None, :], 0.0, MASKED)
    k[:, C_ONES:C_ONES + P] = 1.0
    for m in range(64):
        k[m + 64, C_ROT + m] = -1.0
        k[m, C_ROT + m + 64] = 1.0
    inv = (f(10000.0) ** (-np.arange(64, dtype=f) / f(64))).astype(f)
    pos = np.concatenate([np.arange(SEQ, dtype=f), np.full(NB, PAST_LEN, f)])
    ang = (np.concatenate([inv, inv])[:, None] * pos[None, :]).astype(f)
    for at, v in ((C_COS, np.cos(ang)), (C_SIN, np.sin(ang))):
        k[:, at:at + NT] = v
    for h in range(RH):
        log_g = np.log1p(-np.exp2(-5.0 - h))
        rel = np.arange(SEQ)[None, :] - idx[:, None]
        w = np.where(rel >= 0, np.exp(np.maximum(rel, 0) * log_g), 0.0)
        k[:, C_RET + h * 384:C_RET + h * 384 + SEQ] = w
        k[:, C_RET + h * 384 + SEQ:C_RET + (h + 1) * 384] = w[:, 0:P]
    tie = np.arange(NE)[None, :] < np.arange(NE)[:, None]
    k[:, C_TIE:C_TIE + 64] = tie.reshape(1, 64)
    for j in range(SP):
        k[2 * j, C_SEL2 + j * P:C_SEL2 + j * P + 64] = 1.0
        k[2 * j + 1, C_SEL2 + j * P + 64:C_SEL2 + (j + 1) * P] = 1.0
    k[:, C_EPS] = EPS
    return k


def lay_out(a):
    f = np.float32

    def cols(v):
        return np.asarray(v).reshape(-1, P).T

    def fm(x):
        return np.asarray(x).T.reshape(-1, P, x.shape[0]).transpose(1, 0, 2)

    def tiles(w):
        kk, n = w.shape
        return np.asarray(w).reshape(kk // P, P, n // P, P).transpose(2, 1, 0, 3)

    def blocks(w):
        v = tiles(w).reshape(-1, 2, P, PIECE)
        return v.transpose(0, 2, 1, 3).reshape(-1, P, BLOCK)

    o = {"const": constants()}
    x = np.concatenate([np.asarray(a["x_prompt"])[0], np.asarray(a["x_sample"])[:, 0]], 0)
    o["x"] = fm(x).reshape(P, -1)
    par = np.zeros((P, DEPTH * N_PAR + KT), f)
    for l in range(DEPTH):
        def put(at, v):
            par[:, l * N_PAR + at:l * N_PAR + at + v.shape[1]] = v
        for at, name in ((G_MIX, "norm_mix"), (G_CA, "norm_ca"), (G_MEM, "norm_mem"), (G_FFN, "norm_ffn"), (G_ML, "ml_norm"),
                         (G_SSD, "ssd_norm"), (G_RET, "ret_norm"), (CONV_B, "ssd_conv_b")):
            put(at, cols(a[name][l]))
        put(CONV_K, np.asarray(a["ssd_conv_w"][l]).reshape(4, CONV_T, P).transpose(2, 1, 0).reshape(P, -1))
        put(D_SKIP, cols(np.repeat(np.asarray(a["ssd_d"][l]), 64)))
    par[:, DEPTH * N_PAR:] = cols(a["norm_final"])
    o["par"] = par
    w_in = np.asarray(a["w_in"])
    i0 = 24 * P
    dt0 = i0 + 12 + 16 * P
    wg = np.zeros((P, DEPTH, KT, 76), f)
    hp = np.zeros((P, DEPTH, 3), f)
    w_main = []
    for l in range(DEPTH):
        w = w_in[l]
        w3 = w.reshape(KT, P, -1).transpose(1, 0, 2)
        wg[:, l, :, 0:6] = w3[:, :, i0:i0 + 6]
        wg[:, l, :, 32:38] = w3[:, :, i0 + 6:i0 + 12]
        wg[:, l, :, 64:76] = w3[:, :, dt0:dt0 + 12]
        hp[0:6, l, 0] = a["ml_i_bias"][l]
        hp[32:38, l, 0] = a["ml_f_bias"][l]
        hp[64:76, l, 0] = a["ssd_dt_bias"][l]
        main = np.concatenate([w[:, :i0], w[:, i0 + 12:dt0], w[:, dt0 + 12:]], 1)
        w_main.append(blocks(main))
    o["wgate"], o["hpar"], o["w_in"] = wg.reshape(P, -1), hp.reshape(P, -1), np.stack(w_main)
    o["alog"] = np.asarray(a["ssd_a_log"]).T
    o["m0"] = np.asarray(a["state_mlstm_m"]).transpose(2, 0, 1).reshape(NH, -1)
    o["nst"] = np.asarray(a["state_mlstm_n"]).transpose(3, 0, 2, 1).reshape(P, -1)
    o["cst"] = np.asarray(a["state_ssd_conv"]).reshape(DEPTH, NB, 3, CONV_T, P).transpose(4, 0, 3, 2, 1).reshape(P, -1)
    o["wrt"] = np.asarray(a["moe_w_router"])[0].reshape(KT, P, NE).transpose(1, 0, 2).reshape(P, -1)
    ml = np.asarray(a["state_mlstm_c"]).transpose(0, 2, 3, 1, 4)
    sd = np.asarray(a["state_ssd"]).reshape(DEPTH, NB, SP, P, P).transpose(0, 2, 3, 1, 4)
    rt = np.asarray(a["state_ret"]).transpose(0, 2, 4, 1, 3)
    o["states"] = np.concatenate([ml, sd, rt], 1).reshape(DEPTH, UNITS, P, NB * P)
    o["kc"] = np.asarray(a["cache_mem_k"]).reshape(DEPTH, NB, MEM, KT, P).transpose(0, 1, 4, 3, 2).reshape(DEPTH, NB, P, -1)
    o["vc"] = np.asarray(a["cache_mem_v"]).reshape(DEPTH, NB, 2, P, D_MODEL).transpose(0, 1, 3, 2, 4).reshape(DEPTH, NB, P, -1)
    o["mem"] = fm(np.asarray(a["mem_prompt"])[0])
    o["w_out"] = np.stack([tiles(w).reshape(KT, P, BLOCK) for w in np.asarray(a["w_out"])])
    for name, src in (("w_q", "w_ca_q"), ("w_k", "w_ca_k"), ("w_v", "w_ca_v"), ("w_o", "w_ca_o")):
        o[name] = np.stack([blocks(w) for w in np.asarray(a[src])])
    ff = F_TILES * P
    experts = []
    for h in range(2):
        experts.append([np.asarray(a[n])[0][:, h * ff:(h + 1) * ff] for n in ("ffn_w_gate", "ffn_w_up")]
                       + [np.asarray(a["ffn_w_down"])[0][h * ff:(h + 1) * ff]])
    for e in range(NE):
        experts.append([np.asarray(a[n])[0, e] for n in ("moe_w_gate", "moe_w_up", "moe_w_down")])
    o["w_gu"] = np.stack([np.stack([tiles(g), tiles(u)], 2).reshape(F_TILES, P, BLOCK) for g, u, _ in experts])
    o["w_down"] = np.stack([tiles(d).reshape(KT, P, ff) for _, _, d in experts])
    return {k: np.ascontiguousarray(v, dtype=f) for k, v in o.items()}


OUT_SHAPES = {
    "y": (P, KT * NT), "o_mp": (DEPTH, NH, 1), "o_ms": (DEPTH, NH, NB), "o_cvp": (DEPTH, P, CONV_T * 3), "o_cvs": (DEPTH, P, CONV_T * 3 * NB),
    "o_ns": (DEPTH, P, 48), "o_np": (DEPTH, P, NH), "o_pst": (DEPTH, P, UNITS, P), "o_states": (DEPTH, UNITS, P, NB * P),
    "o_mk": (DEPTH, P, KT, MEM), "o_mv": (DEPTH, P, KT, MEM),
}


def kernel(**inputs):
    from concourse import bacc
    from concourse.bass_utils import run_bass_kernel_spmd

    arrays = lay_out(inputs)
    nc = bacc.Bacc("TRN2", target_bir_lowering=False, num_devices=1)
    t = {k: nc.dram_tensor(f"{k}_dram", v.shape, F32, kind="ExternalInput").ap() for k, v in arrays.items()}
    t.update({k: nc.dram_tensor(f"{k}_dram", s, F32, kind="ExternalOutput").ap() for k, s in OUT_SHAPES.items()})
    program(nc, t)
    r = run_bass_kernel_spmd(nc, [{f"{k}_dram": v for k, v in arrays.items()}], core_ids=[0])
    o = {k: r.results[0][f"{k}_dram"] for k in OUT_SHAPES}

    y = o["y"].reshape(P, KT, NT).transpose(2, 1, 0).reshape(NT, D_MODEL)
    pst = o["o_pst"].transpose(0, 2, 1, 3)
    s = o["o_states"].reshape(DEPTH, UNITS, P, NB, P).transpose(0, 3, 1, 2, 4)
    cv = o["o_cvs"].reshape(DEPTH, P, CONV_T, 3, NB).transpose(0, 4, 3, 2, 1).reshape(DEPTH, NB, 3, -1)
    cvp = o["o_cvp"].reshape(DEPTH, P, CONV_T, 3).transpose(0, 3, 2, 1).reshape(DEPTH, 1, 3, -1)
    mk, mv = (o[n].transpose(0, 3, 2, 1).reshape(DEPTH, 1, MEM, CAH, 2 * P) for n in ("o_mk", "o_mv"))
    out = (
        y[:SEQ][None], y[SEQ:][:, None],
        pst[:, None, 0:NH], o["o_np"].transpose(0, 2, 1)[:, None], o["o_mp"][:, None, :, 0], cvp,
        pst[:, NH:NH + SP].reshape(DEPTH, 1, SH, 64, P), pst[:, None, NH + SP:], mk, mv,
        s[:, :, 0:NH], o["o_ns"].reshape(DEPTH, P, NH, NB).transpose(0, 3, 2, 1), o["o_ms"].transpose(0, 2, 1), cv,
        s[:, :, NH:NH + SP].reshape(DEPTH, NB, SH, 64, P), s[:, :, NH + SP:].swapaxes(-1, -2),
    )
    return tuple(np.ascontiguousarray(v) for v in out)
```

```python
from contextlib import ExitStack

import numpy as np

import concourse.bass as bass
from concourse import mybir

F32 = mybir.dt.float32
F32R = mybir.dt.float32r
ALU = mybir.AluOpType
ACT = mybir.ActivationFunctionType
AX = mybir.AxisListType

P = 128
D_MODEL, SEQ, DEPTH, NB = 1024, 256, 2, 8
PAST_LEN = 2048
KT = D_MODEL // P
NT = SEQ + NB
NH, SH, RH = 6, 12, 4
SP = SH // 2
NE, TOP_K = 8, 2
MEM, CAH = 256, 4
F_TILES = 11
CONV_T = 10
SQ_TILES = 2
EPS = 1e-6
MASKED = -30000.0

XBC, Q_R, K_R, Q_ML, K_ML, V_ML, O_ML, Z, V_R, G_R, N_PROJ = 0, 10, 14, 18, 24, 30, 36, 42, 48, 52, 56
IN_ORDER = ((XBC, 30), (Q_R, 40), (K_R, 44), (Q_ML, 0), (K_ML, 6), (V_ML, 12), (O_ML, 18), (Z, 24), (V_R, 48), (G_R, 52))
B_T, C_T = 6, 8
CA_Q, CA_K, CA_VT, CA_V, CA_O = 0, 8, 16, 24, 32
CA_MEM, CA_MEMN, CA_MEMH = 30, 48, 30
CA_OH, FF_H, FF_L = 40, 0, 11
Y_HI = (K_ML, XBC, K_R)

SLOTS = 4
BLOCK = 2048
PIECE, BUFS, AHEAD = BLOCK // 2, 4, 3
IN_ITERS, PEEL = N_PROJ // (2 * SLOTS), 2
GU_BLOCKS, DOWN_BLOCKS = F_TILES, KT
PAIR_BLOCKS, PAIR_EMPTY = 2 * (GU_BLOCKS + DOWN_BLOCKS), 2
PAIR_PIECES = 2 * PAIR_BLOCKS

G_MIX, G_CA, G_MEM, G_FFN, G_ML, G_SSD, G_RET, CONV_B, CONV_K, D_SKIP = 0, 8, 16, 24, 32, 38, 44, 48, 58, 98
N_PAR = 104
C_ID, C_MASK, C_ONES, C_EPS, N_FIRST = 0, 128, 256, 384, 386
C_ROT, C_COS, C_SIN, C_RET, C_TIE, C_SEL2, C_HALF, C_PAIR, N_CONST = 386, 514, 778, 1042, 2578, 2642, 3410, 3538, 3544
UNITS = NH + SP + RH
STATE_SLOTS = 3


class Steps:

    def __init__(self, eng, sem):
        self.eng, self.sem, self.n, self.i, self.per = eng, sem, 0, None, 0

    def __call__(self, ins):
        self.n += 1
        ins.then_inc(self.sem, 1)
        self.eng.wait_ge(self.sem, self.n if self.i is None else self.i * self.per + self.n)

    def begin(self, i, per):
        self.i, self.per, self.start = i, per, self.n

    def end(self, iters):
        assert self.n - self.start == self.per, (self.n - self.start, self.per)
        self.i, self.n = None, self.start + iters * self.per


class Ring:

    def __init__(self):
        self.used, self.at, self.piece, self.i, self.half = [0] * SLOTS, 0, 0, None, 0

    def block(self):
        if self.at in EMPTY_PLACES:
            self.at += PAIR_EMPTY
        s = self.at % SLOTS
        self.at, self.used[s] = self.at + 1, self.used[s] + 1
        return s, self.before(s)

    def before(self, s):
        return self.used[s] - 1 if self.i is None else self.i * self.per[s] + (self.used[s] - 1)

    def next_piece(self):
        if self.half == 0:
            if self.at in CACHE_PLACES:
                self.at, self.used = self.at + 2 * NB, [u + 2 * NB // SLOTS for u in self.used]
            self.s, _ = self.block()
        q = self.piece if self.i is None else self.i * self.pieces + self.piece
        out = self.s, self.before(self.s), self.half, q, self.piece % BUFS
        self.half, self.piece = 1 - self.half, self.piece + 1
        return out

    def begin(self, blocks):
        self.pieces, self.per, self.first, self.start = 2 * blocks, slot_uses(blocks), list(self.used), self.piece

    def end(self, iters):
        self.used = [b + iters * (u - b) for b, u in zip(self.first, self.used)]
        self.piece = self.start + iters * self.pieces
        self.i = None


def slot_uses(blocks):
    return [len([b for b in range(blocks) if b % SLOTS == s]) for s in range(SLOTS)]


LAYER_PLACES = [SLOTS * (PEEL + 1) + KT + 3 * 4 + 2 * NB + 4 + PAIR_BLOCKS + PAIR_EMPTY for l in range(DEPTH)]
CACHE_PLACES = [sum(LAYER_PLACES[0:l]) + SLOTS * (PEEL + 1) + KT + 3 * 4 for l in range(DEPTH)]
EMPTY_PLACES = [sum(LAYER_PLACES[0:l + 1]) - PAIR_EMPTY for l in range(DEPTH)]
ROUNDS = [1, NE // 2]


def rounds(eng, r, l, expert, st=None, steps=0):
    if ROUNDS[l] == 1:
        for ee in range(2):
            expert(None, ee)
    else:
        r.begin(PAIR_BLOCKS)
        with eng.Fori(0, ROUNDS[l]) as i:
            r.i = i
            if st:
                st.begin(i, steps)
            for ee in range(2):
                expert(i, ee)
        r.end(ROUNDS[l])
        if st:
            st.end(ROUNDS[l])


def program(nc, t):
    with ExitStack() as ctx:
        def sb(name, cols, rows=P, dt=F32):
            return ctx.enter_context(nc.sbuf_tensor(name, [rows, cols], dt))

        def view(name, cols, dt, offset):
            return nc.alloc_sbuf_tensor_at(name, [P, cols], dt, offset=offset)

        def sem(name):
            return ctx.enter_context(nc.semaphore(name))

        base = (nc.sbuf_base + 31) // 32 * 32
        arena = sb("arena", (2 * KT + N_PROJ) * NT + 8)
        hT, hH, hL = view("hT", KT * NT, F32, base), view("hH", KT * NT, F32R, base), view("hL", KT * NT, F32R, base + 4 * KT * NT)
        nrm = view("nrm", 2 * KT * NT, F32, base)
        proj, projR = (view(n_, N_PROJ * NT, dt, base + 8 * KT * NT) for n_, dt in (("proj", F32), ("projR", F32R)))
        wH, wL = sb("wH", BUFS * PIECE, dt=F32R), sb("wL", BUFS * PIECE, dt=F32R)
        ring = sb("ring", SLOTS * BLOCK)
        xT = sb("xT", KT * NT)
        conv = sb("conv", CONV_T * NT)
        tmp = sb("tmp", KT * NT)
        stream = sb("stream", STATE_SLOTS * 1024)
        const = sb("const", N_CONST)
        par = sb("par", DEPTH * N_PAR + KT)
        hpar = sb("hpar", DEPTH * 3)
        wgate = sb("wgate", DEPTH * KT * 76)
        nst = sb("nst", DEPTH * 48)
        cst = sb("cst", DEPTH * CONV_T * 3 * NB)
        m0 = sb("m0", DEPTH * NB, 6)
        alog = sb("alog", DEPTH, 12)
        wrt = sb("wrt", KT * NE)
        rstd = sb("rstd", NT)
        spx = sb("spx", 2 * NT, 12)
        spa, spu, spd, spl = (tmp[0:12, 2 * NT * i:2 * NT * (i + 1)] for i in range(4))
        gI = proj[0:6, (N_PROJ - 1) * NT:N_PROJ * NT]
        negM, negm = sb("negM", SEQ, 6), sb("negm", SEQ, 6)
        cum_f, run_max, grow, arow, lda = (tmp[0:r_, a:b] for r_, a, b in (
            (6, 0, 256), (6, 256, 512), (6, 512, 896), (12, 896, 1280), (12, 1280, 1544)))
        mldiag, ssdiag = tmp[0:6, 1600:1744], tmp[0:12, 1760:1808]
        tapped = tmp[:, 1840:1840 + NT]
        cum_a = sb("cum_a", SEQ, 12)
        small = sb("small", 40, 12)
        smR = sb("smR", 24, 6)
        gcol = sb("gcol", 54)
        gbc = sb("gbc", 192)
        nnew = sb("nnew", 48)
        rden = sb("rden", 48)
        npr = sb("npr", NH)
        vA = sb("vA", 48)
        xds = sb("xds", 48)
        yT = sb("yT", NB)
        yT2 = sb("yT2", 48)
        cvp = sb("cvp", CONV_T * 3)
        sml = sb("sml", 64)
        ps = ctx.enter_context(nc.psum_tensor("ps", [P, 8 * 512], F32))

        dma_const, dma_small, dma_tables, dma_out = sem("dma_const"), sem("dma_small"), sem("dma_tables"), sem("dma_out")
        landed = [sem(f"landed{s}") for s in range(SLOTS)]
        hi_ready, lo_ready = sem("hi_ready"), sem("lo_ready")
        piece_done = sem("piece_done")
        state_in = [sem(f"state_in{s}") for s in range(STATE_SLOTS)]
        state_out = [sem(f"state_out{s}") for s in range(STATE_SLOTS)]
        mem_in = sem("mem_in")
        act_step, dve_step, pool_step = sem("act_step"), sem("dve_step"), sem("pool_step")
        gate_sum, lin_free = sem("gate_sum"), [sem("lin_free0"), sem("lin_free1")]
        sq_ready, ss_ready, rs_ready, h_full, h_high, h_ready, x_ready = (sem(n) for n in (
            "sq_ready", "ss_ready", "rs_ready", "h_full", "h_high", "h_ready", "x_ready"))
        gate_abs, gate_exp, gate_one, gate_log = (sem(n) for n in ("gate_abs", "gate_exp", "gate_one", "gate_log"))
        gate_rows, gate_cols, gate_cols_in, gate_sexp, gate_diag, gate_bc, gate_bc_in = (sem(n) for n in (
            "gate_rows", "gate_cols", "gate_cols_in", "gate_sexp", "gate_diag", "gate_bc", "gate_bc_in"))
        k_scaled, gates_done, conv_acc, conv_done = (sem(n) for n in ("k_scaled", "gates_done", "conv_acc", "conv_done"))
        rot_ready, rot_used, rot_done = sem("rot_ready"), sem("rot_used"), sem("rot_done")
        nq_ready, nden_ready, nden_done = sem("nq_ready"), sem("nden_ready"), sem("nden_done")
        ml_gates, ml_turned, ml_scores, ml_w, ml_weighted, ml_num, ml_h, ml_state = (sem(n) for n in (
            "ml_gates", "ml_turned", "ml_scores", "ml_w", "ml_weighted", "ml_num", "ml_h", "ml_state"))
        ssd_turned, ssd_cb, ssd_dt, ssd_xdt, ssd_L, ssd_w, ssd_S, ssd_y, ssd_h, ssd_state = (sem(n) for n in (
            "ssd_turned", "ssd_cb", "ssd_dt", "ssd_xdt", "ssd_L", "ssd_w", "ssd_S", "ssd_y", "ssd_h", "ssd_state"))
        ret_scores, ret_vk, ret_weighted, ret_num, ret_h = (sem(n) for n in (
            "ret_scores", "ret_vk", "ret_weighted", "ret_num", "ret_h"))
        dec_decay, dec_bc, dec_S, dec_read, dec_y = (sem(n) for n in ("dec_decay", "dec_bc", "dec_S", "dec_read", "dec_y"))
        post_gated = sem("post_gated")
        post_sq, post_ss, post_ln, post_rs, post_y, post_high, post_low = (sem(n) for n in (
            "post_sq", "post_ss", "post_ln", "post_rs", "post_y", "post_high", "post_low"))
        mem_full, mem_high, mem_low, v_turn, v_turned = (sem(n) for n in ("mem_full", "mem_high", "mem_low", "v_turn", "v_turned"))
        o_high, o_low = sem("o_high"), sem("o_low")
        ca_scores, ca_max, ca_exp, ca_p, ca_pt, ca_ptc, ca_o, ca_oc = (sem(n) for n in (
            "ca_scores", "ca_max", "ca_exp", "ca_p", "ca_pt", "ca_ptc", "ca_o", "ca_oc"))
        cs_zero, cs_q, cs_k, cs_max, cs_exp, cs_p, cs_back, cs_backc, cs_v, cs_o, cs_turn, cs_oc = (sem(n) for n in (
            "cs_zero", "cs_q", "cs_k", "cs_max", "cs_exp", "cs_p", "cs_back", "cs_backc", "cs_v", "cs_o", "cs_turn", "cs_oc"))
        rt_logits, rt_max, rt_exp, rt_comb, rt_turn, rt_combT = (sem(n) for n in (
            "rt_logits", "rt_max", "rt_exp", "rt_comb", "rt_turn", "rt_combT"))
        ex_mask, ex_bc, gu_silu, gu_full, gu_high, gu_low, down_free = (sem(n) for n in (
            "ex_mask", "ex_bc", "gu_silu", "gu_full", "gu_high", "gu_low", "down_free"))
        y_out = sem("y_out")

        def bank(b, lo=0, n=512, rows=P, r0=0):
            return ps[r0:r0 + rows, b * 512 + lo:b * 512 + lo + n]

        def tile(buf, i, lo=0, n=NT, rows=P):
            return buf[0:rows, i * NT + lo:i * NT + lo + n]

        def tiles3(buf, i, n, lo=0, w=NT):
            return buf[:, i * NT:(i + n) * NT].rearrange("p (k t) -> p k t", k=n)[:, :, lo:lo + w]

        def c(at, n=P, rows=P):
            return const[0:rows, at:at + n]

        def pcol(l, at):
            return par[:, l * N_PAR + at:l * N_PAR + at + 1]

        def slot(s, lo=0, n=BLOCK):
            return ring[:, s * BLOCK + lo:s * BLOCK + lo + n]

        def state(u):
            return stream[:, (u % STATE_SLOTS) * 1024:(u % STATE_SLOTS + 1) * 1024]

        def unit_bc(u):
            if u < NH:
                tiles = (proj, K_ML + u), (proj, Q_ML + u)
            elif u < NH + SP:
                g = (u - NH) // 3
                tiles = (conv, B_T + g), (conv, C_T + g)
            else:
                tiles = (proj, K_R + u - NH - SP), (proj, Q_R + u - NH - SP)
            return [tile(buf, i, SEQ, NB) for buf, i in tiles]

        def f32(ap):
            return ap.bitcast(F32)

        def split_high(act, r):
            s, landed_before, half, q, buf = r.next_piece()
            act.wait_ge(landed[s], landed_before * 16 + 16)
            if r.i is not None or q >= BUFS:
                act.wait_ge(piece_done, q + (1 - BUFS))
            act.activation(wH[:, buf * PIECE:(buf + 1) * PIECE], slot(s, half * PIECE, PIECE), ACT.Copy).then_inc(hi_ready, 1)

        def split_low(dve, r):
            s, _, half, q, buf = r.next_piece()
            dve.wait_ge(hi_ready, q + 1)
            dve.tensor_tensor(wL[:, buf * PIECE:(buf + 1) * PIECE], slot(s, half * PIECE, PIECE),
                              f32(wH[:, buf * PIECE:(buf + 1) * PIECE]), ALU.subtract).then_inc(lo_ready, 1)

        ident, ones = c(C_ID), c(C_ONES)
        mW, mS, mVK, mKW, mEM, mDN = (hT[:, a:b] for a, b in (
            (0, 384), (384, 768), (768, 1280), (1280, 1536), (1536, 1792), (1792, 2048)))
        sXD, sXT, sS, sXW, sY, sBT = (hT[:, a:b] for a, b in (
            (0, 264), (264, 520), (520, 1288), (1288, 1544), (1544, 1800), (1800, 2056)))
        sL = tmp[:, 0:768]
        dP = tmp[:, 1024:1536]
        caP, caPT = conv[:, 0:512], conv[:, 1024:1536]
        csQ, csPM, csP, csO = tmp[:, 0:2 * 1024], conv[:, 1800:2312], conv[0:32, 1536:1792], tmp[0:NB, 0:D_MODEL]
        combT, combM, combB = conv[0:8, 1024:1024 + NT], conv[0:8, 1300:1300 + NT], conv[:, 1600:1600 + NT]
        sig, full = [tile(tmp, i) for i in range(2)], [tile(tmp, 2 + i) for i in range(2)]
        lg = conv[:, 0:24]

        lin_of, piece_of, n, q = {}, {}, 0, 0
        for name, k, pieces in (("gates", 1, 0), ("in", N_PROJ, 1), ("out", KT, 2), ("memk", KT, 1), ("memv", KT, 1), ("q", KT, 1), ("o", KT, 1)):
            lin_of[name], piece_of[name] = n, q
            n, q = n + k, q + k * pieces
        LIN, piece_of["ffn"] = n, q
        LAYER_PIECE = [0, q + ROUNDS[0] * PAIR_PIECES]
        NORMS = 4
        POST = ((Q_ML, NH, 1, G_ML, 10, 2), (Z, SP, 3, G_SSD, 0, 0), (Q_R, RH, 1, G_RET, 6, 2))
        block = ctx.enter_context(nc.Block())

        @block.sync
        def _(sp):
            r = Ring()
            free = [None] * SLOTS

            def load(src, n=BLOCK, by=None, wrap=0):
                q = r.piece
                s, _ = r.block()
                if r.i is None:
                    if free[s]:
                        sp.wait_ge(*free[s])
                    value = q + 2
                else:
                    sp.wait_ge(lo_ready, r.i * r.pieces + max(free[s][1], wrap))
                    value = q + 2
                free[s] = by or (lo_ready, value)
                if by is None:
                    r.piece += 2
                sp.dma_start(slot(s, 0, n), src).then_inc(landed[s], 16)

            for dst, src in ((xT[:, :], t["x"]), (const[:, 0:N_FIRST], t["const"][:, 0:N_FIRST]), (par[:, :], t["par"]), (wgate[:, :], t["wgate"])):
                sp.dma_start(dst, src).then_inc(dma_const, 16)
            for dst, name in ((hpar, "hpar"), (nst, "nst"), (cst, "cst"), (m0, "m0"), (alog, "alog"), (wrt, "wrt")):
                sp.dma_start(dst[:, :], t[name]).then_inc(dma_small, 16)

            def expert(e, first):
                gu, down = (t[k].rearrange("e b p n -> p (e b) n") for k in ("w_gu", "w_down"))
                for j in range(GU_BLOCKS):
                    load(gu[:, bass.ds(e * GU_BLOCKS + j, 1), :], wrap=wraps[j] if first and j < SLOTS else 0)
                for j in range(DOWN_BLOCKS):
                    load(down[:, bass.ds(e * DOWN_BLOCKS + j, 1), :], F_TILES * P)

            for l in range(DEPTH):
                w_in = t["w_in"][l].rearrange("b p n -> p b n")
                for j in range(PEEL * SLOTS):
                    load(t["w_in"][l, j])
                    if l == 0 and j == SLOTS - 1:
                        sp.dma_start(const[:, N_FIRST:N_CONST], t["const"][:, N_FIRST:N_CONST]).then_inc(dma_tables, 16)
                r.begin(SLOTS)
                with sp.Fori(PEEL, IN_ITERS) as i:
                    r.i = i - PEEL
                    for j in range(SLOTS):
                        load(w_in[:, bass.ds(i * SLOTS + j, 1), :], wrap=r.start - 2 * SLOTS + 2 * j + 2)
                r.end(IN_ITERS - PEEL)
                free = [(lo_ready, r.piece - 2 * SLOTS + 2 * j + 2) for j in range(SLOTS)]
                for j in range(KT):
                    load(t["w_out"][l, j])
                for name in ("w_k", "w_v", "w_q"):
                    for j in range(4):
                        load(t[name][l, j])
                for b in range(NB):
                    load(t["kc"][l, b], by=(cs_k, l * NB + b + 1))
                for b in range(NB):
                    load(t["vc"][l, b], by=(cs_v, l * NB + b + 1))
                for j in range(4):
                    load(t["w_o"][l, j])
                first_piece = r.piece
                wraps = []
                for j in range(SLOTS):
                    place = j + PAIR_BLOCKS + PAIR_EMPTY - SLOTS
                    while place >= PAIR_BLOCKS:
                        place -= SLOTS
                    wraps.append(first_piece + 2 * (place - PAIR_BLOCKS) + 2)
                if l == 0:
                    for e in range(2):
                        expert(e, e == 0)
                else:
                    r.begin(PAIR_BLOCKS)
                    with sp.Fori(0, ROUNDS[l]) as i:
                        r.i = i
                        for e in range(2):
                            expert(i * 2 + (2 + e), e == 0)
                    shift = (ROUNDS[l] - 1) * PAIR_PIECES
                    free = [(lo_ready, f[1] + shift) for f in free]
                    r.end(ROUNDS[l])
            for j in range(2):
                load(t["w_in"][0, j])
            sp.wait_ge(h_full, (3 * DEPTH + 1) * KT)
            sp.dma_start(t["y"], tmp[:, :]).then_inc(y_out, 16)
            sp.wait_ge(y_out, 16)
            sp.wait_ge(dma_out, 16 * DEPTH * OUTS)
            for s in range(STATE_SLOTS):
                sp.wait_ge(state_out[s], 16 * DEPTH * len([u for u in range(UNITS) if u % STATE_SLOTS == s]))
            for s in range(SLOTS):
                sp.wait_ge(landed[s], 16 * r.used[s])

        @block.tensor
        def _(pe):
            r = Ring()

            def lin_bank(n):
                if n >= 2:
                    pe.wait_ge(lin_free[n % 2], n // 2)
                return n % 2

            def norm_sum(k, src, w=NT, s0=0):
                for j in range(KT):
                    if j % SQ_TILES == 0:
                        pe.wait_ge(sq_ready, (k * KT + j) // SQ_TILES + 1)
                    ins = pe.matmul(bank(6, 0, w), ones, tile(src, s0 + j, 0, w), start=j == 0, stop=j == KT - 1)
                ins.then_inc(ss_ready, 1)

            def product(dst, high, low, kts=KT, k0=0, k_all=KT, ready=0):
                _, _, _, q, buf = r.next_piece()
                pe.wait_ge(lo_ready, q + 1)
                for k in range(kts):
                    if ready:
                        pe.wait_ge(h_ready, ready + k + 1)
                    wh, wl = (w[:, buf * PIECE + k * P:buf * PIECE + (k + 1) * P] for w in (wH, wL))
                    pe.matmul(dst, wh, high(k0 + k), start=k0 + k == 0, stop=False)
                    pe.matmul(dst, wh, low(k0 + k), start=False, stop=False)
                    ins = pe.matmul(dst, wl, high(k0 + k), start=False, stop=k0 + k == k_all - 1)
                ins.then_inc(piece_done, 1)

            def tiles_out(name, l, js, high, low, w=NT, halves=1):
                for j in js:
                    b = lin_bank(l * LIN + lin_of[name] + j)
                    for half in range(halves):
                        product(bank(b, 0, w), high, low, k0=half * KT, k_all=halves * KT)

            def causal(dst, h, rows, row):
                sel = ident[0:rows, h:h + 1].to_broadcast([rows, P])
                pe.matmul(dst[:, 0:SEQ], sel, row[:, 0:SEQ], start=True, stop=False, skip_group_check=True)
                pe.matmul(dst[:, 0:P], ident, c(C_MASK), start=False, stop=True, skip_group_check=True)
                pe.matmul(dst[:, SEQ:384], sel, row[:, P:SEQ], start=True, stop=False, skip_group_check=True)
                return pe.matmul(dst[:, SEQ:384], ident, c(C_MASK), start=False, stop=True, skip_group_check=True)

            def blocks3(dst, lhs, rhs):
                pe.matmul(dst[:, 0:P], lhs(0), rhs[:, 0:P], start=True, stop=True, skip_group_check=True)
                pe.matmul(dst[:, P:SEQ], lhs(0), rhs[:, P:SEQ], start=True, stop=False, skip_group_check=True)
                return pe.matmul(dst[:, P:SEQ], lhs(1), rhs[:, SEQ:384], start=False, stop=True, skip_group_check=True)

            pe.wait_ge(dma_const, 64)
            for l in range(DEPTH):
                L0 = l * LIN
                norm_sum(l * NORMS, hT)

                def h_high_part(k):
                    return tile(hH, k)

                def h_low_part(k):
                    return tile(hL, k)

                b = lin_bank(L0 + lin_of["gates"])
                for k in range(KT):
                    pe.wait_ge(h_full, 3 * l * KT + k + 1)
                    ins = pe.matmul(bank(b, 0, NT, 76), wgate[:, (l * KT + k) * 76:(l * KT + k + 1) * 76], tile(tmp, k), start=k == 0, stop=k == KT - 1)
                ins.then_inc(gate_sum, 1)
                pe.wait_ge(h_ready, (3 * l + 1) * KT)
                n0 = L0 + lin_of["in"]
                per = 2 * SLOTS
                tiles_out("in", l, range(PEEL * per), h_high_part, h_low_part)
                r.begin(SLOTS)
                with pe.Fori(PEEL, IN_ITERS) as i:
                    r.i = i - PEEL
                    for j in range(per):
                        n = n0 + j
                        pe.wait_ge(lin_free[n % 2], i * (per // 2) + n // 2)
                        product(bank(n % 2, 0, NT), h_high_part, h_low_part)
                r.end(IN_ITERS - PEEL)
                pe.wait_ge(gate_rows, l + 1)
                for j in range(3):
                    pe.transpose(bank(2, 6 * j, 6), grow[:, j * P:(j + 1) * P], ident[0:6, 0:6])
                for j in range(3):
                    ins = pe.transpose(bank(2, 18 + 12 * j, 12), arow[:, j * P:(j + 1) * P], ident[0:12, 0:12])
                ins.then_inc(gate_cols, 1)
                if l == 0:
                    pe.wait_ge(dma_tables, 16)
                pe.wait_ge(gate_diag, l + 1)
                pe.matmul(bank(3, 0, 144), ones[0:6, :], mldiag, start=True, stop=True)
                pe.matmul(bank(3, 144, 48), c(C_HALF, P, 12), ssdiag, start=True, stop=True).then_inc(gate_bc, 1)

                def rotate(h, banks):
                    for jj, (b, i) in enumerate(zip(banks, (Q_R, K_R))):
                        pe.matmul(bank(b, 0, NT), c(C_ROT), tile(proj, i + h), start=True, stop=True).then_inc(rot_ready, 1)

                for n in (n0 + N_PROJ - 2, n0 + N_PROJ - 1):
                    pe.wait_ge(lin_free[n % 2], n // 2 + 1)

                def spread(u, half):
                    n = 2 * (l * UNITS + u) + half
                    if n > 2 * l * UNITS:
                        pe.wait_ge(dec_read, n)
                    for bk, col in enumerate(unit_bc(u)):
                        for b in range(NB // 2):
                            at = half * (NB // 2) + b
                            ins = pe.matmul(bank(bk, b * P, P), col[:, at:at + 1].to_broadcast([P, P]), ident, start=True, stop=True)
                    ins.then_inc(dec_bc, 1)

                pe.wait_ge(k_scaled, l + 1)
                pe.wait_ge(gate_cols_in, l + 1)
                pe.wait_ge(gate_bc_in, l + 1)

                def turn_vk(b, v, k):
                    for st in range(2):
                        pe.transpose(bank(b, st * P, P), tile(proj, v, st * P, P), ident)
                    for st in range(2):
                        ins = pe.transpose(bank(b, SEQ + st * P, P), tile(proj, k, st * P, P), ident)
                    return ins

                def scores(b, k, q):
                    pe.matmul(bank(b, 0, SEQ), tile(proj, k, 0, P), tile(proj, q, 0, SEQ), start=True, stop=True)
                    return pe.matmul(bank(b, SEQ, P), tile(proj, k, P, P), tile(proj, q, P, P), start=True, stop=True)

                def ml_a(h):
                    n = l * NH + h
                    if h:
                        pe.wait_ge(ml_weighted, n)
                        pe.wait_ge(ml_w, n)
                    causal(bank(3, 0, 384), h, 6, negM)
                    pe.matmul(bank(4, 0, SEQ), ident[0:6, h:h + 1].to_broadcast([6, P]), negm[:, :], start=True, stop=True).then_inc(ml_gates, 1)
                    turn_vk(5, V_ML + h, K_ML + h).then_inc(ml_turned, 1)
                    scores(2, K_ML + h, Q_ML + h).then_inc(ml_scores, 1)

                def ml_d(h):
                    n = l * NH + h
                    pe.wait_ge(ml_weighted, n + 1)
                    if h == 0:
                        pe.wait_ge(nden_done, l + 1)
                    else:
                        pe.wait_ge(ml_h, n)
                        pe.wait_ge(ml_state, n)
                    blocks3(bank(6, 0, SEQ), lambda st: mVK[:, st * P:(st + 1) * P], mS)
                    blocks3(bank(6, SEQ, SEQ), lambda st: ones, mS)
                    for st in range(2):
                        pe.matmul(bank(7, 0, P), mVK[:, st * P:(st + 1) * P], mKW[:, st * P:(st + 1) * P], start=st == 0, stop=st == 1)
                    for st in range(2):
                        ins = pe.matmul(bank(7, P, 1), mKW[:, st * P:(st + 1) * P], ones[:, 0:1], start=st == 0, stop=st == 1)
                    ins.then_inc(ml_num, 1)

                for h in range(NH):
                    ml_a(h)
                    if h == 0:
                        pe.wait_ge(nq_ready, l + 1)
                        pe.matmul(bank(6, 0, 48), ones, yT2[:, :], start=True, stop=True).then_inc(nden_ready, 1)
                    spread(h, 0)
                    ml_d(h)
                    spread(h, 1)
                pe.wait_ge(ml_h, (l + 1) * NH)
                pe.wait_ge(ml_state, (l + 1) * NH)
                pe.wait_ge(conv_done, l + 1)
                for j in range(SP):
                    n, g = l * SP + j, j // 3
                    if j:
                        pe.wait_ge(ssd_w, n)
                    for hh in range(2):
                        ins = causal(bank(6 + hh, 0, 384), 2 * j + hh, 12, cum_a)
                    ins.then_inc(ssd_L, 1)
                    if j % 3 == 0:
                        if j:
                            pe.wait_ge(ssd_S, n)
                        bT, cT = tile(conv, B_T + g), tile(conv, C_T + g)
                        pe.matmul(bank(2, 0, SEQ), bT[:, 0:P], cT[:, 0:SEQ], start=True, stop=True)
                        pe.matmul(bank(2, SEQ, P), bT[:, P:SEQ], cT[:, P:SEQ], start=True, stop=True)
                        for st in range(2):
                            ins = pe.transpose(bank(3, st * P, P), bT[:, st * P:(st + 1) * P], ident)
                        ins.then_inc(ssd_cb, 1)
                    if j:
                        pe.wait_ge(ssd_h, n)
                        pe.wait_ge(ssd_state, n)
                    pe.matmul(bank(4, 0, NT), const[0:12, C_SEL2 + j * P:C_SEL2 + (j + 1) * P], spx[:, NT:2 * NT],
                              start=True, stop=True).then_inc(ssd_dt, 1)
                    pe.wait_ge(ssd_xdt, n + 1)
                    for st in range(2):
                        ins = pe.transpose(bank(5, st * P, P), sXD[:, st * P:(st + 1) * P], ident)
                    ins.then_inc(ssd_turned, 1)
                    spread(NH + j, 0)
                    if j == SP - 1:
                        pe.wait_ge(ssd_w, n + 1)
                        rotate(0, (6, 7))
                    pe.wait_ge(ssd_S, n + 1)
                    for hh in range(2):
                        dst = ps[64 * hh:64 * hh + 64, 4 * 512:4 * 512 + SEQ]
                        blocks3(dst, lambda st: sXT[:, st * P + 64 * hh:st * P + 64 * hh + 64], sS[:, hh * 384:(hh + 1) * 384])
                    for st in range(2):
                        ins = pe.matmul(bank(5, SEQ, P), sXW[:, st * P:(st + 1) * P], sBT[:, st * P:(st + 1) * P], start=st == 0, stop=st == 1)
                    ins.then_inc(ssd_y, 1)
                    spread(NH + j, 1)
                pe.wait_ge(ssd_h, (l + 1) * SP)
                pe.wait_ge(ssd_state, (l + 1) * SP)
                for h in range(RH):
                    n = l * RH + h
                    pe.wait_ge(rot_done, n + 1)
                    if h:
                        pe.wait_ge(ret_h, n)
                    scores(2, K_R + h, Q_R + h)
                    turn_vk(5, V_R + h, K_R + h).then_inc(ret_scores, 1)
                    spread(NH + SP + h, 0)
                    if h + 1 < RH:
                        rotate(h + 1, (3, 4))
                    pe.wait_ge(ret_weighted, n + 1)
                    pe.wait_ge(ret_vk, n + 1)
                    blocks3(bank(6, 0, SEQ), lambda st: mVK[:, st * P:(st + 1) * P], mS)
                    for st in range(2):
                        ins = pe.matmul(bank(7, 0, P), mKW[:, st * P:(st + 1) * P], mVK[:, st * P:(st + 1) * P], start=st == 0, stop=st == 1)
                    ins.then_inc(ret_num, 1)
                    spread(NH + SP + h, 1)
                pe.wait_ge(ret_h, (l + 1) * RH)
                for k, (_, nt, per, _, s0, b0) in enumerate(POST):
                    pe.wait_ge(post_sq, 3 * l + k + 1)
                    if k == 1:
                        pe.wait_ge(dec_read, 2 * (l + 1) * UNITS)
                    if k == 2:
                        pe.wait_ge(post_ln, l + 1)
                    for j in range(nt):
                        ins = pe.matmul(bank(b0 + j // per, 0, NT), ones, tile(nrm, s0 + j), start=j % per == 0, stop=j % per == per - 1)
                    ins.then_inc(post_ss, 1)
                lows = [Q_ML + h for h in range(NH)] + [Z + j for j in range(SP)] + [Q_R + h for h in range(RH)]
                highs = [Y_HI[0] + h for h in range(NH)] + [Y_HI[1] + j for j in range(SP)] + [Y_HI[2] + h for h in range(RH)]
                pe.wait_ge(post_rs, 3 * l + 2)
                for j in range(KT):
                    b = lin_bank(L0 + lin_of["out"] + j)
                    for half in range(2):
                        if j == 0:
                            pe.wait_ge(post_low, 3 * l + 2 + half)
                        product(bank(b, 0, NT), lambda k: tile(projR, highs[k]), lambda k: tile(projR, lows[k]), k0=half * KT, k_all=2 * KT)
                    if j == 3:
                        norm_sum(l * NORMS + 1, proj, MEM, CA_MEMN)
                pe.wait_ge(mem_low, l + 1)
                for name, js in (("memk", range(2)), ("memk", range(2, KT)), ("memv", range(KT))):
                    tiles_out(name, l, js, lambda k: tile(projR, CA_MEMH + k, 0, MEM), lambda k: tile(projR, CA_MEMN + k, 0, MEM), MEM)
                    if js == range(2):
                        norm_sum(l * NORMS + 2, hT)
                for n in (L0 + lin_of["memv"] + 6, L0 + lin_of["memv"] + 7):
                    pe.wait_ge(lin_free[n % 2], n // 2 + 1)
                for mt in range(2):
                    for k in range(KT):
                        ins = pe.transpose(bank(2 + 2 * mt + k // 4, k % 4 * P, P), tile(proj, CA_VT + k, mt * P, P), ident)
                ins.then_inc(v_turn, 1)
                pe.wait_ge(h_ready, (3 * l + 2) * KT)
                tiles_out("q", l, range(KT), h_high_part, h_low_part)
                for n in (L0 + lin_of["q"] + 6, L0 + lin_of["q"] + 7):
                    pe.wait_ge(lin_free[n % 2], n // 2 + 1)
                pe.wait_ge(v_turned, l + 1)

                def key_cache(b):
                    if b == 0:
                        pe.wait_ge(cs_q, l + 1)
                    s, before = r.block()
                    pe.wait_ge(landed[s], 16 * before + 16)
                    kc = slot(s)
                    for h in range(CAH):
                        for kk in range(2):
                            q0 = kk * 1024 + (h * NB + b) * CAH * NB
                            ins = pe.matmul(bank(5, 0, MEM, CAH * NB), csQ[:, q0:q0 + CAH * NB], kc[:, (2 * h + kk) * MEM:(2 * h + kk + 1) * MEM],
                                            start=(b, h, kk) == (0, 0, 0), stop=(b, h, kk) == (NB - 1, CAH - 1, 1))
                    ins.then_inc(cs_k, 1)

                for h in range(CAH):
                    n = l * CAH + h
                    if h:
                        pe.wait_ge(ca_oc, n)
                    for qt in range(2):
                        for kk in range(2):
                            ins = pe.matmul(bank(2, qt * MEM, MEM), tile(proj, CA_Q + 2 * h + kk, qt * P, P),
                                            tile(proj, CA_K + 2 * h + kk, 0, MEM), start=kk == 0, stop=kk == 1)
                    ins.then_inc(ca_scores, 1)
                    key_cache(h)
                    pe.wait_ge(ca_p, n + 1)
                    for mt in range(2):
                        for qt in range(2):
                            ins = pe.transpose(bank(3, mt * SEQ + qt * P, P), caP[:, qt * MEM + mt * P:qt * MEM + (mt + 1) * P], ident)
                    ins.then_inc(ca_pt, 1)
                    pe.wait_ge(ca_ptc, n + 1)
                    for dt in range(2):
                        for mt in range(2):
                            v0 = CA_V * NT + mt * D_MODEL + (2 * h + dt) * P
                            ins = pe.matmul(bank(4, dt * SEQ, SEQ), proj[:, v0:v0 + P], caPT[:, mt * SEQ:(mt + 1) * SEQ],
                                            start=mt == 0, stop=mt == 1)
                    ins.then_inc(ca_o, 1)
                for b in range(CAH, NB):
                    key_cache(b)
                pe.wait_ge(cs_p, l + 1)
                for mt in range(2):
                    ins = pe.transpose(bank(7, mt * 32, 32), csP[:, mt * P:(mt + 1) * P], ident[0:32, 0:32])
                ins.then_inc(cs_back, 1)
                pe.wait_ge(cs_backc, l + 1)
                pe.wait_ge(ca_oc, (l + 1) * CAH)
                for b in range(NB):
                    s, before = r.block()
                    pe.wait_ge(landed[s], 16 * before + 16)
                    vc = slot(s)
                    for h in range(CAH):
                        for mt in range(2):
                            p0 = ((mt * CAH + h) * NB + b) * NB
                            ins = pe.matmul(bank(2 + h, 0, 2 * P, NB), csPM[:, p0:p0 + NB], vc[:, mt * D_MODEL + 2 * h * P:mt * D_MODEL + (2 * h + 2) * P],
                                            start=(b, mt) == (0, 0), stop=(b, mt) == (NB - 1, 1))
                    ins.then_inc(cs_v, 1)
                pe.wait_ge(cs_o, l + 1)
                for d in range(KT):
                    ins = pe.transpose(bank(7, 64 + d * NB, NB), csO[:, d * P:(d + 1) * P], ident[0:NB, 0:NB])
                ins.then_inc(cs_turn, 1)
                pe.wait_ge(o_low, l + 1)
                tiles_out("o", l, range(KT), lambda k: tile(projR, CA_OH + k), lambda k: tile(projR, CA_O + k))
                norm_sum(l * NORMS + 3, hT)
                moe = l % 2 == 1
                if moe:
                    for tt, (lo, w) in enumerate(((0, P), (P, P), (SEQ, NB))):
                        for k in range(KT):
                            if tt == 0:
                                pe.wait_ge(h_full, (3 * l + 2) * KT + k + 1)
                            ins = pe.matmul(bank(7, tt * NE, NE, w), tile(tmp, k, lo, w), wrt[:, k * NE:(k + 1) * NE], start=k == 0, stop=k == KT - 1)
                    ins.then_inc(rt_logits, 1)
                    pe.wait_ge(rt_comb, 1)
                    for tt, (lo, w) in enumerate(((0, P), (P, P), (SEQ, NB))):
                        ins = pe.transpose(bank(7, 64 + lo, w, NE), lg[0:w, tt * NE:(tt + 1) * NE], ident[0:w, 0:w])
                    ins.then_inc(rt_turn, 1)
                    pe.wait_ge(rt_combT, 1)
                    pe.wait_ge(h_ready, (3 * l + 3) * KT)
                for n in (L0 + LIN - 2, L0 + LIN - 1):
                    pe.wait_ge(lin_free[n % 2], n // 2 + 1)

                def expert(i, ee):
                    def at(per, n):
                        return n if i is None else i * (2 * per) + n
                    gu0, dn0 = l * 2 * F_TILES + ee * F_TILES, l * 2 * KT + ee * KT
                    for f in range(F_TILES):
                        if f >= 2:
                            pe.wait_ge(gu_full, at(F_TILES, gu0 + f - 1))
                        for g in range(2):
                            product(bank(2 * g + f % 2, 0, NT), h_high_part, h_low_part,
                                    ready=(3 * l + 2) * KT if not moe and (ee, f, g) == (0, 0, 0) else 0)
                        if moe and f == 0:
                            pe.wait_ge(ex_mask, at(1, ee + 1))
                            pe.matmul(bank(6, 0, NT), ones[0:NE, :], combM, start=True, stop=True).then_inc(ex_bc, 1)
                    for j in range(KT):
                        if j >= 2:
                            pe.wait_ge(down_free, at(KT, dn0 + j - 1))
                        dst = bank(4 + j % 2, 0, NT)
                        if j == 0:
                            pe.wait_ge(gu_low, at(F_TILES, gu0 + KT))
                        product(dst, lambda k: tile(projR, FF_H + k), lambda k: tile(projR, FF_L + k), k_all=F_TILES)
                        if j == 0:
                            pe.wait_ge(gu_low, at(F_TILES, gu0 + F_TILES))
                        product(dst, lambda k: tile(projR, FF_H + k), lambda k: tile(projR, FF_L + k), F_TILES - KT, KT, F_TILES)

                rounds(pe, r, l, expert)
            norm_sum(DEPTH * NORMS, hT)

        @block.scalar
        def _(act):
            act.preload_act_table_set("natural_log_exp_and_others")
            st = Steps(act, act_step)
            act.wait_ge(dma_const, 64)
            act.wait_ge(dma_small, 96)
            eps = c(C_EPS, 1)

            r = Ring()

            def squares(src, sq, w=NT, s0=0, q0=0):
                for j in range(0, KT, SQ_TILES):
                    act.activation(tiles3(sq, q0 + j, SQ_TILES, 0, w), tiles3(src, s0 + j, SQ_TILES, 0, w), ACT.Square).then_inc(sq_ready, 1)

            def inverse_rms(k, w=NT):
                act.wait_ge(ss_ready, k + 1)
                st(act.activation(rstd[:, 0:w], bank(6, 0, w), ACT.Ln, bias=eps, scale=1.0 / D_MODEL))
                act.activation(rstd[:, 0:w], rstd[:, 0:w], ACT.Exp, scale=-0.5).then_inc(rs_ready, 1)

            def norm(k):
                squares(xT, hT)
                inverse_rms(k)

            def high(k, js=range(KT)):
                for j in js:
                    act.wait_ge(h_full, k * KT + j + 1)
                    act.activation(tile(hH, j), tile(tmp, j), ACT.Copy).then_inc(h_high, 1)

            def take(n, q, dst, src, ahead=True):
                if ahead:
                    split_high(act, r)
                act.wait_ge(piece_done, q + 1)
                act.activation(dst, src, ACT.Copy).then_inc(lin_free[n % 2], 1)

            for l in range(DEPTH):
                L0 = l * LIN
                Q0 = LAYER_PIECE[l]
                if l:
                    act.wait_ge(x_ready, 3 * l)
                squares(xT, hT)
                if l == 0:
                    for _ in range(AHEAD):
                        split_high(act, r)
                inverse_rms(l * NORMS)
                high(3 * l)
                n0 = L0 + lin_of["in"]
                for j in range(2 * SLOTS * PEEL):
                    take(n0 + j, Q0 + j, tile(proj, j), bank((n0 + j) % 2, 0, NT))
                    if j == 1:
                        act.wait_ge(gate_abs, l + 1)
                        act.activation(spu[:, :], spa[:, :], ACT.Exp, scale=-1.0).then_inc(gate_exp, 1)
                        act.activation(small[:, 0:1], alog[:, l:l + 1], ACT.Exp)
                    elif j == 3:
                        act.wait_ge(gate_one, l + 1)
                        act.activation(spl[:, :], spa[:, :], ACT.Ln).then_inc(gate_log, 1)
                    elif j == 2 * SLOTS * PEEL - 1:
                        act.wait_ge(gate_rows, l + 1)
                        act.activation(smR[:, :], smR[:, :], ACT.Exp)
                        act.activation(small[:, 8:16], lda[:, SEQ:NT], ACT.Exp).then_inc(gate_sexp, 1)
                r.begin(SLOTS)
                with act.Fori(PEEL, IN_ITERS) as i:
                    r.i = i - PEEL
                    for j in range(2 * SLOTS):
                        n = n0 + j
                        split_high(act, r)
                        act.wait_ge(piece_done, i * (2 * SLOTS) + (Q0 + j + 1))
                        act.activation(proj[:, bass.ds(i * (2 * SLOTS * NT) + j * NT, NT)], bank(n % 2, 0, NT), ACT.Copy).then_inc(lin_free[n % 2], 1)
                r.end(IN_ITERS - PEEL)
                for n in (n0 + N_PROJ - 2, n0 + N_PROJ - 1):
                    act.wait_ge(lin_free[n % 2], n // 2 + 1)
                act.activation(proj[:, K_ML * NT:V_ML * NT], proj[:, K_ML * NT:V_ML * NT], ACT.Copy, scale=P ** -0.5)
                act.activation(proj[:, K_R * NT:(K_R + RH) * NT], proj[:, K_R * NT:(K_R + RH) * NT], ACT.Copy, scale=P ** -0.5).then_inc(k_scaled, 1)
                act.preload_act_table_set("natural_log_exp_and_others")

                def post_squares(group):
                    y0, nt, _, _, s0, _ = group
                    act.activation(nrm[:, s0 * NT:(s0 + nt) * NT], proj[:, y0 * NT:(y0 + nt) * NT], ACT.Square).then_inc(post_sq, 1)

                act.wait_ge(gate_cols_in, l + 1)
                for h in range(NH):
                    n = l * NH + h
                    act.wait_ge(ml_gates, n + 1)
                    if h:
                        act.wait_ge(ml_weighted, n)
                    for q, (lo, hi) in enumerate(((0, P), (P, SEQ), (SEQ, 384))):
                        act.activation(mW[:, lo:hi], bank(3, lo, hi - lo), ACT.Exp, bias=gcol[:, 6 * q + h:6 * q + h + 1])
                    if h:
                        act.wait_ge(ml_h, n)
                    act.activation(mEM, bank(4, 0, SEQ), ACT.Exp)
                    act.wait_ge(ml_turned, n + 1)
                    act.activation(mVK, bank(5), ACT.Copy).then_inc(ml_w, 1)
                    if h == 0:
                        act.wait_ge(conv_acc, l + 1)
                        act.activation(conv[:, :], conv[:, :], ACT.Silu).then_inc(conv_done, 1)
                        for a, z in ((Z, Z + SP), (G_R, N_PROJ)):
                            act.activation(proj[:, a * NT:z * NT], proj[:, a * NT:z * NT], ACT.Silu)
                    elif h == 1:
                        act.activation(proj[:, O_ML * NT:Z * NT], proj[:, O_ML * NT:Z * NT], ACT.Sigmoid).then_inc(gates_done, 1)
                    if h < 2:
                        act.preload_act_table_set("natural_log_exp_and_others")
                    act.wait_ge(ml_num, n + 1)
                    act.activation(tile(proj, K_ML + h, 0, P), bank(7, 0, P), ACT.Copy)
                    act.activation(npr[:, h:h + 1], bank(7, P, 1), ACT.Copy).then_inc(ml_state, 1)
                for j in range(SP):
                    n = l * SP + j
                    if j % 3 == 0:
                        act.wait_ge(ssd_cb, 2 * l + j // 3 + 1)
                        act.activation(sBT, bank(3, 0, SEQ), ACT.Copy)
                    act.wait_ge(ssd_L, n + 1)
                    if j:
                        act.wait_ge(ssd_S, n)
                    for hh in range(2):
                        for q, (lo, hi) in enumerate(((0, P), (P, SEQ), (SEQ, 384))):
                            col = 18 + 12 * q + 2 * j + hh
                            ins = act.activation(sL[:, hh * 384 + lo:hh * 384 + hi], bank(6 + hh, lo, hi - lo), ACT.Exp, bias=gcol[:, col:col + 1])
                    act.wait_ge(ssd_turned, n + 1)
                    act.activation(sXT, bank(5, 0, SEQ), ACT.Copy).then_inc(ssd_w, 1)
                    if j == 0:
                        act.wait_ge(dec_y, l * UNITS + NH)
                        post_squares(POST[0])
                    act.wait_ge(ssd_y, n + 1)
                    act.activation(tile(proj, V_ML + j, 0, P), bank(5, SEQ, P), ACT.Copy).then_inc(ssd_state, 1)
                for h in range(RH):
                    n = l * RH + h
                    act.wait_ge(ret_scores, n + 1)
                    act.activation(mVK, bank(5), ACT.Copy).then_inc(ret_vk, 1)
                    act.wait_ge(ret_num, n + 1)
                    act.activation(tile(proj, Q_R + h, 0, SEQ), bank(6, 0, SEQ), ACT.Copy)
                    act.activation(tile(proj, K_R + h, 0, P), bank(7, 0, P), ACT.Copy).then_inc(ret_h, 1)
                act.wait_ge(dec_y, (l + 1) * UNITS)
                act.wait_ge(ret_h, (l + 1) * RH)
                post_squares(POST[1])
                post_squares(POST[2])
                for k, (_, nt, per, _, s0, b0) in enumerate(POST):
                    act.wait_ge(post_ss, 3 * l + k + 1)
                    for g in range(nt // per):
                        ins = act.activation(tile(nrm, s0 + g), bank(b0 + g, 0, NT), ACT.Ln, bias=eps, scale=1.0 / (per * P))
                    if k == 0:
                        ins.then_inc(post_ln, 1)
                        act.wait_ge(post_ln, l + 1)
                    else:
                        st(ins)
                    rs = nrm[:, s0 * NT:(s0 + nt // per) * NT]
                    act.activation(rs, rs, ACT.Exp, scale=-0.5).then_inc(post_rs, 1)
                act.wait_ge(dma_out, 16 * (OUTS * l + OUTS - 2))
                for k, (y0, nt, _, _, _, _) in enumerate(POST):
                    act.wait_ge(post_y, 3 * l + k + 1)
                    act.activation(projR[:, Y_HI[k] * NT:(Y_HI[k] + nt) * NT], proj[:, y0 * NT:(y0 + nt) * NT], ACT.Copy).then_inc(post_high, 1)
                for j in range(2 * KT):
                    split_high(act, r)
                    if j == 5:
                        act.wait_ge(mem_in, 16 * (l + 1))
                        squares(proj, proj, MEM, CA_MEM, CA_MEMN)
                    elif j == 9:
                        inverse_rms(l * NORMS + 1, MEM)
                    elif j == 14:
                        act.wait_ge(mem_full, l + 1)
                        act.activation(tiles3(projR, CA_MEMH, KT, 0, MEM), tiles3(proj, CA_MEMN, KT, 0, MEM), ACT.Copy).then_inc(mem_high, 1)
                act.wait_ge(x_ready, 3 * l + 1)
                squares(xT, hT)
                for name, at in (("memk", CA_K), ("memv", CA_VT)):
                    for j in range(KT):
                        n = L0 + lin_of[name] + j
                        take(n, Q0 + piece_of[name] + j, tile(proj, at + j, 0, MEM), bank(n % 2, 0, MEM))
                        if name == "memk" and j == 2:
                            inverse_rms(l * NORMS + 2)
                        if name == "memk" and j >= 4:
                            high(3 * l + 1, range(2 * (j - 4), 2 * (j - 3)))
                act.wait_ge(v_turn, l + 1)
                for mt in range(2):
                    v0 = CA_V * NT + mt * D_MODEL
                    ins = act.activation(proj[:, v0:v0 + D_MODEL], ps[:, (2 + 2 * mt) * 512:(4 + 2 * mt) * 512], ACT.Copy)
                ins.then_inc(v_turned, 1)
                for j in range(KT):
                    n = L0 + lin_of["q"] + j
                    take(n, Q0 + piece_of["q"] + j, tile(proj, CA_Q + j), bank(n % 2, 0, NT), j < KT - AHEAD)
                for h in range(CAH):
                    n = l * CAH + h
                    act.wait_ge(ca_max, n + 1)
                    for qt in range(2):
                        ins = act.activation(caP[:, qt * MEM:(qt + 1) * MEM], bank(2, qt * MEM, MEM), ACT.Exp, bias=sml[:, qt:qt + 1],
                                             scale=1.0 / 16, accum_out=sml[:, 2 + qt:3 + qt])
                    ins.then_inc(ca_exp, 1)
                    act.wait_ge(ca_pt, n + 1)
                    act.activation(caPT, bank(3), ACT.Copy).then_inc(ca_ptc, 1)
                    act.wait_ge(ca_o, n + 1)
                    act.activation(tiles3(proj, CA_O + 2 * h, 2, 0, SEQ), bank(4).rearrange("p (a t) -> p a t", a=2), ACT.Copy).then_inc(ca_oc, 1)
                act.wait_ge(cs_max, l + 1)
                act.activation(csP, bank(5, 0, MEM, 32), ACT.Exp, bias=sml[0:32, 8:9], scale=1.0 / 16, accum_out=sml[0:32, 9:10]).then_inc(cs_exp, 1)
                act.wait_ge(cs_back, l + 1)
                act.wait_ge(cs_zero, 2 * (l + 1))
                act.activation(csPM.rearrange("p (a c) -> p a c", a=2 * CAH)[:, :, 0:NB * NB:NB + 1],
                               bank(7, 0, 64).rearrange("p (a b) -> p a b", a=2 * CAH), ACT.Copy).then_inc(cs_backc, 1)
                for _ in range(AHEAD):
                    split_high(act, r)
                act.wait_ge(cs_v, (l + 1) * NB)
                act.activation(csO.rearrange("p (h d) -> p h d", h=CAH), bank(2, 0, CAH * 512, NB).rearrange("p (h d) -> p h d", h=CAH)[:, :, 0:2 * P],
                               ACT.Copy).then_inc(cs_o, 1)
                act.wait_ge(cs_turn, l + 1)
                act.activation(tiles3(proj, CA_O, KT, SEQ, NB), bank(7, 64, 64).rearrange("p (a t) -> p a t", a=KT), ACT.Copy).then_inc(cs_oc, 1)
                act.wait_ge(cs_oc, l + 1)
                act.wait_ge(ca_oc, (l + 1) * CAH)
                act.activation(projR[:, CA_OH * NT:(CA_OH + KT) * NT], proj[:, CA_O * NT:(CA_O + KT) * NT], ACT.Copy).then_inc(o_high, 1)
                for j in range(KT):
                    split_high(act, r)
                act.wait_ge(x_ready, 3 * l + 2)
                norm(l * NORMS + 3)
                high(3 * l + 2)
                if l % 2 == 1:
                    act.wait_ge(rt_max, 1)
                    act.activation(conv[:, 24:48], conv[:, 24:48], ACT.Exp).then_inc(rt_exp, 1)
                act.wait_ge(dma_out, 16 * OUTS * (l + 1))

                def expert(i, ee):
                    def at(per, n):
                        return n if i is None else i * (2 * per) + n
                    gu0 = l * 2 * F_TILES + ee * F_TILES
                    q0 = Q0 + piece_of["ffn"] + ee * (PAIR_PIECES // 2)
                    for f in range(F_TILES):
                        split_high(act, r)
                        split_high(act, r)
                        if f >= 2:
                            act.wait_ge(gu_full, at(F_TILES, gu0 + f - 1))
                        act.wait_ge(piece_done, at(PAIR_PIECES // 2, q0 + 2 * f + 2))
                        act.activation(sig[f % 2], bank(f % 2, 0, NT), ACT.Silu).then_inc(gu_silu, 1)
                        act.wait_ge(gu_full, at(F_TILES, gu0 + f + 1))
                        act.activation(tile(projR, FF_H + f), full[f % 2], ACT.Copy).then_inc(gu_high, 1)
                    for j in range(KT):
                        for _ in range(2):
                            split_high(act, r)

                rounds(act, r, l, expert)
                act.preload_act_table_set("natural_log_exp_and_others")
            act.wait_ge(x_ready, 3 * DEPTH)
            norm(DEPTH * NORMS)

        @block.vector
        def _(dve):
            st = Steps(dve, dve_step)
            st(dve.memset(spx[:, :], 0.0))
            dve.wait_ge(dma_const, 64)
            dve.wait_ge(dma_small, 96)

            r = Ring()

            def scale(k, src, dst, gain, w=NT, s0=0, d0=0):
                dve.wait_ge(rs_ready, k + 1)
                for j in range(KT):
                    yield dve.scalar_tensor_tensor(out=tile(dst, d0 + j, 0, w), in0=tile(src, s0 + j, 0, w), scalar=gain(j),
                                                   in1=rstd[:, 0:w], op0=ALU.mult, op1=ALU.mult)

            def low(k_h, js=range(KT)):
                for j in js:
                    dve.wait_ge(h_high, k_h * KT + j + 1)
                    dve.tensor_tensor(tile(hL, j), tile(tmp, j), f32(tile(hH, j)), ALU.subtract).then_inc(h_ready, 1)

            def norm(k, gain, k_h=None):
                for j, ins in enumerate(scale(k, xT, tmp, gain)):
                    ins.then_inc(h_full, 1)
                    if k_h is not None and j:
                        low(k_h, [j - 1])
                if k_h is not None:
                    low(k_h, [KT - 1])

            def add_to_x(n, q, j, pieces):
                for _ in range(pieces):
                    split_low(dve, r)
                dve.wait_ge(piece_done, q + 1)
                dve.tensor_tensor(tile(xT, j), bank(n % 2, 0, NT), tile(xT, j), ALU.add).then_inc(lin_free[n % 2], 1)
                if j == KT - 1:
                    for k in (n - 1, n):
                        dve.wait_ge(lin_free[k % 2], k // 2 + 1)
                    dve.sem_inc(x_ready, 1)

            for _ in range(AHEAD):
                split_low(dve, r)
            for l in range(DEPTH):
                L0 = l * LIN
                Q0 = LAYER_PIECE[l]
                norm(l * NORMS, lambda j: pcol(l, G_MIX + j), 3 * l)

                def gates():
                    n = L0 + lin_of["gates"]
                    dve.wait_ge(gate_sum, l + 1)
                    b = n % 2
                    dve.tensor_scalar(gI[:, :], bank(b, 0, NT, 6), hpar[0:6, 3 * l:3 * l + 1], None, ALU.add)
                    yield
                    dve.tensor_scalar(spx[0:6, 0:NT], bank(b, 0, NT, 6, 32), hpar[32:38, 3 * l:3 * l + 1], -1.0, ALU.add, ALU.mult)
                    yield
                    dve.tensor_scalar(spx[:, NT:2 * NT], bank(b, 0, NT, 12, 64), hpar[64:76, 3 * l:3 * l + 1], None, ALU.add).then_inc(lin_free[b], 1)
                    yield
                    dve.wait_ge(lin_free[b], n // 2 + 1)
                    dve.scalar_tensor_tensor(out=spa[:, :], in0=spx[:, :], scalar=-1.0, in1=spx[:, :], op0=ALU.mult, op1=ALU.max).then_inc(gate_abs, 1)
                    yield
                    dve.wait_ge(gate_exp, l + 1)
                    st(dve.tensor_scalar(spd[:, :], spu[:, :], 1.0, -1.0, ALU.add, ALU.add))
                    yield
                    dve.tensor_scalar(spa[:, :], spu[:, :], 1.0, None, ALU.add).then_inc(gate_one, 1)
                    yield
                    dve.wait_ge(gate_log, l + 1)
                    st(dve.tensor_scalar(spa[:, :], spd[:, :], 0.0, None, ALU.is_equal))
                    yield
                    st(dve.tensor_tensor(spd[:, :], spd[:, :], spa[:, :], ALU.add))
                    yield
                    st(dve.tensor_tensor(spl[:, :], spl[:, :], spa[:, :], ALU.add))
                    yield
                    st(dve.reciprocal(spd[:, :], spd[:, :]))
                    yield
                    st(dve.tensor_tensor(spl[:, :], spl[:, :], spd[:, :], ALU.mult))
                    yield
                    st(dve.tensor_tensor(spl[:, :], spl[:, :], spu[:, :], ALU.mult))
                    yield
                    st(dve.scalar_tensor_tensor(out=spx[:, :], in0=spx[:, :], scalar=0.0, in1=spl[:, :], op0=ALU.max, op1=ALU.add))
                    yield
                    on = const[0:12, C_ONES:C_ONES + P]
                    for ch in range(2):
                        a, z = ch * P, (ch + 1) * P
                        st(dve.tensor_tensor_scan(cum_f[:, a:z], on[0:6, :], spx[0:6, a:z], 0.0, ALU.mult, ALU.subtract))
                        yield
                    g0, g1 = grow[:, 0:P], grow[:, SEQ:384]
                    st(dve.tensor_tensor(g0, gI[:, 0:P], cum_f[:, 0:P], ALU.subtract))
                    yield
                    st(dve.tensor_tensor(g1, gI[:, P:SEQ], cum_f[:, P:SEQ], ALU.subtract))
                    yield
                    st(dve.tensor_tensor_scan(run_max[:, 0:P], g0, g0, 0.0, ALU.max, ALU.max))
                    yield
                    st(dve.tensor_tensor(small[0:6, 1:2], cum_f[:, P - 1:P], run_max[:, P - 1:P], ALU.add))
                    yield
                    st(dve.tensor_tensor_scan(run_max[:, P:SEQ], g1, g1, small[0:6, 1:2], ALU.max, ALU.max))
                    yield
                    st(dve.tensor_scalar(negM[:, :], run_max[:, :], -1.0, None, ALU.mult))
                    yield
                    st(dve.scalar_tensor_tensor(out=negm[:, :], in0=cum_f[:, :], scalar=-1.0, in1=run_max[:, :], op0=ALU.mult, op1=ALU.subtract))
                    yield
                    st(dve.tensor_scalar(grow[:, P:SEQ], g0, cum_f[:, P - 1:P], None, ALU.add))
                    yield
                    st(dve.tensor_scalar(small[0:6, 2:3], negm[:, SEQ - 1:SEQ], -1.0, None, ALU.mult))
                    yield
                    st(dve.tensor_tensor(small[0:6, 16:24], m0[:, l * NB:(l + 1) * NB], spx[0:6, SEQ:NT], ALU.subtract))
                    yield
                    st(dve.tensor_tensor(small[0:6, 24:32], small[0:6, 16:24], gI[:, SEQ:NT], ALU.max))
                    yield
                    st(dve.tensor_tensor(smR[:, 0:8], gI[:, SEQ:NT], small[0:6, 24:32], ALU.subtract))
                    yield
                    st(dve.tensor_tensor(smR[:, 8:16], small[0:6, 16:24], small[0:6, 24:32], ALU.subtract))
                    yield
                    st(dve.tensor_scalar(smR[:, 16:24], small[0:6, 24:32], -1.0, None, ALU.mult))
                    yield
                    st(dve.tensor_scalar(lda[:, :], spx[:, NT:2 * NT], small[:, 0:1], -1.0, ALU.mult, ALU.mult))
                    yield
                    for ch in range(2):
                        a, z = ch * P, (ch + 1) * P
                        st(dve.tensor_tensor_scan(cum_a[:, a:z], on, lda[:, a:z], 0.0, ALU.mult, ALU.add))
                        yield
                        st(dve.tensor_scalar(arow[:, 2 * a:2 * a + P], cum_a[:, a:z], -1.0, None, ALU.mult))
                        yield
                    dve.tensor_scalar(arow[:, P:SEQ], arow[:, 0:P], cum_a[:, P - 1:P], None, ALU.add).then_inc(gate_rows, 1)
                    yield

                steps = gates()
                for j in range(2 * SLOTS * PEEL):
                    split_low(dve, r)
                    for _ in range(3):
                        next(steps, None)
                r.begin(SLOTS)
                with dve.Fori(PEEL, IN_ITERS) as i:
                    r.i = i - PEEL
                    for j in range(2 * SLOTS):
                        split_low(dve, r)
                r.end(IN_ITERS - PEEL)
                if l == 0:
                    dve.wait_ge(dma_tables, 16)
                dve.wait_ge(gate_sexp, l + 1)
                dve.tensor_tensor(mldiag.rearrange("p (h c) -> p h c", h=NH), smR[:, :].unsqueeze(1).to_broadcast([NH, NH, 24]),
                                  ident[0:NH, 0:NH].unsqueeze(2).to_broadcast([NH, NH, 24]), ALU.mult)
                dve.tensor_tensor(ssdiag.rearrange("p (j b) -> p j b", j=SP), small[:, 8:16].unsqueeze(1).to_broadcast([SH, SP, NB]),
                                  const[0:SH, C_PAIR:C_PAIR + SP].unsqueeze(2).to_broadcast([SH, SP, NB]), ALU.mult).then_inc(gate_diag, 1)

                def rotate(h):
                    for jj, i in enumerate((Q_R, K_R)):
                        n = 2 * (l * RH + h) + jj
                        b = ((6, 7), (3, 4))[h > 0][jj]
                        dve.wait_ge(rot_ready, n + 1)
                        dve.tensor_tensor(tile(tmp, jj), bank(b, 0, NT), c(C_SIN, NT), ALU.mult).then_inc(rot_used, 1)
                        st(dve.tensor_tensor(tile(proj, i + h), tile(proj, i + h), c(C_COS, NT), ALU.mult))
                        dve.wait_ge(rot_used, n + 1)
                        st(dve.tensor_tensor(tile(proj, i + h), tile(proj, i + h), tile(tmp, jj), ALU.add))
                    dve.sem_inc(rot_done, 1)

                dve.wait_ge(gate_cols, l + 1)
                dve.tensor_copy(gcol[:, :], bank(2, 0, 54)).then_inc(gate_cols_in, 1)
                dve.wait_ge(gate_bc, l + 1)
                dve.tensor_copy(gbc[:, :], bank(3, 0, 192)).then_inc(gate_bc_in, 1)
                dve.wait_ge(gate_bc_in, l + 1)
                gb = gbc[:, 0:144].rearrange("p (h q b) -> p h q b", h=NH, q=3)
                dve.wait_ge(k_scaled, l + 1)

                def r3(buf, n=6):
                    return buf.rearrange("p (h b) -> p h b", h=n)

                nn, vv = r3(nnew[:, :]), r3(vA[:, :])
                st(dve.tensor_tensor(nn, r3(nst[:, l * 48:(l + 1) * 48]), gb[:, :, 1, :], ALU.mult))
                st(dve.tensor_tensor(r3(yT2[:, :]), tiles3(proj, K_ML, NH, SEQ, NB), gb[:, :, 0, :], ALU.mult))
                st(dve.tensor_tensor(nn, nn, r3(yT2[:, :]), ALU.add))
                st(dve.tensor_tensor(vv, tiles3(proj, V_ML, NH, SEQ, NB), gb[:, :, 0, :], ALU.mult))
                dve.tensor_tensor(r3(yT2[:, :]), nn, tiles3(proj, Q_ML, NH, SEQ, NB), ALU.mult).then_inc(nq_ready, 1)
                dve.wait_ge(nden_ready, l + 1)
                st(dve.scalar_tensor_tensor(out=r3(rden[:, :]), in0=r3(bank(6, 0, 48)), scalar=-1.0, in1=gb[:, :, 2, :], op0=ALU.mult, op1=ALU.max))
                st(dve.tensor_tensor(rden[:, :], bank(6, 0, 48), rden[:, :], ALU.max))
                dve.reciprocal(rden[:, :], rden[:, :]).then_inc(nden_done, 1)
                def unit_half(u, half):
                    n = l * UNITS + u
                    S = state(u)[:, half * 512:(half + 1) * 512]
                    if u < NH:
                        a = vA[:, u * NB:(u + 1) * NB]
                    elif u < NH + SP:
                        a = xds[:, (u - NH) * NB:(u - NH + 1) * NB]
                    else:
                        a = tile(proj, V_R + u - NH - SP, SEQ, NB)
                    dve.wait_ge(dec_decay, n + 1)
                    dve.wait_ge(dec_bc, 2 * n + half + 1)
                    for b in range(NB // 2):
                        at = half * (NB // 2) + b
                        ins = dve.scalar_tensor_tensor(out=S[:, b * P:(b + 1) * P], in0=bank(0, b * P, P), scalar=a[:, at:at + 1],
                                                       in1=S[:, b * P:(b + 1) * P], op0=ALU.mult, op1=ALU.add)
                    ins.then_inc(dec_S, 1)
                    dve.wait_ge(dec_S, 2 * n + half + 1)
                    dve.tensor_tensor(dP, S, bank(1), ALU.mult).then_inc(dec_read, 1)
                    dve.wait_ge(dec_read, 2 * n + half + 1)
                    st(dve.tensor_reduce(yT[:, half * (NB // 2):(half + 1) * (NB // 2)], dP.rearrange("p (b f) -> p b f", b=NB // 2), AX.X, ALU.add))
                    if half == 0:
                        return
                    if u < NH:
                        ins = dve.tensor_tensor(tile(proj, Q_ML + u, SEQ, NB), yT[:, :], rden[:, u * NB:(u + 1) * NB], ALU.mult)
                    elif u < NH + SP:
                        j = u - NH
                        st(dve.scalar_tensor_tensor(out=yT[:, :], in0=tile(conv, j, SEQ, NB), scalar=pcol(l, D_SKIP + j), in1=yT[:, :], op0=ALU.mult, op1=ALU.add))
                        ins = dve.tensor_tensor(tile(proj, Z + j, SEQ, NB), tile(proj, Z + j, SEQ, NB), yT[:, :], ALU.mult)
                    else:
                        ins = dve.tensor_copy(tile(proj, Q_R + u - NH - SP, SEQ, NB), yT[:, :])
                    ins.then_inc(dec_y, 1)
                    dve.wait_ge(dec_y, n + 1)

                for h in range(NH):
                    n = l * NH + h
                    dve.wait_ge(ml_w, n + 1)
                    dve.wait_ge(ml_scores, n + 1)
                    dve.tensor_tensor(mS, mW, bank(2, 0, 384), ALU.mult)
                    dve.tensor_scalar(mKW[:, 0:P], mVK[:, SEQ:384], mW[:, SEQ - 1:SEQ], None, ALU.mult)
                    dve.tensor_scalar(mKW[:, P:SEQ], mVK[:, 384:512], mW[:, 383:384], None, ALU.mult).then_inc(ml_weighted, 1)
                    unit_half(h, 0)
                    dve.wait_ge(ml_num, n + 1)
                    st(dve.scalar_tensor_tensor(out=mDN, in0=bank(6, SEQ, SEQ), scalar=-1.0, in1=mEM, op0=ALU.mult, op1=ALU.max))
                    st(dve.tensor_tensor(mDN, bank(6, SEQ, SEQ), mDN, ALU.max))
                    st(dve.reciprocal(mDN, mDN))
                    dve.tensor_tensor(tile(proj, Q_ML + h, 0, SEQ), bank(6, 0, SEQ), mDN, ALU.mult).then_inc(ml_h, 1)
                    unit_half(h, 1)
                dve.wait_ge(ml_h, (l + 1) * NH)
                dve.wait_ge(conv_done, l + 1)
                dve.wait_ge(gates_done, l + 1)
                for j in range(SP):
                    n, g = l * SP + j, j // 3
                    dve.wait_ge(ssd_dt, n + 1)
                    dve.tensor_tensor(sXD, tile(conv, j), bank(4, 0, NT), ALU.mult).then_inc(ssd_xdt, 1)
                    dve.wait_ge(ssd_xdt, n + 1)
                    st(dve.tensor_copy(xds[:, j * NB:(j + 1) * NB], sXD[:, SEQ:NT]))
                    dve.wait_ge(ssd_w, n + 1)
                    for hh in range(2):
                        dve.tensor_tensor(sS[:, hh * 384:(hh + 1) * 384], sL[:, hh * 384:(hh + 1) * 384], bank(2, 0, 384), ALU.mult)
                        for s_, at in ((0, SEQ - 1), (1, 383)):
                            ins = dve.tensor_scalar(sXW[:, s_ * P + 64 * hh:s_ * P + 64 * hh + 64], sXT[:, s_ * P + 64 * hh:s_ * P + 64 * hh + 64],
                                                    sL[:, hh * 384 + at:hh * 384 + at + 1], None, ALU.mult)
                    ins.then_inc(ssd_S, 1)
                    unit_half(NH + j, 0)
                    dve.wait_ge(ssd_y, n + 1)
                    st(dve.scalar_tensor_tensor(out=sY, in0=tile(conv, j, 0, SEQ), scalar=pcol(l, D_SKIP + j), in1=bank(4, 0, SEQ), op0=ALU.mult, op1=ALU.add))
                    dve.tensor_tensor(tile(proj, Z + j, 0, SEQ), tile(proj, Z + j, 0, SEQ), sY, ALU.mult).then_inc(ssd_h, 1)
                    if j == SP - 1:
                        rotate(0)
                    unit_half(NH + j, 1)
                for h in range(RH):
                    n = l * RH + h
                    dve.wait_ge(ret_scores, n + 1)
                    if h == 0:
                        dve.wait_ge(ssd_state, (l + 1) * SP)
                    w0 = C_RET + h * 384
                    dve.tensor_tensor(mS, bank(2, 0, 384), c(w0, 384), ALU.mult)
                    dve.wait_ge(ret_vk, n + 1)
                    dve.tensor_scalar(mKW[:, 0:P], mVK[:, SEQ:384], c(w0 + SEQ - 1, 1), None, ALU.mult)
                    dve.tensor_scalar(mKW[:, P:SEQ], mVK[:, 384:512], c(w0 + 383, 1), None, ALU.mult).then_inc(ret_weighted, 1)
                    unit_half(NH + SP + h, 0)
                    if h + 1 < RH:
                        rotate(h + 1)
                    unit_half(NH + SP + h, 1)
                dve.wait_ge(ret_h, (l + 1) * RH)
                def post_low_parts(k):
                    y0, nt = POST[k][0:2]
                    dve.wait_ge(post_high, 3 * l + k + 1)
                    a, z = y0 * NT, (y0 + nt) * NT
                    dve.tensor_tensor(projR[:, a:z], proj[:, a:z], f32(projR[:, Y_HI[k] * NT:(Y_HI[k] + nt) * NT]), ALU.subtract).then_inc(post_low, 1)

                for k, (y0, nt, per, gain, s0, _) in enumerate(POST):
                    dve.wait_ge(post_rs, 3 * l + k + 1)
                    if k != 1:
                        dve.wait_ge(post_gated, 2 * l + (k + 2) // 2)
                    for j in range(nt):
                        ins = dve.scalar_tensor_tensor(out=tile(proj, y0 + j), in0=tile(proj, y0 + j), scalar=pcol(l, gain + j),
                                                       in1=tile(nrm, s0 + j // per), op0=ALU.mult, op1=ALU.mult)
                    ins.then_inc(post_y, 1)
                    if k == 1:
                        post_low_parts(0)
                        post_low_parts(1)
                post_low_parts(2)
                for j in range(KT):
                    add_to_x(L0 + lin_of["out"] + j, Q0 + piece_of["out"] + 2 * j + 1, j, 2)
                    if j == 5:
                        for ins in scale(l * NORMS + 1, proj, proj, lambda j: pcol(l, G_MEM + j), MEM, CA_MEM, CA_MEMN):
                            last = ins
                        last.then_inc(mem_full, 1)
                dve.wait_ge(mem_high, l + 1)
                dve.tensor_tensor(tiles3(projR, CA_MEMN, KT, 0, MEM), tiles3(proj, CA_MEMN, KT, 0, MEM),
                                  f32(tiles3(projR, CA_MEMH, KT, 0, MEM)), ALU.subtract).then_inc(mem_low, 1)
                for j in range(2 * KT):
                    split_low(dve, r)
                    if j == 3:
                        norm(l * NORMS + 2, lambda j: pcol(l, G_CA + j))
                    if 6 <= j < 10:
                        low(3 * l + 1, range(2 * (j - 6), 2 * (j - 5)))
                for j in range(KT - AHEAD):
                    split_low(dve, r)
                for h in range(CAH):
                    n = l * CAH + h
                    dve.wait_ge(ca_scores, n + 1)
                    st(dve.tensor_reduce(sml[:, 4:6], bank(2).rearrange("p (a m) -> p a m", a=2), AX.X, ALU.max))
                    dve.tensor_scalar(sml[:, 0:2], sml[:, 4:6], -1.0 / 16, None, ALU.mult).then_inc(ca_max, 1)
                    dve.wait_ge(ca_exp, n + 1)
                    st(dve.reciprocal(sml[:, 6:8], sml[:, 2:4]))
                    for qt in range(2):
                        ins = dve.tensor_scalar(caP[:, qt * MEM:(qt + 1) * MEM], caP[:, qt * MEM:(qt + 1) * MEM], sml[:, 6 + qt:7 + qt], None, ALU.mult)
                    ins.then_inc(ca_p, 1)
                dve.wait_ge(cs_k, (l + 1) * NB)
                st(dve.tensor_reduce(sml[0:32, 10:11], bank(5, 0, MEM, 32), AX.X, ALU.max))
                dve.tensor_scalar(sml[0:32, 8:9], sml[0:32, 10:11], -1.0 / 16, None, ALU.mult).then_inc(cs_max, 1)
                dve.wait_ge(cs_exp, l + 1)
                st(dve.reciprocal(sml[0:32, 11:12], sml[0:32, 9:10]))
                dve.tensor_scalar(csP, csP, sml[0:32, 11:12], None, ALU.mult).then_inc(cs_p, 1)
                for _ in range(AHEAD):
                    split_low(dve, r)
                dve.wait_ge(o_high, l + 1)
                a, z = CA_O * NT, (CA_O + KT) * NT
                dve.tensor_tensor(projR[:, a:z], proj[:, a:z], f32(projR[:, CA_OH * NT:(CA_OH + KT) * NT]), ALU.subtract).then_inc(o_low, 1)
                for j in range(KT):
                    add_to_x(L0 + lin_of["o"] + j, Q0 + piece_of["o"] + j, j, 1)
                norm(l * NORMS + 3, lambda j: pcol(l, G_FFN + j), 3 * l + 2)
                moe = l % 2 == 1
                if moe:
                    T3 = 3 * NE
                    st(dve.memset(conv[:, 0:T3], 0.0))
                    dve.wait_ge(rt_logits, 1)
                    dve.tensor_copy(conv[:, 0:2 * NE], bank(7, 0, 2 * NE))
                    st(dve.tensor_copy(conv[0:NB, 2 * NE:T3], bank(7, 2 * NE, NE, NB)))
                    l3 = conv[:, 0:T3].rearrange("p (t e) -> p t e", t=3)
                    x3 = conv[:, 24:48].rearrange("p (t e) -> p t e", t=3)
                    st(dve.tensor_reduce(conv[:, 48:51], l3, AX.X, ALU.max))
                    dve.tensor_tensor(x3, l3, conv[:, 48:51].unsqueeze(2).to_broadcast([P, 3, NE]), ALU.subtract).then_inc(rt_max, 1)
                    gt, eq = conv[:, 64:64 + 192], conv[:, 256:256 + 192]
                    shape = [P, 3, NE, NE]
                    tie = c(C_TIE, 64).rearrange("p (e j) -> p e j", e=NE).unsqueeze(1).to_broadcast(shape)
                    other, own = l3.unsqueeze(2).to_broadcast(shape), l3.unsqueeze(3).to_broadcast(shape)
                    g_, e_ = (x.rearrange("p (t e j) -> p t e j", t=3, e=NE) for x in (gt, eq))
                    dve.tensor_tensor(g_, other, own, ALU.is_gt)
                    st(dve.tensor_tensor(e_, other, own, ALU.is_equal))
                    st(dve.tensor_tensor(e_, e_, tie, ALU.mult))
                    st(dve.tensor_tensor(g_, g_, e_, ALU.add))
                    st(dve.tensor_reduce(conv[:, 512:536], gt.rearrange("p (t j) -> p t j", j=NE), AX.X, ALU.add))
                    st(dve.tensor_scalar(conv[:, 512:536], conv[:, 512:536], TOP_K - 0.5, None, ALU.is_lt))
                    dve.wait_ge(rt_exp, 1)
                    st(dve.tensor_tensor(conv[:, 512:536], conv[:, 512:536], conv[:, 24:48], ALU.mult))
                    w3 = conv[:, 512:536].rearrange("p (t e) -> p t e", t=3)
                    st(dve.tensor_reduce(conv[:, 48:51], w3, AX.X, ALU.add))
                    st(dve.reciprocal(conv[:, 48:51], conv[:, 48:51]))
                    dve.tensor_tensor(l3, w3, conv[:, 48:51].unsqueeze(2).to_broadcast([P, 3, NE]), ALU.mult).then_inc(rt_comb, 1)
                    dve.wait_ge(rt_turn, 1)
                    dve.tensor_copy(combT, bank(7, 64, NT, NE)).then_inc(rt_combT, 1)
                    dve.wait_ge(rt_combT, 1)
                dve.wait_ge(dma_out, 16 * OUTS * (l + 1))

                def expert(i, ee):
                    def at(per, n):
                        return n if i is None else i * (2 * per) + n
                    gu0, q0 = l * 2 * F_TILES + ee * F_TILES, Q0 + piece_of["ffn"] + ee * (PAIR_PIECES // 2)
                    if moe:
                        dve.tensor_scalar(combM, combT, const[0:NE, bass.ds(i * 2 + (C_ID + ee), 1)], None, ALU.mult).then_inc(ex_mask, 1)
                    for f in range(F_TILES):
                        split_low(dve, r)
                        split_low(dve, r)
                        if moe and f == 0:
                            dve.wait_ge(ex_bc, at(1, ee + 1))
                            st(dve.tensor_copy(combB, bank(6, 0, NT)))
                        dve.wait_ge(gu_silu, at(F_TILES, gu0 + f + 1))
                        sg = sig[f % 2]
                        if moe:
                            st(dve.tensor_tensor(sg, sg, combB, ALU.mult))
                        dve.tensor_tensor(full[f % 2], sg, bank(2 + f % 2, 0, NT), ALU.mult).then_inc(gu_full, 1)
                        dve.wait_ge(gu_high, at(F_TILES, gu0 + f + 1))
                        dve.tensor_tensor(tile(projR, FF_L + f), full[f % 2], f32(tile(projR, FF_H + f)), ALU.subtract).then_inc(gu_low, 1)
                    for j in range(KT):
                        for _ in range(2):
                            split_low(dve, r)
                        dve.wait_ge(piece_done, at(PAIR_PIECES // 2, q0 + 2 * F_TILES + 2 * j + 2))
                        dve.tensor_tensor(tile(xT, j), tile(xT, j), bank(4 + j % 2, 0, NT), ALU.add).then_inc(down_free, 1)

                rounds(dve, r, l, expert, st, 2 * (F_TILES + 1))
                dve.wait_ge(down_free, (2 * KT, 2 * KT + NE * KT)[l])
                dve.sem_inc(x_ready, 1)
            norm(DEPTH * NORMS, lambda j: par[:, DEPTH * N_PAR + j:DEPTH * N_PAR + j + 1])

        @block.gpsimd
        def _(pool):
            pool.wait_ge(dma_const, 64)
            pool.wait_ge(dma_small, 96)
            st = Steps(pool, pool_step)

            def load_state(l, u):
                pool.dma_start(state(u), t["states"][l, u]).then_inc(state_in[u % STATE_SLOTS], 16)

            for l in range(DEPTH):
                for u in range(STATE_SLOTS):
                    if l:
                        pool.wait_ge(state_out[u], 16 * (state_count(l, u) - 1))
                        pool.wait_ge(dec_read, 2 * l * UNITS)
                    load_state(l, u)
                pool.wait_ge(gate_rows, l + 1)
                for k in range(CONV_T):
                    u, y = tile(proj, XBC + k), tile(conv, k)
                    n = l * LIN + lin_of["in"] + XBC + k
                    pool.wait_ge(lin_free[n % 2], n // 2 + 1)

                    def tap(i):
                        return pcol(l, CONV_K + 4 * k + i)
                    st(pool.tensor_scalar(y, u, tap(3), pcol(l, CONV_B + k), ALU.mult, ALU.add))
                    for d in range(1, 4):
                        w = cst[:, ((l * CONV_T + k) * 3 + 3 - d) * NB:((l * CONV_T + k) * 3 + 4 - d) * NB]
                        pool.tensor_scalar(tapped[:, d:SEQ], u[:, 0:SEQ - d], tap(3 - d), None, ALU.mult)
                        st(pool.tensor_scalar(tapped[:, SEQ:NT], w, tap(3 - d), None, ALU.mult))
                        st(pool.tensor_tensor(y[:, d:NT], y[:, d:NT], tapped[:, d:NT], ALU.add))
                st(pool.tensor_copy(cvp[:, :].rearrange("p (c i) -> p c i", i=3), tiles3(proj, XBC, CONV_T, SEQ - 3, 3)))
                old = cst[:, l * CONV_T * 24:(l + 1) * CONV_T * 24].rearrange("p (c i b) -> p c i b", c=CONV_T, i=3)
                for i in range(2):
                    st(pool.tensor_copy(old[:, :, i, :], old[:, :, i + 1, :]))
                st(pool.tensor_copy(old[:, :, 2, :], tiles3(proj, XBC, CONV_T, SEQ, NB)))
                pool.sem_inc(conv_acc, 1)
                pool.wait_ge(gate_rows, l + 1)
                pool.dma_start(t["o_mp"][l], small[0:6, 2:3]).then_inc(dma_out, 16)
                pool.dma_start(t["o_ms"][l], small[0:6, 24:32]).then_inc(dma_out, 16)
                pool.wait_ge(conv_acc, l + 1)
                pool.dma_start(t["o_cvp"][l], cvp[:, :]).then_inc(dma_out, 16)
                pool.dma_start(t["o_cvs"][l], cst[:, l * CONV_T * 24:(l + 1) * CONV_T * 24]).then_inc(dma_out, 16)
                pool.wait_ge(nden_done, l + 1)
                pool.dma_start(t["o_ns"][l], nnew[:, :]).then_inc(dma_out, 16)
                def decay(u):
                    S = state(u)
                    pool.wait_ge(state_in[u % STATE_SLOTS], 16 * state_count(l, u))
                    if u < NH + SP:
                        gb = gbc[:, 0:144].rearrange("p (h q b) -> p h q b", h=NH, q=3)
                        dec = gb[:, u, 1, :] if u < NH else gbc[:, 144 + (u - NH) * NB:144 + (u - NH + 1) * NB]
                        S3 = S.rearrange("p (b f) -> p b f", b=NB)
                        pool.tensor_tensor(S3, S3, dec.unsqueeze(2).to_broadcast([P, NB, P]), ALU.mult).then_inc(dec_decay, 1)
                    else:
                        gamma = float(np.float32(1.0) - np.float32(2.0) ** np.float32(-5.0 - (u - NH - SP)))
                        pool.tensor_scalar(S, S, gamma, None, ALU.mult).then_inc(dec_decay, 1)

                def output_gate(k):
                    pool.wait_ge(gates_done, l + 1)
                    pool.wait_ge(post_sq, 3 * l + k + 1)
                    y0, nt = POST[k][0:2]
                    gate = {0: O_ML, 2: G_R}[k]
                    ys = proj[:, y0 * NT:(y0 + nt) * NT]
                    pool.tensor_tensor(ys, ys, proj[:, gate * NT:(gate + nt) * NT], ALU.mult).then_inc(post_gated, 1)

                pool.wait_ge(gate_bc_in, l + 1)
                for u in range(2):
                    decay(u)
                for u in range(UNITS):
                    if u + 2 < UNITS:
                        decay(u + 2)
                    pool.wait_ge(dec_S, 2 * (l * UNITS + u + 1))
                    pool.dma_start(t["o_states"][l, u], state(u)).then_inc(state_out[u % STATE_SLOTS], 16)
                    if u + STATE_SLOTS < UNITS:
                        pool.wait_ge(state_out[u % STATE_SLOTS], 16 * state_count(l, u))
                        pool.wait_ge(dec_read, 2 * (l * UNITS + u + 1))
                        load_state(l, u + STATE_SLOTS)
                    if u == NH + 1:
                        output_gate(0)
                    if u == NH:
                        pool.wait_ge(ml_state, (l + 1) * NH)
                        pool.dma_start(t["o_np"][l], npr[:, :]).then_inc(dma_out, 16)
                        pool.dma_start(t["o_pst"][l, :, 0:NH, :], tiles3(proj, K_ML, NH, 0, P)).then_inc(dma_out, 16)
                    if u == NH + SP:
                        pool.wait_ge(ssd_state, (l + 1) * SP)
                        pool.dma_start(t["o_pst"][l, :, NH:NH + SP, :], tiles3(proj, V_ML, SP, 0, P)).then_inc(dma_out, 16)
                output_gate(2)
                pool.wait_ge(ret_h, (l + 1) * RH)
                pool.dma_start(t["o_pst"][l, :, NH + SP:UNITS, :], tiles3(proj, K_R, RH, 0, P)).then_inc(dma_out, 16)
                pool.wait_ge(dma_out, 16 * (OUTS * l + OUTS - 2))
                pool.wait_ge(post_y, 3 * (l + 1))
                pool.dma_start(tiles3(proj, CA_MEM, KT, 0, MEM), t["mem"]).then_inc(mem_in, 16)
                pool.wait_ge(v_turn, l + 1)
                pool.dma_start(t["o_mk"][l], tiles3(proj, CA_K, KT, 0, MEM)).then_inc(dma_out, 16)
                pool.dma_start(t["o_mv"][l], tiles3(proj, CA_VT, KT, 0, MEM)).then_inc(dma_out, 16)
                pool.wait_ge(h_ready, (3 * l + 2) * KT)
                pool.memset(csQ, 0.0).then_inc(cs_zero, 1)
                pool.memset(csPM, 0.0).then_inc(cs_zero, 1)
                pool.wait_ge(cs_zero, 2 * (l + 1))
                for n in (l * LIN + lin_of["q"] + 6, l * LIN + lin_of["q"] + 7):
                    pool.wait_ge(lin_free[n % 2], n // 2 + 1)
                qs = tiles3(proj, CA_Q, KT, SEQ, NB).rearrange("p (h k) b -> p k h b", k=2)
                for kk in range(2):
                    at = csQ[:, kk * 1024:(kk + 1) * 1024][:, 0:1024:CAH * NB + 1].rearrange("p (h b) -> p h b", h=CAH)
                    ins = pool.tensor_copy(at, qs[:, kk])
                ins.then_inc(cs_q, 1)
                pool.wait_ge(dma_out, 16 * OUTS * (l + 1))


OUTS = 11


def state_count(l, u):
    s = u % STATE_SLOTS
    per = len([q for q in range(UNITS) if q % STATE_SLOTS == s])
    return l * per + u // STATE_SLOTS + 1


def constants():
    f = np.float32
    k = np.zeros((P, N_CONST), f)
    idx = np.arange(P)
    k[:, C_ID:C_ID + P] = np.eye(P, dtype=f)
    k[:, C_MASK:C_MASK + P] = np.where(idx[:, None] <= idx[None, :], 0.0, MASKED)
    k[:, C_ONES:C_ONES + P] = 1.0
    for m in range(64):
        k[m + 64, C_ROT + m] = -1.0
        k[m, C_ROT + m + 64] = 1.0
    inv = (f(10000.0) ** (-np.arange(64, dtype=f) / f(64))).astype(f)
    pos = np.concatenate([np.arange(SEQ, dtype=f), np.full(NB, PAST_LEN, f)])
    ang = (np.concatenate([inv, inv])[:, None] * pos[None, :]).astype(f)
    for at, v in ((C_COS, np.cos(ang)), (C_SIN, np.sin(ang))):
        k[:, at:at + NT] = v
    for h in range(RH):
        log_g = np.log1p(-np.exp2(-5.0 - h))
        rel = np.arange(SEQ)[None, :] - idx[:, None]
        w = np.where(rel >= 0, np.exp(np.maximum(rel, 0) * log_g), 0.0)
        k[:, C_RET + h * 384:C_RET + h * 384 + SEQ] = w
        k[:, C_RET + h * 384 + SEQ:C_RET + (h + 1) * 384] = w[:, 0:P]
    tie = np.arange(NE)[None, :] < np.arange(NE)[:, None]
    k[:, C_TIE:C_TIE + 64] = tie.reshape(1, 64)
    for j in range(SP):
        k[2 * j, C_SEL2 + j * P:C_SEL2 + j * P + 64] = 1.0
        k[2 * j + 1, C_SEL2 + j * P + 64:C_SEL2 + (j + 1) * P] = 1.0
        k[2 * j:2 * j + 2, C_PAIR + j] = 1.0
    k[0:SH:2, C_HALF:C_HALF + 64] = 1.0
    k[1:SH:2, C_HALF + 64:C_HALF + P] = 1.0
    k[:, C_EPS] = EPS
    return k


def lay_out(a):
    f = np.float32

    def cols(v):
        return np.asarray(v).reshape(-1, P).T

    def fm(x):
        return np.asarray(x).T.reshape(-1, P, x.shape[0]).transpose(1, 0, 2)

    def tiles(w):
        kk, n = w.shape
        return np.asarray(w).reshape(kk // P, P, n // P, P).transpose(2, 1, 0, 3)

    def blocks(w):
        v = tiles(w).reshape(-1, 2, P, PIECE)
        return v.transpose(0, 2, 1, 3).reshape(-1, P, BLOCK)

    o = {"const": constants()}
    x = np.concatenate([np.asarray(a["x_prompt"])[0], np.asarray(a["x_sample"])[:, 0]], 0)
    o["x"] = fm(x).reshape(P, -1)
    par = np.zeros((P, DEPTH * N_PAR + KT), f)
    for l in range(DEPTH):
        def put(at, v):
            par[:, l * N_PAR + at:l * N_PAR + at + v.shape[1]] = v
        for at, name in ((G_MIX, "norm_mix"), (G_CA, "norm_ca"), (G_MEM, "norm_mem"), (G_FFN, "norm_ffn"), (G_ML, "ml_norm"),
                         (G_SSD, "ssd_norm"), (G_RET, "ret_norm"), (CONV_B, "ssd_conv_b")):
            put(at, cols(a[name][l]))
        put(CONV_K, np.asarray(a["ssd_conv_w"][l]).reshape(4, CONV_T, P).transpose(2, 1, 0).reshape(P, -1))
        put(D_SKIP, cols(np.repeat(np.asarray(a["ssd_d"][l]), 64)))
    par[:, DEPTH * N_PAR:] = cols(a["norm_final"])
    o["par"] = par
    w_in = np.asarray(a["w_in"])
    i0 = 24 * P
    dt0 = i0 + 12 + 16 * P
    wg = np.zeros((P, DEPTH, KT, 76), f)
    hp = np.zeros((P, DEPTH, 3), f)
    w_main = []
    for l in range(DEPTH):
        w = w_in[l]
        w3 = w.reshape(KT, P, -1).transpose(1, 0, 2)
        wg[:, l, :, 0:6] = w3[:, :, i0:i0 + 6]
        wg[:, l, :, 32:38] = w3[:, :, i0 + 6:i0 + 12]
        wg[:, l, :, 64:76] = w3[:, :, dt0:dt0 + 12]
        hp[0:6, l, 0] = a["ml_i_bias"][l]
        hp[32:38, l, 0] = a["ml_f_bias"][l]
        hp[64:76, l, 0] = a["ssd_dt_bias"][l]
        main = np.concatenate([w[:, :i0], w[:, i0 + 12:dt0], w[:, dt0 + 12:]], 1)
        width = dict(zip((a_ for a_, _ in IN_ORDER), (b_ - a_ for (a_, _), (b_, _) in zip(IN_ORDER, IN_ORDER[1:] + ((N_PROJ, 0),)))))
        main = np.concatenate([main[:, src * P:(src + width[at]) * P] for at, src in IN_ORDER], 1)
        w_main.append(blocks(main))
    o["wgate"], o["hpar"], o["w_in"] = wg.reshape(P, -1), hp.reshape(P, -1), np.stack(w_main)
    o["alog"] = np.asarray(a["ssd_a_log"]).T
    o["m0"] = np.asarray(a["state_mlstm_m"]).transpose(2, 0, 1).reshape(NH, -1)
    o["nst"] = np.asarray(a["state_mlstm_n"]).transpose(3, 0, 2, 1).reshape(P, -1)
    o["cst"] = np.asarray(a["state_ssd_conv"]).reshape(DEPTH, NB, 3, CONV_T, P).transpose(4, 0, 3, 2, 1).reshape(P, -1)
    o["wrt"] = np.asarray(a["moe_w_router"])[0].reshape(KT, P, NE).transpose(1, 0, 2).reshape(P, -1)
    ml = np.asarray(a["state_mlstm_c"]).transpose(0, 2, 3, 1, 4)
    sd = np.asarray(a["state_ssd"]).reshape(DEPTH, NB, SP, P, P).transpose(0, 2, 3, 1, 4)
    rt = np.asarray(a["state_ret"]).transpose(0, 2, 4, 1, 3)
    o["states"] = np.concatenate([ml, sd, rt], 1).reshape(DEPTH, UNITS, P, NB * P)
    o["kc"] = np.asarray(a["cache_mem_k"]).reshape(DEPTH, NB, MEM, KT, P).transpose(0, 1, 4, 3, 2).reshape(DEPTH, NB, P, -1)
    o["vc"] = np.asarray(a["cache_mem_v"]).reshape(DEPTH, NB, 2, P, D_MODEL).transpose(0, 1, 3, 2, 4).reshape(DEPTH, NB, P, -1)
    o["mem"] = fm(np.asarray(a["mem_prompt"])[0])
    o["w_out"] = np.stack([tiles(w).reshape(KT, P, BLOCK) for w in np.asarray(a["w_out"])])
    for name, src in (("w_q", "w_ca_q"), ("w_k", "w_ca_k"), ("w_v", "w_ca_v"), ("w_o", "w_ca_o")):
        o[name] = np.stack([blocks(w) for w in np.asarray(a[src])])
    ff = F_TILES * P
    experts = []
    for h in range(2):
        experts.append([np.asarray(a[n])[0][:, h * ff:(h + 1) * ff] for n in ("ffn_w_gate", "ffn_w_up")]
                       + [np.asarray(a["ffn_w_down"])[0][h * ff:(h + 1) * ff]])
    for e in range(NE):
        experts.append([np.asarray(a[n])[0, e] for n in ("moe_w_gate", "moe_w_up", "moe_w_down")])
    o["w_gu"] = np.stack([np.stack([tiles(g), tiles(u)], 2).reshape(F_TILES, P, BLOCK) for g, u, _ in experts])
    o["w_down"] = np.stack([tiles(d).reshape(KT, P, ff) for _, _, d in experts])
    return {k: np.ascontiguousarray(v, dtype=f) for k, v in o.items()}


OUT_SHAPES = {
    "y": (P, KT * NT), "o_mp": (DEPTH, NH, 1), "o_ms": (DEPTH, NH, NB), "o_cvp": (DEPTH, P, CONV_T * 3), "o_cvs": (DEPTH, P, CONV_T * 3 * NB),
    "o_ns": (DEPTH, P, 48), "o_np": (DEPTH, P, NH), "o_pst": (DEPTH, P, UNITS, P), "o_states": (DEPTH, UNITS, P, NB * P),
    "o_mk": (DEPTH, P, KT, MEM), "o_mv": (DEPTH, P, KT, MEM),
}


def kernel(**inputs):
    from concourse import bacc
    from concourse.bass_utils import run_bass_kernel_spmd

    arrays = lay_out(inputs)
    nc = bacc.Bacc("TRN2", target_bir_lowering=False, num_devices=1)
    t = {k: nc.dram_tensor(f"{k}_dram", v.shape, F32, kind="ExternalInput").ap() for k, v in arrays.items()}
    t.update({k: nc.dram_tensor(f"{k}_dram", s, F32, kind="ExternalOutput").ap() for k, s in OUT_SHAPES.items()})
    program(nc, t)
    r = run_bass_kernel_spmd(nc, [{f"{k}_dram": v for k, v in arrays.items()}], core_ids=[0])
    o = {k: r.results[0][f"{k}_dram"] for k in OUT_SHAPES}

    y = o["y"].reshape(P, KT, NT).transpose(2, 1, 0).reshape(NT, D_MODEL)
    pst = o["o_pst"].transpose(0, 2, 1, 3)
    s = o["o_states"].reshape(DEPTH, UNITS, P, NB, P).transpose(0, 3, 1, 2, 4)
    cv = o["o_cvs"].reshape(DEPTH, P, CONV_T, 3, NB).transpose(0, 4, 3, 2, 1).reshape(DEPTH, NB, 3, -1)
    cvp = o["o_cvp"].reshape(DEPTH, P, CONV_T, 3).transpose(0, 3, 2, 1).reshape(DEPTH, 1, 3, -1)
    mk, mv = (o[n].transpose(0, 3, 2, 1).reshape(DEPTH, 1, MEM, CAH, 2 * P) for n in ("o_mk", "o_mv"))
    out = (
        y[:SEQ][None], y[SEQ:][:, None],
        pst[:, None, 0:NH], o["o_np"].transpose(0, 2, 1)[:, None], o["o_mp"][:, None, :, 0], cvp,
        pst[:, NH:NH + SP].reshape(DEPTH, 1, SH, 64, P), pst[:, None, NH + SP:], mk, mv,
        s[:, :, 0:NH], o["o_ns"].reshape(DEPTH, P, NH, NB).transpose(0, 3, 2, 1), o["o_ms"].transpose(0, 2, 1), cv,
        s[:, :, NH:NH + SP].reshape(DEPTH, NB, SH, 64, P), s[:, :, NH + SP:].swapaxes(-1, -2),
    )
    return tuple(np.ascontiguousarray(v) for v in out)
```
